# Optimizing a Trainium2 kernel written in Bass

```python
import jax, jax.numpy as jnp
from jax import lax
import numpy as np

D_MODEL = 1024
BATCH = 1
SEQ = 1024
DEPTH = 2

MIX_WIDTH = D_MODEL
RWKV_WIDTH = MIX_WIDTH // 2
RWKV_HEAD = 64
RWKV_HEADS = RWKV_WIDTH // RWKV_HEAD
W_LORA = 64
A_LORA = 64
G_LORA = 128
LRU_WIDTH = MIX_WIDTH - RWKV_WIDTH
LRU_BLOCKS = 8
LRU_BLOCK = LRU_WIDTH // LRU_BLOCKS
LRU_CONV = 4
LRU_C = 8.0
S5_WIDTH = MIX_WIDTH
S5_GROUP = 16
S5_GROUPS = S5_WIDTH // S5_GROUP
S5_STATE = 64
D_FF = 2816
FFN_CONV = 3
NORM_EPS = 1e-6
GN_EPS = 64e-5
N_EVEN = (DEPTH + 1) // 2
N_ODD = DEPTH // 2
RWKV_SHIFT_COLS = 3 * RWKV_WIDTH + W_LORA + A_LORA + G_LORA
EVEN_IN_COLS = RWKV_SHIFT_COLS + 2 * LRU_WIDTH

kernel_name = "hybrid_rwkv7_rglru_s5_convffn"

def rms_norm(x, g):
    x32 = x.astype(jnp.float32)
    y = x32 * lax.rsqrt(jnp.mean(x32 * x32, axis=-1, keepdims=True) + NORM_EPS)
    return (y * g.astype(jnp.float32)).astype(x.dtype)

def causal_dwconv(x, w, b):
    k, c = w.shape
    y = lax.conv_general_dilated(x, w[:, None, :].astype(x.dtype), window_strides=(1,),
                                 padding=[(k - 1, 0)], dimension_numbers=('NWC', 'WIO', 'NWC'),
                                 feature_group_count=c)
    return y + b.astype(y.dtype)

def token_shift(p):
    return jnp.pad(p, ((0, 0), (1, 0), (0, 0)))[:, :-1]

def _lin_op(e1, e2):
    a1, b1 = e1
    a2, b2 = e2
    return a1 * a2, a2 * b1 + b2

def _cplx_op(e1, e2):
    a1r, a1i, b1r, b1i = e1
    a2r, a2i, b2r, b2i = e2
    return (a1r * a2r - a1i * a2i, a1r * a2i + a1i * a2r,
            a2r * b1r - a2i * b1i + b2r, a2r * b1i + a2i * b1r + b2i)

def wkv7(r, w, k, v, z, b):
    bn, s, h, n = r.shape

    def step(state, inp):
        r_t, w_t, k_t, v_t, z_t, b_t = inp
        sa = jnp.einsum('bhvk,bhk->bhv', state, z_t)
        state = (state * w_t[:, :, None, :] + sa[..., None] * b_t[:, :, None, :]
                 + v_t[..., None] * k_t[:, :, None, :])
        return state, jnp.einsum('bhvk,bhk->bhv', state, r_t)

    xs = tuple(jnp.swapaxes(t.astype(jnp.float32), 0, 1) for t in (r, w, k, v, z, b))
    state0 = jnp.zeros((bn, h, n, n), jnp.float32)
    _, ys = lax.scan(step, state0, xs)
    return jnp.swapaxes(ys, 0, 1)

def even_mixer(xn, w_in, mu, w0, w2, a0, a2, g2, k_k, k_a, r_k, ln_w, ln_b,
               conv_w, conv_b, gate_a_w, gate_a_b, gate_x_w, gate_x_b, lru_lambda, w_out):
    bn, s, _ = xn.shape
    f32 = jnp.float32
    rw = RWKV_WIDTH
    p = (xn @ w_in).astype(f32)
    pa = p[..., :RWKV_SHIFT_COLS]
    pa = pa + mu.astype(f32) * (token_shift(pa) - pa)
    r, k, v, wd, ad, gd = jnp.split(pa, [rw, 2 * rw, 3 * rw, 3 * rw + W_LORA, 3 * rw + W_LORA + A_LORA], axis=-1)
    w_log = -jax.nn.softplus(-(w0.astype(f32) + jnp.tanh(wd) @ w2.astype(f32))) - 0.5
    decay = jnp.exp(-jnp.exp(w_log))
    a = jax.nn.sigmoid(a0.astype(f32) + ad @ a2.astype(f32))
    g = jax.nn.sigmoid(gd) @ g2.astype(f32)
    hs = lambda t: t.reshape(bn, s, RWKV_HEADS, RWKV_HEAD)
    kk = hs(k * k_k.astype(f32))
    kk = kk / jnp.maximum(jnp.sqrt(jnp.sum(kk * kk, axis=-1, keepdims=True)), 1e-12)
    k = k * (1.0 + (a - 1.0) * k_a.astype(f32))
    y = wkv7(hs(r), hs(decay), hs(k), hs(v), -kk, kk * hs(a))
    mean = jnp.mean(y, axis=-1, keepdims=True)
    var = jnp.mean(jnp.square(y - mean), axis=-1, keepdims=True)
    y = ((y - mean) * lax.rsqrt(var + GN_EPS)).reshape(bn, s, rw) * ln_w.astype(f32) + ln_b.astype(f32)
    bonus = jnp.sum(hs(r) * hs(k) * r_k.astype(f32), axis=-1, keepdims=True) * hs(v)
    y_a = (y + bonus.reshape(bn, s, rw)) * g
    bx = p[..., RWKV_SHIFT_COLS:RWKV_SHIFT_COLS + LRU_WIDTH]
    bg = p[..., RWKV_SHIFT_COLS + LRU_WIDTH:]
    xc = causal_dwconv(bx, conv_w.astype(f32), conv_b.astype(f32))
    xb = xc.reshape(bn, s, LRU_BLOCKS, LRU_BLOCK)
    gr = jax.nn.sigmoid(jnp.einsum('bshi,hij->bshj', xb, gate_a_w.astype(f32)).reshape(bn, s, LRU_WIDTH) + gate_a_b.astype(f32))
    gi = jax.nn.sigmoid(jnp.einsum('bshi,hij->bshj', xb, gate_x_w.astype(f32)).reshape(bn, s, LRU_WIDTH) + gate_x_b.astype(f32))
    log_a = -LRU_C * gr * jax.nn.softplus(-lru_lambda.astype(f32))
    a_t = jnp.exp(log_a)
    u = xc * gi * jnp.sqrt(-jnp.expm1(2.0 * log_a))
    _, h = lax.associative_scan(_lin_op, (a_t, u), axis=1)
    y_b = h * jax.nn.gelu(bg)
    y_cat = jnp.concatenate([y_a, y_b], axis=-1).astype(xn.dtype)
    return y_cat @ w_out

def odd_mixer(xn, w_in, A_re, A_im, log_dt, B_re, B_im, C_re, C_im, D, w_glu):
    bn, s, _ = xn.shape
    f32 = jnp.float32
    u = (xn @ w_in).astype(f32)
    ug = u.reshape(bn, s, S5_GROUPS, S5_GROUP)
    lam_re = jnp.minimum(A_re.astype(f32), -1e-4)
    lam_im = A_im.astype(f32)
    dt = jnp.exp(log_dt.astype(f32))[:, None]
    mag = jnp.exp(lam_re * dt)
    ab_re = mag * jnp.cos(lam_im * dt)
    ab_im = mag * jnp.sin(lam_im * dt)
    den = lam_re * lam_re + lam_im * lam_im
    zr = ab_re - 1.0
    q_re = (zr * lam_re + ab_im * lam_im) / den
    q_im = (ab_im * lam_re - zr * lam_im) / den
    b_re = B_re.astype(f32)
    b_im = B_im.astype(f32)
    bb_re = q_re[..., None] * b_re - q_im[..., None] * b_im
    bb_im = q_re[..., None] * b_im + q_im[..., None] * b_re
    bu_re = jnp.einsum('bsgc,gnc->bsgn', ug, bb_re)
    bu_im = jnp.einsum('bsgc,gnc->bsgn', ug, bb_im)
    a_re = jnp.broadcast_to(ab_re[None, None], (1, s, S5_GROUPS, S5_STATE))
    a_im = jnp.broadcast_to(ab_im[None, None], (1, s, S5_GROUPS, S5_STATE))
    _, _, st_re, st_im = lax.associative_scan(_cplx_op, (a_re, a_im, bu_re, bu_im), axis=1)
    y = (jnp.einsum('gcn,bsgn->bsgc', C_re.astype(f32), st_re)
         - jnp.einsum('gcn,bsgn->bsgc', C_im.astype(f32), st_im)).reshape(bn, s, S5_WIDTH)
    y = jax.nn.gelu(y + D.astype(f32) * u).astype(xn.dtype)
    val, gate = jnp.split(y @ w_glu, 2, axis=-1)
    return val * jax.nn.sigmoid(gate)

def conv_ffn(xn, w_up, conv_w, conv_b, w_down):
    h = causal_dwconv(xn @ w_up, conv_w, conv_b)
    gate, val = jnp.split(h, 2, axis=-1)
    return (jax.nn.silu(gate) * val) @ w_down

def setup_inputs(seed: int = 0) -> dict:
    key = jax.random.key(seed)
    ks = iter(jax.random.split(key, 64))
    f32 = jnp.float32
    nrm = lambda shape, scale: jax.random.normal(next(ks), shape, f32) * scale
    uni = lambda shape, lo, hi: jax.random.uniform(next(ks), shape, f32, lo, hi)
    rw = RWKV_WIDTH
    inp = {}
    inp['x'] = nrm((BATCH, SEQ, D_MODEL), 1.0)
    inp['e_norm_g'] = 1.0 + nrm((N_EVEN, D_MODEL), 0.02)
    inp['e_w_in'] = nrm((N_EVEN, D_MODEL, EVEN_IN_COLS), D_MODEL ** -0.5)
    inp['e_mu'] = uni((N_EVEN, RWKV_SHIFT_COLS), 0.0, 1.0)
    inp['e_w0'] = uni((N_EVEN, rw), -6.0, -1.0)
    inp['e_w2'] = nrm((N_EVEN, W_LORA, rw), 0.1 * W_LORA ** -0.5)
    inp['e_a0'] = nrm((N_EVEN, rw), 0.1)
    inp['e_a2'] = nrm((N_EVEN, A_LORA, rw), 0.1 * A_LORA ** -0.5)
    inp['e_g2'] = nrm((N_EVEN, G_LORA, rw), G_LORA ** -0.5)
    inp['e_k_k'] = 0.85 + nrm((N_EVEN, rw), 0.02)
    inp['e_k_a'] = 1.0 + nrm((N_EVEN, rw), 0.02)
    inp['e_r_k'] = nrm((N_EVEN, RWKV_HEADS, RWKV_HEAD), 0.1)
    inp['e_ln_w'] = 1.0 + nrm((N_EVEN, rw), 0.02)
    inp['e_ln_b'] = nrm((N_EVEN, rw), 0.02)
    inp['e_conv_w'] = nrm((N_EVEN, LRU_CONV, LRU_WIDTH), LRU_CONV ** -0.5)
    inp['e_conv_b'] = nrm((N_EVEN, LRU_WIDTH), 0.02)
    inp['e_gate_a_w'] = nrm((N_EVEN, LRU_BLOCKS, LRU_BLOCK, LRU_BLOCK), LRU_BLOCK ** -0.5)
    inp['e_gate_a_b'] = nrm((N_EVEN, LRU_WIDTH), 0.02)
    inp['e_gate_x_w'] = nrm((N_EVEN, LRU_BLOCKS, LRU_BLOCK, LRU_BLOCK), LRU_BLOCK ** -0.5)
    inp['e_gate_x_b'] = nrm((N_EVEN, LRU_WIDTH), 0.02)
    a_c = uni((N_EVEN, LRU_WIDTH), 0.9, 0.999)
    a_base = a_c ** (1.0 / LRU_C)
    inp['e_lru_lambda'] = jnp.log(a_base) - jnp.log1p(-a_base)
    inp['e_w_out'] = nrm((N_EVEN, MIX_WIDTH, D_MODEL), MIX_WIDTH ** -0.5)
    n_idx = jnp.arange(S5_STATE, dtype=f32)
    inp['o_norm_g'] = 1.0 + nrm((N_ODD, D_MODEL), 0.02)
    inp['o_w_in'] = nrm((N_ODD, D_MODEL, S5_WIDTH), D_MODEL ** -0.5)
    inp['o_A_re'] = -0.5 + nrm((N_ODD, S5_GROUPS, S5_STATE), 0.01)
    inp['o_A_im'] = jnp.pi * n_idx + nrm((N_ODD, S5_GROUPS, S5_STATE), 0.01)
    inp['o_log_dt'] = uni((N_ODD, S5_GROUPS), float(np.log(1e-3)), float(np.log(1e-1)))
    inp['o_B_re'] = nrm((N_ODD, S5_GROUPS, S5_STATE, S5_GROUP), (2 * S5_GROUP) ** -0.5)
    inp['o_B_im'] = nrm((N_ODD, S5_GROUPS, S5_STATE, S5_GROUP), (2 * S5_GROUP) ** -0.5)
    inp['o_C_re'] = nrm((N_ODD, S5_GROUPS, S5_GROUP, S5_STATE), S5_STATE ** -0.5)
    inp['o_C_im'] = nrm((N_ODD, S5_GROUPS, S5_GROUP, S5_STATE), S5_STATE ** -0.5)
    inp['o_D'] = nrm((N_ODD, S5_WIDTH), 1.0)
    inp['o_w_glu'] = nrm((N_ODD, S5_WIDTH, 2 * D_MODEL), S5_WIDTH ** -0.5)
    inp['f_norm_g'] = 1.0 + nrm((DEPTH, D_MODEL), 0.02)
    inp['f_w_up'] = nrm((DEPTH, D_MODEL, 2 * D_FF), D_MODEL ** -0.5)
    inp['f_conv_w'] = nrm((DEPTH, FFN_CONV, 2 * D_FF), FFN_CONV ** -0.5)
    inp['f_conv_b'] = nrm((DEPTH, 2 * D_FF), 0.02)
    inp['f_w_down'] = nrm((DEPTH, D_FF, D_MODEL), D_FF ** -0.5)
    inp['final_norm_g'] = 1.0 + nrm((D_MODEL,), 0.02)
    return inp

def reference(x, e_norm_g, e_w_in, e_mu, e_w0, e_w2, e_a0, e_a2, e_g2, e_k_k, e_k_a, e_r_k,
              e_ln_w, e_ln_b, e_conv_w, e_conv_b, e_gate_a_w, e_gate_a_b, e_gate_x_w, e_gate_x_b,
              e_lru_lambda, e_w_out, o_norm_g, o_w_in, o_A_re, o_A_im, o_log_dt, o_B_re, o_B_im,
              o_C_re, o_C_im, o_D, o_w_glu, f_norm_g, f_w_up, f_conv_w, f_conv_b, f_w_down,
              final_norm_g):
    for i in range(DEPTH):
        j = i // 2
        if i % 2 == 0:
            x = x + even_mixer(rms_norm(x, e_norm_g[j]), e_w_in[j], e_mu[j], e_w0[j], e_w2[j],
                               e_a0[j], e_a2[j], e_g2[j], e_k_k[j], e_k_a[j], e_r_k[j],
                               e_ln_w[j], e_ln_b[j], e_conv_w[j], e_conv_b[j],
                               e_gate_a_w[j], e_gate_a_b[j], e_gate_x_w[j], e_gate_x_b[j],
                               e_lru_lambda[j], e_w_out[j])
        else:
            x = x + odd_mixer(rms_norm(x, o_norm_g[j]), o_w_in[j], o_A_re[j], o_A_im[j],
                              o_log_dt[j], o_B_re[j], o_B_im[j], o_C_re[j], o_C_im[j],
                              o_D[j], o_w_glu[j])
        x = x + conv_ffn(rms_norm(x, f_norm_g[i]), f_w_up[i], f_conv_w[i], f_conv_b[i], f_w_down[i])
    return rms_norm(x, final_norm_g)


_drawn_inputs = setup_inputs


def setup_inputs(seed=0):
    import zlib

    import numpy as np

    out = dict(_drawn_inputs(seed))
    spreads = {}
    factors = {'e_norm_g': 2.889,
     'e_w2': 23.197,
     'e_a0': 3.09,
     'e_a2': 3.301,
     'e_k_k': 56.16,
     'e_k_a': 6.126,
     'e_ln_w': 53.008,
     'e_ln_b': 51.639,
     'e_gate_a_b': 44.881,
     'e_gate_x_b': 33.765,
     'o_norm_g': 50.02,
     'o_A_re': 64.0,
     'o_B_re': 3.168,
     'o_B_im': 3.1,
     'o_C_re': 3.139,
     'o_C_im': 3.131,
     'f_norm_g': 8.491,
     'f_conv_b': 8.352,
     'final_norm_g': 8.251,
     'e_conv_b': 3.41}
    for name, (base, spread) in spreads.items():
        noise = np.random.default_rng([zlib.crc32(name.encode()), seed]).standard_normal(out[name].shape)
        drawn = base * np.exp(spread * noise) if base else spread * noise
        out[name] = __import__('jax').numpy.asarray(drawn.astype(out[name].dtype))
    for name, factor in factors.items():
        out[name] = (out[name] * factor).astype(out[name].dtype)
    return out
```

```python
from contextlib import ExitStack

import concourse.bass as bass
from concourse import mybir

F32 = mybir.dt.float32
F32R = mybir.dt.float32r
ALU = mybir.AluOpType
ACT = mybir.ActivationFunctionType

P = 128
D_MODEL = 1024
SEQ = 1024
HALF = 512
DT = D_MODEL // P
RW = 512
RT = RW // P
HEAD = 64
HEADS = RW // HEAD
D_FF = 2816
FT = D_FF // P
FGROUP = FT // 2
NORM_EPS = 1e-6
GN_EPS = 64e-5
LRU_C = 8.0
EXP_MINUS_HALF = 0.6065306597126334
CH = 128
NCH = SEQ // CH
L5 = 8
N5 = SEQ // L5
S5_PAIRS = 32

ROWS0 = [("e_mu", 14), ("e_w0", 4), ("e_a0", 4), ("e_k_k", 4), ("e_k_a", 4), ("e_r_k", 4),
         ("e_ln_w", 4), ("e_ln_b", 4), ("e_conv_w", 16), ("e_conv_b", 4), ("e_gate_a_b", 4),
         ("e_gate_x_b", 4), ("e_lru_lambda", 4), ("e_norm_g", 8), ("o_norm_g", 8),
         ("f_norm_g", 16), ("final_norm_g", 8), ("o_D", 8)]
COL = {}
_at = 0
for _name, _rows in ROWS0:
    COL[_name] = _at
    _at += _rows
ROWS0_USED = _at
COL["f_conv_w"] = P
COL["f_conv_b"] = P + 2 * 3 * 2 * FT
PCOLS = COL["f_conv_b"] + 2 * 2 * FT


def flat(ap):
    names = "abcdef"[:len(ap.shape)]
    return ap.rearrange(f"{' '.join(names)} -> ({' '.join(names)})")


def trunk(nc, io, out):
    ctx = ExitStack()
    sems = {}

    def sem(name):
        if name not in sems:
            sems[name] = ctx.enter_context(nc.semaphore(name))
        return sems[name]

    def sb(scope, name, shape, dt=F32):
        return scope.enter_context(nc.sbuf_tensor(name, shape, dt))

    def ps(scope, name, shape):
        return scope.enter_context(nc.psum_tensor(name, shape, F32))

    class Link:

        def __init__(self, eng, name):
            self.eng, self.sem, self.n, self.loop = eng, sem(name), totals.get(name, 0), 0
            self.name = name

        def did(self, ins):
            ins.then_inc(self.sem, 1)
            self.n += 1

        def wait(self):
            self.eng.wait_ge(self.sem, self.loop + self.n)

        def run(self, ins):
            self.did(ins)
            self.wait()

        def enter(self, i, per):
            self.loop, self.start, self.per = i * per, self.n, per

        def leave(self, times):
            assert self.n - self.start == self.per, (self.name, self.n - self.start)
            self.loop, self.n = 0, self.start + self.per * times

        def close(self):
            totals[self.name] = self.n

    totals = {}

    class Rounds:

        def __init__(self, tag, raises):
            self.tag, self.raises = tag, raises
            self.per = {n: k for own in raises.values() for n, k in own.items()}

        def start(self, eng, own):
            for n, k in self.raises[own].items():
                eng.sem_inc(sem(f"{self.tag}_{n}"), 2 * k)

        def wait(self, eng, name, i, k=1, back=0):
            eng.wait_ge(sem(f"{self.tag}_{name}"), i * self.per[name] + ((2 - back) * self.per[name] + k))

        def up(self, ins, name):
            ins.then_inc(sem(f"{self.tag}_{name}"), 1)

    x_res = sb(ctx, "x_res", [P, DT, SEQ])
    prm = sb(ctx, "prm", [P, 4 * P])
    ident = sb(ctx, "ident", [P, P])

    def col(name, k=0):
        return prm[:, COL[name] + k:COL[name] + k + 1]

    def col_at(name, k):
        return prm[:, bass.ds(k + COL[name], 1)]

    with ExitStack() as sc:
        rows = sb(sc, "param_rows", [P, 4, P])
        stage = sb(sc, "x_stage", [P, 2, D_MODEL])
        turned = [ps(sc, f"turned{s}", [P, 2 * HALF]) for s in range(2)]
        turned_prm = ps(sc, "turned_prm", [P, 4, P])
        x_loaded = [sem("x_loaded0"), sem("x_loaded1")]
        prm_loaded, rows_clear, ident_ready = sem("prm_loaded"), sem("rows_clear"), sem("ident_ready")
        x_turned, x_kept, prm_turned = sem("x_turned"), sem("x_kept"), sem("prm_turned")
        n_prm = len(ROWS0) + 4
        x_rows = io["x"].rearrange("b (n t) d -> (b n) t d", t=P)
        with nc.Block() as block:
            @block.sync
            def _(sp):
                for s in range(2):
                    sp.dma_start(stage[:, s, :], x_rows[s, :, :]).then_inc(x_loaded[s], 16)
                with sp.Fori(1, SEQ // P // 2) as i:
                    for s in range(2):
                        sp.wait_ge(x_turned, i * 2 + s - 1)
                        sp.dma_start(stage[:, s, :], x_rows[bass.ds(i * 2 + s, 1), :, :]).then_inc(x_loaded[s], 16)

            @block.gpsimd
            def _(pool):
                pool.memset(ident[:, :], 0.0).then_inc(ident_ready, 1)
                pool.memset(rows[:, 0, :], 0.0).then_inc(rows_clear, 1)
                pool.memset(rows[:, 3, :], 0.0).then_inc(rows_clear, 1)
                pool.wait_ge(ident_ready, 1)
                pool.affine_select(out=ident[:, :], in_=ident[:, :], compare_op=ALU.not_equal, fill=1.0,
                                   base=0, pattern=[[-1, P]], channel_multiplier=1).then_inc(ident_ready, 1)

            @block.scalar
            def _(act):
                act.wait_ge(rows_clear, 2)
                for name, n in ROWS0:
                    act.dma_start(rows[COL[name]:COL[name] + n, 0, :],
                                  flat(io[name]).rearrange("(r p) -> r p", p=P)).then_inc(prm_loaded, 16)
                taps = flat(io["f_conv_w"]).rearrange("(r p) -> r p", p=P)
                for k in range(3):
                    n = min(P, taps.shape[0] - k * P)
                    act.dma_start(rows[0:n, 1 + k, :], taps[k * P:k * P + n, :]).then_inc(prm_loaded, 16)
                bias = flat(io["f_conv_b"]).rearrange("(r p) -> r p", p=P)
                at = COL["f_conv_b"] - 3 * P
                act.dma_start(rows[at:at + bias.shape[0], 3, :], bias).then_inc(prm_loaded, 16)
                act.wait_ge(prm_turned, 1)
                act.copy(prm[:, :], turned_prm[:, :, :]).then_inc(sem("prm_ready"), 1)

            @block.tensor
            def _(pe):
                pe.wait_ge(ident_ready, 2)
                with pe.Fori(0, SEQ // P // 2) as i:
                    for s in range(2):
                        pe.wait_ge(x_loaded[s], i * 16 + 16)
                        pe.wait_ge(x_kept, i * 2 + s + 1)
                        for c in range(DT):
                            last = nc.tensor.transpose(turned[s][:, c * P:(c + 1) * P],
                                                       stage[:, s, c * P:(c + 1) * P], ident[:, :])
                        last.then_inc(x_turned, 1)
                pe.wait_ge(prm_loaded, 16 * n_prm)
                for k in range(4):
                    last = nc.tensor.transpose(turned_prm[:, k, :], rows[:, k, :], ident[:, :])
                last.then_inc(prm_turned, 1)

            @block.vector
            def _(dve):
                dve.sem_inc(x_kept, 2)
                with dve.Fori(0, SEQ // P // 2) as i:
                    for s in range(2):
                        dve.wait_ge(x_turned, i * 2 + s + 1)
                        nc.vector.tensor_copy(x_res[:, :, bass.ds(i * (2 * P) + s * P, P)],
                                              turned[s][:, :].rearrange("p (c t) -> p c t", c=DT)).then_inc(x_kept, 1)

    def norm(tag, g_name, g_at, xn_hi, xn_lo):
        with ExitStack() as sc:
            sq = sb(sc, f"sq_{tag}", [P, 2, SEQ])
            rstd = sb(sc, f"rstd_{tag}", [P, SEQ])
            xn = sb(sc, f"xn_{tag}", [P, 2, SEQ])
            ones = sb(sc, f"ones_{tag}", [P, P])
            eps = sb(sc, f"eps_{tag}", [P, 1])
            total = ps(sc, f"total_{tag}", [P, SEQ])
            squared, summed, root, consts, inv, scaled, hi_done, lo_done = (
                sem("n_" + n) for n in ("squared", "summed", "root", "consts", "inv", "scaled", "hi", "lo"))
            before = totals.get("norms", 0)
            totals["norms"] = before + 1
            tiles = before * DT
            with nc.Block() as block:
                @block.scalar
                def _(act):
                    for c in range(DT):
                        if c >= 2:
                            act.wait_ge(summed, tiles + c - 1)
                        nc.scalar.activation(sq[:, c % 2, :], x_res[:, c, :], ACT.Square).then_inc(squared, 1)
                    act.wait_ge(summed, tiles + DT)
                    act.wait_ge(consts, 2 * before + 2)
                    nc.scalar.activation(rstd[:, :], total[:, :], ACT.Sqrt, scale=1.0 / D_MODEL, bias=eps[:, 0:1]).then_inc(root, 1)
                    for c in range(DT) if xn_hi else ():
                        act.wait_ge(scaled, tiles + c + 1)
                        nc.scalar.copy(xn_hi[:, c, :], xn[:, c % 2, :]).then_inc(hi_done, 1)

                @block.tensor
                def _(pe):
                    pe.wait_ge(consts, 2 * before + 2)
                    for c in range(DT):
                        pe.wait_ge(squared, tiles + c + 1)
                        for h in range(2):
                            last = nc.tensor.matmul(total[:, h * HALF:(h + 1) * HALF], ones[:, :],
                                                    sq[:, c % 2, h * HALF:(h + 1) * HALF],
                                                    start=c == 0, stop=c == DT - 1)
                        last.then_inc(summed, 1)

                @block.vector
                def _(dve):
                    nc.vector.memset(ones[:, :], 1.0).then_inc(consts, 1)
                    nc.vector.memset(eps[:, :], NORM_EPS).then_inc(consts, 1)
                    dve.wait_ge(root, before + 1)
                    nc.vector.reciprocal(rstd[:, :], rstd[:, :]).then_inc(inv, 1)
                    dve.wait_ge(inv, before + 1)
                    for c in range(DT):
                        if c >= 2 and xn_hi:
                            dve.wait_ge(lo_done, tiles + c - 1)
                        nc.vector.scalar_tensor_tensor(out=xn[:, c % 2, :] if xn_hi else x_res[:, c, :], in0=x_res[:, c, :],
                                                       scalar=col(g_name, g_at + c), in1=rstd[:, :],
                                                       op0=ALU.mult, op1=ALU.mult).then_inc(scaled, 1)

                @block.gpsimd
                def _(pool):
                    for c in range(DT) if xn_hi else ():
                        pool.wait_ge(hi_done, tiles + c + 1)
                        pool.tensor_tensor(xn_lo[:, c, :], xn[:, c % 2, :], xn_hi[:, c, :].bitcast(F32),
                                           op=ALU.subtract).then_inc(lo_done, 1)

    w_loaded = [sem("w_loaded0"), sem("w_loaded1")]
    w_hi_done, w_lo_done, w_used = sem("w_hi_done"), sem("w_lo_done"), sem("w_used")
    unit_free = sem("unit_free")
    KC = 4

    class Dense:

        q = 0
        u = 0

        def __init__(self, sc, tag):
            self.raw = sb(sc, f"w_raw_{tag}", [P, 2, KC, P])
            self.hi = sb(sc, f"w_hi_{tag}", [P, 2, KC, P], F32R)
            self.lo = sb(sc, f"w_lo_{tag}", [P, 2, KC, P], F32R)
            self.acc = [ps(sc, f"acc{s}_{tag}", [P, SEQ]) for s in range(2)]

        @staticmethod
        def chunks(kt):
            return [(k, min(KC, kt - k)) for k in range(0, kt, KC)]

        def load(self, sp, w, kt, n0, pair, par):
            for k, n in self.chunks(kt):
                sp.wait_ge(w_lo_done, pair * 2 + (par + 1))
                sp.dma_start(self.raw[:, par, 0:n, :], w[:, k:k + n, n0]).then_inc(w_loaded[par], 16)
                pair, par = (pair + 1, 0) if par else (pair, 1)

        def take_hi(self, act, kt, pair, par):
            for k, n in self.chunks(kt):
                act.wait_ge(w_loaded[par], pair * 16 + 16)
                act.wait_ge(w_used, pair * 2 + (par + 1))
                nc.scalar.copy(self.hi[:, par, 0:n, :], self.raw[:, par, 0:n, :]).then_inc(w_hi_done, 1)
                pair, par = (pair + 1, 0) if par else (pair, 1)

        def take_lo(self, pool, kt, pair, par):
            for k, n in self.chunks(kt):
                pool.wait_ge(w_hi_done, pair * 2 + (par + 1))
                pool.tensor_tensor(self.lo[:, par, 0:n, :], self.raw[:, par, 0:n, :],
                                   self.hi[:, par, 0:n, :].bitcast(F32), op=ALU.subtract).then_inc(w_lo_done, 1)
                pair, par = (pair + 1, 0) if par else (pair, 1)

        @staticmethod
        def wait_unit(eng, pair, par):
            eng.wait_ge(w_used, pair * 2 + (par + 3))

        def product(self, pe, kt, in_hi, in_lo, unit, slot, pair, par):
            pe.wait_ge(unit_free, unit + 1)
            acc = self.acc[slot]
            for k, n in self.chunks(kt):
                pe.wait_ge(w_lo_done, pair * 2 + (par + 3))
                for j in range(n):
                    for w, x in ((self.hi, in_hi), (self.hi, in_lo), (self.lo, in_hi)):
                        first = k + j == 0 and w is self.hi and x is in_hi
                        final = k + j == kt - 1 and w is self.lo
                        for h in range(2):
                            last = nc.tensor.matmul(acc[:, h * HALF:(h + 1) * HALF], w[:, par, j, :],
                                                    x[:, k + j, h * HALF:(h + 1) * HALF], start=first, stop=final)
                last.then_inc(w_used, 1)
                pair, par = (pair + 1, 0) if par else (pair, 1)

    def dense_credit_pool(pool):
        pool.sem_inc(w_lo_done, 2)

    def dense_credit_pe(pe):
        pe.sem_inc(w_used, 2)

    def dense_credit_dve(dve):
        dve.sem_inc(unit_free, 2)

    proj = ctx.enter_context(ExitStack())
    EV = 22
    p_even = sb(proj, "p_even", [P, EV, SEQ])
    w_in = io["e_w_in"].rearrange("a (k p) n -> (a p) k n", p=P)
    with ExitStack() as sc:
        xn_hi = sb(sc, "xn_hi_e", [P, DT, SEQ], F32R)
        xn_lo = sb(sc, "xn_lo_e", [P, DT, SEQ], F32R)
        norm("e", "e_norm_g", 0, xn_hi, xn_lo)
        dn = Dense(sc, "e")
        start_scale = sb(sc, "start_scale", [P, EV])
        start_bias = sb(sc, "start_bias", [P, EV])
        tables, started, spent = sem("e_tables"), sem("e_started"), sem("e_spent")
        with nc.Block() as block:
            @block.sync
            def _(sp):
                with sp.Fori(0, EV // 2) as i:
                    for s in range(2):
                        dn.load(sp, w_in, DT, bass.ds(i * (2 * P) + s * P, P), i * 2 + s, 0)

            @block.gpsimd
            def _(pool):
                dense_credit_pool(pool)
                with pool.Fori(0, EV // 2) as i:
                    for s in range(2):
                        dn.take_lo(pool, DT, i * 2 + s, 0)

            @block.tensor
            def _(pe):
                dense_credit_pe(pe)
                with pe.Fori(0, EV // 2) as i:
                    for s in range(2):
                        dn.product(pe, DT, xn_hi, xn_lo, i * 2 + s, s, i * 2 + s, 0)

            @block.scalar
            def _(act):
                def start_unit(u, slot):
                    act.wait_ge(w_used, u * 2 + 4)
                    nc.scalar.activation(p_even[:, bass.ds(u, 1), :], dn.acc[slot][:, :], ACT.Identity,
                                         scale=start_scale[:, bass.ds(u, 1)],
                                         bias=start_bias[:, bass.ds(u, 1)]).then_inc(started, 1)

                act.wait_ge(tables, 6)
                dn.take_hi(act, DT, 0, 0)
                dn.take_hi(act, DT, 1, 0)
                start_unit(0, 0)
                with act.Fori(1, EV // 2) as i:
                    for s in range(2):
                        dn.take_hi(act, DT, i * 2 + s, 0)
                        start_unit(i * 2 + (s - 1), 1 - s)
                start_unit(EV - 1, 1)

            @block.vector
            def _(dve):
                dense_credit_dve(dve)
                nc.vector.tensor_scalar(start_scale[:, 0:14], prm[:, COL["e_mu"]:COL["e_mu"] + 14],
                                        -1.0, 1.0, ALU.mult, ALU.add).then_inc(tables, 1)
                nc.vector.tensor_copy(start_scale[:, 14:18],
                                      prm[:, COL["e_conv_w"] + 12:COL["e_conv_w"] + 16]).then_inc(tables, 1)
                nc.vector.memset(start_scale[:, 18:22], 1.0).then_inc(tables, 1)
                nc.vector.memset(start_bias[:, 0:14], 0.0).then_inc(tables, 1)
                nc.vector.tensor_copy(start_bias[:, 14:18],
                                      prm[:, COL["e_conv_b"]:COL["e_conv_b"] + 4]).then_inc(tables, 1)
                nc.vector.memset(start_bias[:, 18:22], 0.0).then_inc(tables, 1)

                def tap(u, slot, scale, back):
                    here = p_even[:, bass.ds(u, 1), back:SEQ]
                    return nc.vector.scalar_tensor_tensor(out=here, in0=dn.acc[slot][:, 0:SEQ - back],
                                                          scalar=scale, in1=here, op0=ALU.mult, op1=ALU.add)

                with dve.Fori(0, 7) as i:
                    for s in range(2):
                        dve.wait_ge(started, i * 2 + s + 1)
                        tap(i * 2 + s, s, col_at("e_mu", i * 2 + s), 1).then_inc(unit_free, 1)
                with dve.Fori(0, 2) as i:
                    for s in range(2):
                        dve.wait_ge(started, i * 2 + (s + 15))
                        for back in (1, 2, 3):
                            ins = tap(i * 2 + (s + 14), s, col_at("e_conv_w", i * 2 + (s + 4 * (3 - back))), back)
                            if back < 3:
                                ins.then_inc(spent, 1)
                                dve.wait_ge(spent, i * 4 + (2 * s + back))
                        ins.then_inc(unit_free, 1)
                dve.wait_ge(unit_free, 2 + 18)
                with dve.Fori(18, EV) as i:
                    dve.wait_ge(started, i + 1)
                    dve.sem_inc(unit_free, 1)

    LEVELS = 7
    level_mask = sb(proj, "level_mask", [P, LEVELS, P])
    causal = sb(proj, "causal", [P, 2, P])
    head_ones = sb(proj, "head_ones", [P, P])
    centre = sb(proj, "centre", [P, P])
    scratch_w = p_even[:, 18:22, :]

    with ExitStack() as sc:
        gw = sb(sc, "gw", [P, 2, 4, P])
        same_block = sb(sc, "same_block", [P, LEVELS + 1, P])
        decay_c = sb(sc, "decay_c", [P, 4])
        lam_abs = sb(sc, "lam_abs", [P, 4])
        z = sb(sc, "lam_z", [P, 4])
        z2 = sb(sc, "lam_z2", [P, 4])
        den = sb(sc, "lam_den", [P, 4])
        poly = sb(sc, "lam_poly", [P, 4])
        g_r = sb(sc, "g_r", [P, 2, SEQ])
        g_i = sb(sc, "g_i", [P, 2, SEQ])
        a_t = sb(sc, "a_t", [P, 2, SEQ])
        th = sb(sc, "th", [P, 2, SEQ])
        g_psum = [ps(sc, f"g_psum{k}", [P, SEQ]) for k in range(4)]
        gw_clear, gw_loaded, lam_exp, decay_ready = sem("gw_clear"), sem("gw_loaded"), sem("lam_exp"), sem("decay_ready")
        lam_ready = sem("lam_ready")
        l_gates, l_sig, l_tanh, l_exp, l_arg, l_root, l_gelu, l_out = (
            sem("l_" + n) for n in ("gates", "sig", "tanh", "exp", "arg", "root", "gelu", "out"))
        masks_pool, masks_dve, l_gated, l_h, l_sq = sem("masks_pool"), sem("masks_dve"), sem("l_gated"), sem("l_h"), sem("l_sq")
        with nc.Block() as block:
            @block.gpsimd
            def _(pool):
                link = Link(pool, "masks_pool")
                link.run(pool.memset(same_block[:, :, :], 1.0))
                for k in range(LEVELS):
                    m = same_block[:, k, :].rearrange("p (b c) -> p b c", c=1 << k)
                    link.run(pool.affine_select(out=m, in_=m, compare_op=ALU.is_ge, fill=0.0, base=0,
                                                pattern=[[-(1 << k), P >> k], [0, 1 << k]], channel_multiplier=1))
                    link.run(pool.affine_select(out=m, in_=m, compare_op=ALU.is_ge, fill=0.0, base=(1 << k) - 1,
                                                pattern=[[1 << k, P >> k], [0, 1 << k]], channel_multiplier=-1))
                link.run(pool.memset(causal[:, :, :], 1.0))
                for k in range(2):
                    link.run(pool.affine_select(out=causal[:, k, :], in_=causal[:, k, :], compare_op=ALU.is_ge, fill=0.0,
                                                base=k - 1, pattern=[[1, P]], channel_multiplier=-1))
                link.close()

            @block.sync
            def _(sp):
                sp.wait_ge(gw_clear, 1)
                for g, name in enumerate(("e_gate_a_w", "e_gate_x_w")):
                    w = io[name].rearrange("a (c h) i j -> (a h) i c j", h=2)
                    for h in range(2):
                        sp.dma_start(gw[h * HEAD:(h + 1) * HEAD, g, :, h * HEAD:(h + 1) * HEAD],
                                     w[h, :, :, :]).then_inc(gw_loaded, 16)

            @block.tensor
            def _(pe):
                pe.wait_ge(gw_loaded, 64)
                for c in range(4):
                    if c >= 2:
                        pe.wait_ge(l_sig, 2 * (c - 1))
                    for g in range(2):
                        for h in range(2):
                            last = nc.tensor.matmul(g_psum[2 * (c % 2) + g][:, h * HALF:(h + 1) * HALF], gw[:, g, c, :],
                                                    p_even[:, 14 + c, h * HALF:(h + 1) * HALF], start=True, stop=True)
                    last.then_inc(l_gates, 1)

            @block.scalar
            def _(act):
                act.wait_ge(lam_ready, 1)
                nc.scalar.activation(lam_abs[:, :], lam_abs[:, :], ACT.Exp, scale=-1.0).then_inc(lam_exp, 1)
                act.wait_ge(decay_ready, 1)
                for c in range(4):
                    s = c % 2
                    act.wait_ge(l_gates, c + 1)
                    if c >= 2:
                        act.wait_ge(l_out, c - 1)
                    nc.scalar.activation(g_r[:, s, :], g_psum[2 * s][:, :], ACT.Sigmoid,
                                         bias=col("e_gate_a_b", c)).then_inc(l_sig, 1)
                    nc.scalar.activation(g_i[:, s, :], g_psum[2 * s + 1][:, :], ACT.Sigmoid,
                                         bias=col("e_gate_x_b", c)).then_inc(l_sig, 1)
                    act.wait_ge(l_sig, 2 * c + 1)
                    nc.scalar.activation(th[:, s, :], g_r[:, s, :], ACT.Tanh, scale=decay_c[:, c:c + 1]).then_inc(l_tanh, 1)
                    act.wait_ge(l_arg, 4 * c + 1)
                    nc.scalar.activation(a_t[:, s, :], a_t[:, s, :], ACT.Exp).then_inc(l_exp, 1)
                    act.wait_ge(l_arg, 4 * c + 3)
                    nc.scalar.activation(th[:, s, :], th[:, s, :], ACT.Sqrt).then_inc(l_root, 1)
                    nc.scalar.activation(p_even[:, 18 + c, :], p_even[:, 18 + c, :], ACT.Gelu_apprx_tanh).then_inc(l_gelu, 1)

            @block.vector
            def _(dve):
                nc.vector.memset(gw[:, :, :, :], 0.0).then_inc(gw_clear, 1)
                lam = prm[:, COL["e_lru_lambda"]:COL["e_lru_lambda"] + 4]
                nc.vector.scalar_tensor_tensor(out=lam_abs[:, :], in0=lam, scalar=-1.0, in1=lam, op0=ALU.mult,
                                               op1=ALU.max).then_inc(lam_ready, 1)
                dve.wait_ge(lam_exp, 1)
                link = Link(dve, "masks_dve")
                link.run(nc.vector.tensor_scalar(den[:, :], lam_abs[:, :], 2.0, None, ALU.add))
                link.run(nc.vector.reciprocal(den[:, :], den[:, :]))
                link.run(nc.vector.tensor_tensor(z[:, :], lam_abs[:, :], den[:, :], ALU.mult))
                link.run(nc.vector.tensor_tensor(z2[:, :], z[:, :], z[:, :], ALU.mult))
                link.run(nc.vector.memset(poly[:, :], 1.0 / 17))
                for k in range(15, 0, -2):
                    link.run(nc.vector.tensor_tensor(poly[:, :], poly[:, :], z2[:, :], ALU.mult))
                    link.run(nc.vector.tensor_scalar(poly[:, :], poly[:, :], 1.0 / k, None, ALU.add))
                link.run(nc.vector.tensor_tensor(poly[:, :], poly[:, :], z[:, :], ALU.mult))
                link.run(nc.vector.tensor_scalar(poly[:, :], poly[:, :], 2 * LRU_C, None, ALU.mult))
                link.run(nc.vector.tensor_scalar(den[:, :], lam, -LRU_C, 0.0, ALU.mult, ALU.max))
                nc.vector.tensor_tensor(decay_c[:, :], poly[:, :], den[:, :], ALU.add).then_inc(decay_ready, 1)
                dve.wait_ge(decay_ready, 1)
                for c in range(4):
                    s = c % 2
                    dve.wait_ge(l_sig, 2 * c + 2)
                    nc.vector.tensor_scalar(a_t[:, s, :], g_r[:, s, :], decay_c[:, c:c + 1], -1.0,
                                            ALU.mult, ALU.mult).then_inc(l_arg, 1)
                    nc.vector.tensor_tensor(g_i[:, s, :], g_i[:, s, :], p_even[:, 14 + c, :], ALU.mult).then_inc(l_gated, 1)
                    dve.wait_ge(l_exp, c + 1)
                    nc.vector.tensor_tensor(g_r[:, s, :], a_t[:, s, :], a_t[:, s, :], ALU.mult).then_inc(l_arg, 1)
                    dve.wait_ge(l_arg, 4 * c + 2)
                    dve.wait_ge(l_tanh, c + 1)
                    nc.vector.scalar_tensor_tensor(out=th[:, s, :], in0=g_r[:, s, :], scalar=1.0, in1=th[:, s, :],
                                                   op0=ALU.add, op1=ALU.mult).then_inc(l_arg, 1)
                    dve.wait_ge(l_gated, c + 1)
                    dve.wait_ge(l_root, c + 1)
                    nc.vector.tensor_tensor(g_i[:, s, :], g_i[:, s, :], th[:, s, :], ALU.mult).then_inc(l_arg, 1)
                    dve.wait_ge(l_arg, 4 * c + 4)
                    nc.vector.tensor_tensor_scan(g_r[:, s, :], a_t[:, s, :], g_i[:, s, :], 0.0, ALU.mult, ALU.add).then_inc(l_h, 1)
                    dve.wait_ge(l_h, c + 1)
                    dve.wait_ge(l_gelu, c + 1)
                    nc.vector.tensor_tensor(p_even[:, 14 + c, :], g_r[:, s, :], p_even[:, 18 + c, :], ALU.mult).then_inc(l_out, 1)
                dve.wait_ge(masks_pool, 1 + 2 * LEVELS + 3)
                for k in range(LEVELS):
                    link.run(nc.vector.tensor_tensor(level_mask[:, k, :], same_block[:, k + 1, :], same_block[:, k, :], ALU.subtract))
                    link.run(nc.vector.tensor_tensor(level_mask[:, k, :], level_mask[:, k, :], causal[:, 0, :], ALU.mult))
                link.run(nc.vector.tensor_copy(head_ones[:, :], same_block[:, 6, :]))
                link.run(nc.vector.scalar_tensor_tensor(out=centre[:, :], in0=head_ones[:, :], scalar=-1.0 / HEAD,
                                                        in1=ident[:, :], op0=ALU.mult, op1=ALU.add))
                link.close()

    with ExitStack() as sc:
        lora_w = sb(sc, "lora_w", [P, RW])
        lora_g = sb(sc, "lora_g", [P, RW])
        segment = sb(sc, "segment", [P, RT, CH])
        gn_eps = sb(sc, "gn_eps", [P, 1])
        lora_x = sb(sc, "lora_x", [P, CH])
        sig_g = sb(sc, "sig_g", [P, CH])
        temps = p_even[:, 18:22, :].rearrange("p c (k t) -> p (c k) t", k=SEQ // CH // 4 * 4)
        names = ("decay", "logsum", "grow", "a", "kk", "norm", "k2", "rk")
        flat_temps = p_even[:, 18:22, :].rearrange("p c t -> p (c t)")
        T = {n: flat_temps[:, HALF * k:HALF * (k + 1)].rearrange("p (i t) -> p i t", i=RT)
             for k, n in enumerate(names)}
        v_now = sb(sc, "v_now", [P, RT, CH])
        mid = sb(sc, "mid", [P, RT])
        zr = sb(sc, "zr", [P, 2, RT, 2, CH])
        k_t = sb(sc, "k_t", [P, 2, RT, CH])
        b_t = sb(sc, "b_t", [P, 2, RT, CH])
        mid_scale = sb(sc, "mid_scale", [P, 2, RT])
        end_scale = sb(sc, "end_scale", [P, 2, RT])
        by_token = sb(sc, "by_token", [P, 4, RW])
        a_b = [sb(sc, f"a_b{g}", [P, RT, 2, CH]) for g in range(2)]
        a_k = [sb(sc, f"a_k{g}", [P, RT, 2, CH]) for g in range(2)]
        step_t = [sb(sc, f"step_t{g}", [P, RT, CH]) for g in range(2)]
        x_inv = [sb(sc, f"x_inv{g}", [P, RT, CH]) for g in range(2)]
        x_inv_t = [sb(sc, f"x_inv_t{g}", [P, RT, CH]) for g in range(2)]
        mx = [sb(sc, f"mx{g}", [P, RT, CH]) for g in range(2)]
        akv = sb(sc, "akv", [P, RW])
        w_t = sb(sc, "w_t", [P, RT, CH])
        sa = sb(sc, "sa", [P, RW])
        y_c = sb(sc, "y_c", [P, RT, CH])
        y_sq = sb(sc, "y_sq", [P, RT, CH])
        state = sb(sc, "state", [P, RT, HEAD])
        state_mid = sb(sc, "state_mid", [P, RT, HEAD])
        prep_ps = [ps(sc, f"prep_ps{k}", [P, HALF]) for k in range(2)]
        m = [ps(sc, f"main_ps{k}", [P, SEQ]) for k in range(3)]

        R7 = Rounds("r", {
            "act": {"lora_in": 3, "sigmoid": 2, "exps": 4, "squared": 1, "norm_root": 1, "g_kept": 1, "turned_kept": 4,
                    "mx0": 6, "mx1": 6, "akv": 1, "w_t": 1, "sa": 2, "y": 1, "y_sq": 2, "y_root": 1},
            "pe": {"lora": 3, "norm_sum": 1, "bonus_sum": 1, "turned": 4, "a_ps": 4, "mx_ps0": 7, "mx_ps1": 7,
                   "inc_ps0": 11, "inc_ps1": 11, "akv_ps": 1, "w_ps": 1, "sa_ps": 2, "y_ps": 1, "s_ps": 1,
                   "yc_ps": 1, "var_ps": 1},
            "dve": {"biased": 2, "kk_raw": 1, "logsum": 1, "mids": 1, "centred": 2, "k2": 2, "normed": 3, "rk": 2,
                    "b_raw": 1, "zrbk": 4, "ends": 1, "bonus": 1, "a_kept": 4, "x0": 13, "x1": 13,
                    "state_mid": 1, "state": 2, "gn": 6},
            "pool": {"v_now": 1, "step0": 7, "step1": 7},
        })
        start, wait, up = R7.start, R7.wait, R7.up

        def per_channel(name):
            return prm[:, COL[name]:COL[name] + RT].unsqueeze(2).to_broadcast([P, RT, CH])

        def over_tokens(ap, n=CH):
            return ap.unsqueeze(2).to_broadcast([P, RT, n])

        def tokens(first, n, c):
            return p_even[:, first:first + n, bass.ds(c * CH, CH)]

        def tt(out_, a, b, op):
            return nc.vector.tensor_tensor(out_, a, b, op)

        def psum4(ap):
            return ap.rearrange("p (i t) -> p i t", i=RT)

        def prep_act(act, c, s):
            wait(act, "lora", c, 3, back=1)
            up(nc.scalar.activation(lora_x[0:HEAD, :], p_even[0:HEAD, 12, bass.ds(c * CH, CH)], ACT.Tanh), "lora_in")
            up(nc.scalar.activation(lora_x[HEAD:P, :], p_even[HEAD:P, 12, bass.ds(c * CH, CH)], ACT.Copy), "lora_in")
            up(nc.scalar.activation(sig_g[:, :], p_even[:, 13, bass.ds(c * CH, CH)], ACT.Sigmoid), "lora_in")
            wait(act, "biased", c, 1)
            up(nc.scalar.activation(T["decay"], T["decay"], ACT.Sigmoid), "sigmoid")
            wait(act, "biased", c, 2)
            up(nc.scalar.activation(T["a"], T["a"], ACT.Sigmoid), "sigmoid")
            wait(act, "kk_raw", c)
            up(nc.scalar.activation(T["norm"], T["kk"], ACT.Square), "squared")
            wait(act, "k2", c, 2)
            wait(act, "lora", c, 3)
            up(nc.scalar.activation(tokens(4, RT, c), psum4(prep_ps[0]), ACT.Copy), "g_kept")
            wait(act, "norm_sum", c)
            up(nc.scalar.activation(T["norm"], psum4(prep_ps[1]), ACT.Sqrt), "norm_root")
            wait(act, "centred", c, 1)
            wait(act, "state_mid", c, back=2)
            up(nc.scalar.activation(mid_scale[:, s, :], mid[:, :], ACT.Exp, scale=-EXP_MINUS_HALF), "exps")
            up(nc.scalar.activation(T["grow"], T["logsum"], ACT.Exp, scale=EXP_MINUS_HALF), "exps")
            wait(act, "centred", c, 2)
            up(nc.scalar.activation(T["decay"], T["decay"], ACT.Exp, scale=-EXP_MINUS_HALF), "exps")
            wait(act, "exps", c, 2)
            up(nc.scalar.activation(T["logsum"], T["logsum"], ACT.Exp, scale=-EXP_MINUS_HALF), "exps")

        def prep_dve(dve, c, s):
            up(tt(T["kk"], tokens(4, RT, c), per_channel("e_k_k"), ALU.mult), "kk_raw")
            wait(dve, "lora", c, 1)
            up(tt(T["decay"], psum4(prep_ps[0]), per_channel("e_w0"), ALU.add), "biased")
            wait(dve, "lora", c, 2)
            up(tt(T["a"], psum4(prep_ps[1]), per_channel("e_a0"), ALU.add), "biased")
            wait(dve, "sigmoid", c, 1)
            up(nc.vector.tensor_tensor_scan(T["logsum"].rearrange("p i t -> p (i t)"),
                                            segment[:, :, :].rearrange("p i t -> p (i t)"),
                                            T["decay"].rearrange("p i t -> p (i t)"), 0.0, ALU.mult, ALU.add), "logsum")
            wait(dve, "logsum", c)
            wait(dve, "exps", c, 1, back=1)
            up(nc.vector.tensor_copy(mid[:, :], T["logsum"][:, :, CH // 2 - 1]), "mids")
            wait(dve, "mids", c)
            up(tt(T["logsum"], T["logsum"], over_tokens(mid[:, :]), ALU.subtract), "centred")
            wait(dve, "centred", c, 1)
            up(tt(T["decay"], T["logsum"], T["decay"], ALU.subtract), "centred")
            wait(dve, "sigmoid", c, 2)
            up(nc.vector.scalar_tensor_tensor(out=T["k2"], in0=T["a"], scalar=-1.0, in1=per_channel("e_k_a"),
                                              op0=ALU.add, op1=ALU.mult), "k2")
            wait(dve, "k2", c, 1)
            up(nc.vector.scalar_tensor_tensor(out=T["k2"], in0=T["k2"], scalar=1.0, in1=tokens(4, RT, c),
                                              op0=ALU.add, op1=ALU.mult), "k2")
            wait(dve, "k2", c, 2)
            up(tt(T["rk"], tokens(0, RT, c), T["k2"], ALU.mult), "rk")
            wait(dve, "rk", c, 1)
            up(tt(T["rk"], T["rk"], per_channel("e_r_k"), ALU.mult), "rk")
            wait(dve, "norm_root", c)
            up(nc.vector.tensor_scalar(T["norm"], T["norm"], 1e-12, None, ALU.max), "normed")
            wait(dve, "normed", c, 1)
            up(nc.vector.reciprocal(T["norm"], T["norm"]), "normed")
            wait(dve, "normed", c, 2)
            up(tt(T["kk"], T["kk"], T["norm"], ALU.mult), "normed")
            wait(dve, "normed", c, 3)
            wait(dve, "exps", c, 3)
            wait(dve, "y_ps", c, back=2)
            up(nc.vector.scalar_tensor_tensor(out=zr[:, s, :, 0, :], in0=T["kk"], scalar=-1.0, in1=T["decay"],
                                              op0=ALU.mult, op1=ALU.mult), "zrbk")
            up(tt(T["kk"], T["kk"], T["a"], ALU.mult), "b_raw")
            wait(dve, "b_raw", c)
            up(tt(b_t[:, s, :, :], T["kk"], T["grow"], ALU.mult), "zrbk")
            up(tt(k_t[:, s, :, :], T["k2"], T["grow"], ALU.mult), "zrbk")
            wait(dve, "exps", c, 4)
            up(tt(zr[:, s, :, 1, :], tokens(0, RT, c), T["logsum"], ALU.mult), "zrbk")
            up(nc.vector.tensor_copy(end_scale[:, s, :], T["logsum"][:, :, CH - 1]), "ends")
            wait(dve, "bonus_sum", c)
            wait(dve, "v_now", c)
            up(tt(tokens(8, RT, c), psum4(prep_ps[0]), v_now[:, :, :], ALU.mult), "bonus")

        def prep_pool(pool, c, s):
            wait(pool, "turned", c, 4, back=1)
            wait(pool, "bonus", c, back=1)
            up(pool.tensor_copy(v_now[:, :, :], tokens(8, RT, c)), "v_now")

        def prep_pe(pe, c, s):
            wait(pe, "lora_in", c, 3)
            wait(pe, "turned_kept", c, 4, back=1)
            for i in range(RT):
                last = nc.tensor.matmul(prep_ps[0][:, i * CH:(i + 1) * CH], lora_w[0:HEAD, i * P:(i + 1) * P],
                                        lora_x[0:HEAD, :], start=True, stop=True)
            up(last, "lora")
            for i in range(RT):
                last = nc.tensor.matmul(prep_ps[1][:, i * CH:(i + 1) * CH], lora_w[HEAD:P, i * P:(i + 1) * P],
                                        lora_x[HEAD:P, :], start=True, stop=True)
            up(last, "lora")
            wait(pe, "biased", c, 1)
            for i in range(RT):
                last = nc.tensor.matmul(prep_ps[0][:, i * CH:(i + 1) * CH], lora_g[:, i * P:(i + 1) * P],
                                        sig_g[:, :], start=True, stop=True)
            up(last, "lora")
            wait(pe, "biased", c, 2)
            wait(pe, "squared", c)
            up(nc.tensor.matmul(prep_ps[1][:, :], head_ones[:, :], T["norm"], start=True, stop=True), "norm_sum")
            wait(pe, "g_kept", c)
            wait(pe, "rk", c, 2)
            up(nc.tensor.matmul(prep_ps[0][:, :], head_ones[:, :], T["rk"], start=True, stop=True), "bonus_sum")

        def turn_pe(pe, c, s):
            wait(pe, "norm_root", c)
            wait(pe, "zrbk", c, 4)
            wait(pe, "v_now", c)
            for n, src in enumerate((zr[:, s, :, 0, :], b_t[:, s, :, :], k_t[:, s, :, :], v_now[:, :, :])):
                bank = prep_ps[(n + 1) % 2]
                if n == 1:
                    wait(pe, "bonus", c)
                if n >= 2:
                    wait(pe, "turned_kept", c, n - 1)
                for i in range(RT):
                    last = nc.tensor.transpose(bank[:, i * CH:(i + 1) * CH], src[:, i, :], ident[:, :])
                up(last, "turned")

        def turn_act(act, c, s):
            wait(act, "s_ps", c, back=1)
            wait(act, "y_ps", c, back=1)
            for n in range(4):
                wait(act, "turned", c, n + 1)
                up(nc.scalar.copy(by_token[:, n, :], prep_ps[(n + 1) % 2][:, :]), "turned_kept")

        def main_pe(pe, c, s):
            for n, (src, g) in enumerate(((b_t, 0), (b_t, 1), (k_t, 0), (k_t, 1))):
                if n == 0:
                    wait(pe, "y_root", c, back=1)
                if n == 1:
                    wait(pe, "y", c, back=1)
                if n == 2:
                    wait(pe, "state", c, 1, back=1)
                    wait(pe, "y_sq", c, 2, back=1)
                if n == 3:
                    wait(pe, "a_kept", c, 1)
                h = g * HEAD
                for i in range(RT):
                    last = nc.tensor.matmul(m[n % 3][:, i * 2 * CH:(i + 1) * 2 * CH], src[h:h + HEAD, s, i, :],
                                            zr[h:h + HEAD, s, i, :, :], start=True, stop=True)
                up(last, "a_ps")
            banks = [(m[0][:, 0:HALF], m[0][:, HALF:SEQ], m[1][:, 0:HALF]),
                     (m[1][:, HALF:SEQ], m[2][:, 0:HALF], m[2][:, HALF:SEQ])]
            for k in range(LEVELS):
                for g in range(2):
                    wait(pe, f"step{g}", c, k + 1)
                    if k == 0:
                        wait(pe, "a_kept", c, 4)
                    else:
                        wait(pe, f"x{g}", c, 2 * k)
                    for i in range(RT):
                        last = nc.tensor.matmul(banks[g][0][:, i * CH:(i + 1) * CH], step_t[g][:, i, :],
                                                ident[:, :] if k == 0 else x_inv[g][:, i, :], start=True, stop=True)
                    up(last, f"mx_ps{g}")
                if k == 0:
                    continue
                for g in range(2):
                    wait(pe, f"mx{g}", c, k)
                    for i in range(RT):
                        last = nc.tensor.matmul(banks[g][2][:, i * CH:(i + 1) * CH], mx[g][:, i, :],
                                                x_inv_t[g][:, i, :], start=True, stop=True)
                    up(last, f"inc_ps{g}")
                    if k < LEVELS - 1:
                        for i in range(RT):
                            last = nc.tensor.matmul(banks[g][1][:, i * CH:(i + 1) * CH], x_inv_t[g][:, i, :],
                                                    mx[g][:, i, :], start=True, stop=True)
                        up(last, f"inc_ps{g}")
            vt = by_token[:, 3, :]
            wait(pe, "turned_kept", c, 4)
            wait(pe, "mx0", c, 6)
            for h in range(HEADS):
                i, g = h // 2, h % 2
                last = nc.tensor.matmul(m[0][:, h * HEAD:(h + 1) * HEAD], a_k[g][:, i, 0, :],
                                        vt[:, h * HEAD:(h + 1) * HEAD], start=True, stop=True)
            up(last, "akv_ps")
            for g in range(2):
                wait(pe, f"x{g}", c, 13)
                for i in range(RT):
                    h = 2 * i + g
                    last = nc.tensor.matmul(m[0][g * HEAD:(g + 1) * HEAD, HALF + i * CH:HALF + (i + 1) * CH],
                                            by_token[:, 0, h * HEAD:(h + 1) * HEAD], x_inv_t[g][:, i, :],
                                            start=True, stop=True)
            up(last, "w_ps")
            wait(pe, "akv", c)
            wait(pe, "w_t", c)
            wait(pe, "state_mid", c)
            for g, bank in enumerate((m[1][:, 0:HALF], m[2][:, HALF:SEQ])):
                o = g * HEAD
                for i in range(RT):
                    h = 2 * i + g
                    dst = bank[:, i * HEAD:(i + 1) * HEAD]
                    nc.tensor.matmul(dst, x_inv_t[g][:, i, :], akv[:, h * HEAD:(h + 1) * HEAD],
                                     start=True, stop=False)
                    last = nc.tensor.matmul(dst, w_t[o:o + HEAD, i, :], state_mid[o:o + HEAD, i, :],
                                            start=False, stop=True)
                up(last, "sa_ps")
            wait(pe, "sa", c, 2)
            for h in range(HEADS):
                i, g = h // 2, h % 2
                o = g * HEAD
                dst = m[2][o:o + HEAD, i * HEAD:(i + 1) * HEAD]
                cols = slice(h * HEAD, (h + 1) * HEAD)
                nc.tensor.matmul(dst, by_token[:, 1, cols], sa[:, cols], start=True, stop=False)
                last = nc.tensor.matmul(dst, by_token[:, 2, cols], vt[:, cols], start=False, stop=True)
            up(last, "s_ps")
            for h in range(HEADS):
                i, g = h // 2, h % 2
                o = g * HEAD
                dst = m[1][o:o + HEAD, HALF + i * CH:HALF + (i + 1) * CH]
                cols = slice(h * HEAD, (h + 1) * HEAD)
                nc.tensor.matmul(dst, state_mid[o:o + HEAD, i, :], zr[o:o + HEAD, s, i, 1, :], start=True, stop=False)
                nc.tensor.matmul(dst, sa[:, cols], a_b[g][:, i, 1, :], start=False, stop=False)
                last = nc.tensor.matmul(dst, vt[:, cols], a_k[g][:, i, 1, :], start=False, stop=True)
            up(last, "y_ps")
            wait(pe, "y", c)
            up(nc.tensor.matmul(m[2][:, HALF:SEQ], centre[:, :], y_c[:, :, :], start=True, stop=True), "yc_ps")
            wait(pe, "y_sq", c, 2)
            up(nc.tensor.matmul(m[0][:, 0:HALF], head_ones[:, :], y_sq[:, :, :], start=True, stop=True), "var_ps")

        def main_act(act, c, s):
            for k in range(1, LEVELS):
                for g, bank in enumerate((m[0][:, 0:HALF], m[1][:, HALF:SEQ])):
                    wait(act, f"mx_ps{g}", c, k + 1)
                    up(nc.scalar.copy(mx[g][:, :, :], psum4(bank)), f"mx{g}")
            wait(act, "akv_ps", c)
            up(nc.scalar.copy(akv[:, :], m[0][:, 0:HALF]), "akv")
            wait(act, "w_ps", c)
            up(nc.scalar.copy(w_t[:, :, :], psum4(m[0][:, HALF:SEQ])), "w_t")
            by_half = sa[:, :].rearrange("p (i g v) -> p g i v", g=2, v=HEAD)
            for g, bank in enumerate((m[1][:, 0:RT * HEAD], m[2][:, HALF:HALF + RT * HEAD])):
                wait(act, "sa_ps", c, g + 1)
                up(nc.scalar.copy(by_half[:, g, :, :], bank.rearrange("p (i v) -> p i v", i=RT)), "sa")
            wait(act, "y_ps", c)
            wait(act, "gn", c, 6, back=1)
            up(nc.scalar.copy(y_c[:, :, :], psum4(m[1][:, HALF:SEQ])), "y")
            wait(act, "yc_ps", c)
            up(nc.scalar.activation(y_c[:, :, :], psum4(m[2][:, HALF:SEQ]), ACT.Copy), "y_sq")
            up(nc.scalar.activation(y_sq[:, :, :], psum4(m[2][:, HALF:SEQ]), ACT.Square), "y_sq")
            wait(act, "var_ps", c)
            up(nc.scalar.activation(y_sq[:, :, :], psum4(m[0][:, 0:HALF]), ACT.Sqrt, scale=1.0 / HEAD,
                                    bias=gn_eps[:, 0:1]), "y_root")

        def main_dve(dve, c, s):
            wait(dve, "exps", c, 1)
            wait(dve, "state", c, 2, back=1)
            up(tt(state_mid[:, :, :], state[:, :, :], over_tokens(mid_scale[:, s, :], HEAD), ALU.mult), "state_mid")
            mask = causal[:, :, :].rearrange("p a t -> p (a t)").unsqueeze(1).to_broadcast([P, RT, 2 * CH])
            for n, dst in enumerate((a_b[0], a_b[1], a_k[0], a_k[1])):
                wait(dve, "a_ps", c, n + 1)
                up(tt(dst[:, :, :, :].rearrange("p i a t -> p i (a t)"),
                      m[n % 3][:, :].rearrange("p (i a) -> p i a", i=RT), mask, ALU.mult), "a_kept")
            eye = ident[:, :].unsqueeze(1).to_broadcast([P, RT, CH])
            for g, bank in enumerate((m[0][:, 0:HALF], m[1][:, HALF:SEQ])):
                wait(dve, f"mx_ps{g}", c, 1)
                up(tt(x_inv[g][:, :, :], psum4(bank), eye, ALU.add), f"x{g}")
                up(tt(x_inv_t[g][:, :, :], step_t[g][:, :, :], eye, ALU.add), f"x{g}")
            for k in range(1, LEVELS):
                for g, (inc, inc_t) in enumerate(((m[0][:, HALF:SEQ], m[1][:, 0:HALF]),
                                                  (m[2][:, 0:HALF], m[2][:, HALF:SEQ]))):
                    wait(dve, f"x{g}", c, 2 * k)
                    wait(dve, f"inc_ps{g}", c, 2 * k if k < LEVELS - 1 else 2 * k - 1)
                    if k < LEVELS - 1:
                        up(tt(x_inv[g][:, :, :], x_inv[g][:, :, :], psum4(inc), ALU.add), f"x{g}")
                    up(tt(x_inv_t[g][:, :, :], x_inv_t[g][:, :, :], psum4(inc_t), ALU.add), f"x{g}")
            wait(dve, "s_ps", c)
            up(tt(state[:, :, :], state_mid[:, :, :], m[2][:, 0:RT * HEAD].rearrange("p (i v) -> p i v", i=RT),
                  ALU.add), "state")
            wait(dve, "state", c, 1)
            up(tt(state[:, :, :], state[:, :, :], over_tokens(end_scale[:, s, :], HEAD), ALU.mult), "state")
            wait(dve, "y_root", c)
            up(nc.vector.reciprocal(y_sq[:, :, :], y_sq[:, :, :]), "gn")
            wait(dve, "gn", c, 1)
            up(tt(y_c[:, :, :], y_c[:, :, :], y_sq[:, :, :], ALU.mult), "gn")
            wait(dve, "gn", c, 2)
            up(tt(y_c[:, :, :], y_c[:, :, :], per_channel("e_ln_w"), ALU.mult), "gn")
            wait(dve, "gn", c, 3)
            up(tt(y_c[:, :, :], y_c[:, :, :], per_channel("e_ln_b"), ALU.add), "gn")
            wait(dve, "gn", c, 4)
            up(tt(y_c[:, :, :], y_c[:, :, :], tokens(8, RT, c), ALU.add), "gn")
            wait(dve, "gn", c, 5)
            up(tt(tokens(0, RT, c), y_c[:, :, :], tokens(4, RT, c), ALU.mult), "gn")

        def main_pool(pool, c, s):
            for k in range(LEVELS):
                for g in range(2):
                    if k == 0:
                        wait(pool, "a_kept", c, g + 1)
                        wait(pool, f"mx_ps{g}", c, LEVELS, back=1)
                    else:
                        wait(pool, f"mx_ps{g}", c, k)
                    if k == 1:
                        wait(pool, f"x{g}", c, 2)
                    up(pool.tensor_tensor(step_t[g][:, :, :], a_b[g][:, :, 0, :],
                                          level_mask[:, k, :].unsqueeze(1).to_broadcast([P, RT, CH]), op=ALU.mult),
                       f"step{g}")

        lora_loaded, r_consts = sem("lora_loaded"), sem("r_consts")
        with nc.Block() as block:
            @block.sync
            def _(sp):
                sp.dma_start(lora_w[0:HEAD, :], io["e_w2"][0, :, :]).then_inc(lora_loaded, 16)
                sp.dma_start(lora_w[HEAD:P, :], io["e_a2"][0, :, :]).then_inc(lora_loaded, 16)
                sp.dma_start(lora_g[:, :], io["e_g2"][0, :, :]).then_inc(lora_loaded, 16)

            @block.scalar
            def _(act):
                start(act, "act")
                act.wait_ge(r_consts, 5)
                with act.Fori(0, NCH // 2) as n:
                    for s in range(2):
                        c = n * 2 + s
                        prep_act(act, c, s)
                        turn_act(act, c, s)
                        main_act(act, c, s)

            @block.vector
            def _(dve):
                start(dve, "dve")
                nc.vector.memset(segment[:, :, :], 1.0).then_inc(r_consts, 1)
                nc.vector.memset(state[:, :, :], 0.0).then_inc(r_consts, 1)
                nc.vector.memset(gn_eps[:, :], GN_EPS).then_inc(r_consts, 1)
                dve.wait_ge(r_consts, 3)
                nc.vector.memset(segment[:, :, 0:1], 0.0).then_inc(r_consts, 1)
                dve.wait_ge(r_consts, 4)
                dve.sem_inc(r_consts, 1)
                with dve.Fori(0, NCH // 2) as n:
                    for s in range(2):
                        c = n * 2 + s
                        prep_dve(dve, c, s)
                        main_dve(dve, c, s)

            @block.gpsimd
            def _(pool):
                start(pool, "pool")
                with pool.Fori(0, NCH // 2) as n:
                    for s in range(2):
                        c = n * 2 + s
                        prep_pool(pool, c, s)
                        main_pool(pool, c, s)

            @block.tensor
            def _(pe):
                start(pe, "pe")
                pe.wait_ge(lora_loaded, 48)
                pe.wait_ge(r_consts, 5)
                with pe.Fori(0, NCH // 2) as n:
                    for s in range(2):
                        c = n * 2 + s
                        prep_pe(pe, c, s)
                        turn_pe(pe, c, s)
                        main_pe(pe, c, s)

    Dense.q, Dense.u = 2 * EV, EV

    def residual_add_dve(dve, dn, c, slot, pair, par):
        dn.wait_unit(dve, pair, par)
        here = x_res[:, bass.ds(c, 1), :]
        nc.vector.tensor_tensor(here, here, dn.acc[slot][:, :], ALU.add).then_inc(unit_free, 1)

    with ExitStack() as sc:
        y_hi = sb(sc, "y_hi", [P, DT, SEQ], F32R)
        y_lo = sb(sc, "y_lo", [P, DT, SEQ], F32R)
        dn = Dense(sc, "o")
        w_out = io["e_w_out"].rearrange("a (k p) n -> (a p) k n", p=P)
        y_hi_done, y_lo_done = sem("y_hi_done"), sem("y_lo_done")
        y_tiles = (0, 1, 2, 3, 14, 15, 16, 17)
        q0, u0 = Dense.q // 2, Dense.u
        with nc.Block() as block:
            @block.sync
            def _(sp):
                with sp.Fori(0, DT // 2) as i:
                    for s in range(2):
                        dn.load(sp, w_out, DT, bass.ds(i * (2 * P) + s * P, P), i * 2 + (q0 + s), 0)

            @block.gpsimd
            def _(pool):
                with pool.Fori(0, DT // 2) as i:
                    for s in range(2):
                        dn.take_lo(pool, DT, i * 2 + (q0 + s), 0)

            @block.scalar
            def _(act):
                for k, tile in enumerate(y_tiles):
                    nc.scalar.copy(y_hi[:, k, :], p_even[:, tile, :]).then_inc(y_hi_done, 1)
                with act.Fori(0, DT // 2) as i:
                    for s in range(2):
                        dn.take_hi(act, DT, i * 2 + (q0 + s), 0)

            @block.tensor
            def _(pe):
                pe.wait_ge(y_lo_done, DT)
                with pe.Fori(0, DT // 2) as i:
                    for s in range(2):
                        dn.product(pe, DT, y_hi, y_lo, i * 2 + (u0 + s), s, i * 2 + (q0 + s), 0)

            @block.vector
            def _(dve):
                for k, tile in enumerate(y_tiles):
                    dve.wait_ge(y_hi_done, k + 1)
                    nc.vector.tensor_tensor(y_lo[:, k, :], p_even[:, tile, :], y_hi[:, k, :].bitcast(F32),
                                            ALU.subtract).then_inc(y_lo_done, 1)
                with dve.Fori(0, DT // 2) as i:
                    for s in range(2):
                        residual_add_dve(dve, dn, i * 2 + s, s, i * 2 + (q0 + s), 1)
        Dense.q += 2 * DT
        Dense.u += DT
    proj.close()

    def conv_ffn(layer):
        tag = f"f{layer}"
        with ExitStack() as sc:
            xn_hi = sb(sc, "xn_hi_" + tag, [P, DT, SEQ], F32R)
            xn_lo = sb(sc, "xn_lo_" + tag, [P, DT, SEQ], F32R)
            norm(tag, "f_norm_g", DT * layer, xn_hi, xn_lo)
            dn = Dense(sc, tag)
            h_hi = sb(sc, "h_hi_" + tag, [P, FGROUP, SEQ], F32R)
            h_lo = sb(sc, "h_lo_" + tag, [P, FGROUP, SEQ], F32R)
            gate = sb(sc, "gate_" + tag, [P, SEQ])
            val = sb(sc, "val_" + tag, [P, SEQ])
            w_up = io["f_w_up"][layer, :, :].rearrange("(k p) n -> p k n", p=P)
            w_down = io["f_w_down"][layer, :, :].rearrange("(g k p) n -> g p k n", g=2, p=P)
            f_start, f_tap, f_silu, f_h, f_hi, f_lo = (
                sem("f_" + n) for n in ("start", "tap", "silu", "h", "hi", "lo"))
            made = layer * FT
            UP = 2 * FGROUP
            PAIRS = UP + 3 * DT // 2
            UNITS = 2 * FGROUP + DT
            q0, u0 = Dense.q // 2, Dense.u
            taps, bias = COL["f_conv_w"] + layer * 3 * 2 * FT, COL["f_conv_b"] + layer * 2 * FT

            def param(first, tile):
                return prm[:, bass.ds(tile + first, 1)]

            def tile_of(g, m, half):
                return g * FGROUP + m + half * FT

            def up_cols(g, m, half):
                return bass.ds(g * (FGROUP * P) + m * P + half * D_FF, P)

            def up_pair(g, m, half):
                return g * PAIRS + m * 2 + (half + q0)

            def up_unit(g, m, half):
                return g * UNITS + m * 2 + (half + u0)

            with nc.Block() as block:
                @block.sync
                def _(sp):
                    with sp.Fori(0, 2) as g:
                        with sp.Fori(0, FGROUP) as m:
                            for half in range(2):
                                dn.load(sp, w_up, DT, up_cols(g, m, half), up_pair(g, m, half), 0)
                        with sp.Fori(0, DT // 2) as i:
                            for s in range(2):
                                dn.load(sp, w_down[bass.ds(g, 1), :, :, :].rearrange("g p k n -> (g p) k n"), FGROUP,
                                        bass.ds(i * (2 * P) + s * P, P), g * PAIRS + i * 3 + (UP + q0 + s), s)

                @block.tensor
                def _(pe):
                    with pe.Fori(0, 2) as g:
                        with pe.Fori(0, FGROUP) as m:
                            for half in range(2):
                                dn.product(pe, DT, xn_hi, xn_lo, up_unit(g, m, half), half, up_pair(g, m, half), 0)
                        with pe.Fori(0, DT // 2) as i:
                            for s in range(2):
                                pe.wait_ge(f_lo, g * FGROUP + (made + FGROUP + 1))
                                dn.product(pe, FGROUP, h_hi, h_lo, g * UNITS + i * 2 + (2 * FGROUP + u0 + s), s,
                                           g * PAIRS + i * 3 + (UP + q0 + s), s)

                @block.scalar
                def _(act):
                    def begin(g, m, half):
                        act.wait_ge(f_lo if half else f_h, g * FGROUP + m + (made + 1))
                        dn.wait_unit(act, up_pair(g, m, half), 1)
                        nc.scalar.activation((gate, val)[half][:, :], dn.acc[half][:, :], ACT.Identity,
                                             scale=param(taps + 2 * 2 * FT, tile_of(g, m, half)),
                                             bias=param(bias, tile_of(g, m, half))).then_inc(f_start, 1)

                    def silu(g, m):
                        act.wait_ge(unit_free, up_unit(g, m, 0) + 3)
                        nc.scalar.activation(gate[:, :], gate[:, :], ACT.Silu).then_inc(f_silu, 1)

                    def keep_hi(g, m):
                        act.wait_ge(f_h, g * FGROUP + m + (made + 2))
                        nc.scalar.copy(h_hi[:, bass.ds(m, 1), :], val[:, :]).then_inc(f_hi, 1)

                    with act.Fori(0, 2) as g:
                        dn.take_hi(act, DT, g * PAIRS + q0, 0)
                        dn.take_hi(act, DT, g * PAIRS + (q0 + 1), 0)
                        begin(g, 0, 0)
                        silu(g, 0)
                        with act.Fori(1, FGROUP) as m:
                            dn.take_hi(act, DT, up_pair(g, m, 0), 0)
                            begin(g, m + (-1), 1)
                            keep_hi(g, m + (-1))
                            dn.take_hi(act, DT, up_pair(g, m, 1), 0)
                            begin(g, m, 0)
                            silu(g, m)
                        begin(g, FGROUP - 1, 1)
                        keep_hi(g, FGROUP - 1)
                        with act.Fori(0, DT // 2) as i:
                            for s in range(2):
                                dn.take_hi(act, FGROUP, g * PAIRS + i * 3 + (UP + q0 + s), s)

                @block.vector
                def _(dve):
                    with dve.Fori(0, 2) as g:
                        with dve.Fori(0, FGROUP) as m:
                            for half in range(2):
                                n = g * (2 * FGROUP) + m * 2 + (half + 2 * made)
                                dve.wait_ge(f_start, n + 1)
                                for back in (1, 2):
                                    here = (gate, val)[half][:, back:SEQ]
                                    if back == 2:
                                        dve.wait_ge(f_tap, n + 1)
                                    nc.vector.scalar_tensor_tensor(
                                        out=here, in0=dn.acc[half][:, 0:SEQ - back],
                                        scalar=param(taps + (2 - back) * 2 * FT, tile_of(g, m, half)), in1=here,
                                        op0=ALU.mult, op1=ALU.add).then_inc(f_tap if back == 1 else unit_free, 1)
                        with dve.Fori(0, DT // 2) as i:
                            residual_add_dve(dve, dn, i * 2, 0, g * PAIRS + i * 3 + (UP + q0 + 1), 0)
                            residual_add_dve(dve, dn, i * 2 + 1, 1, g * PAIRS + i * 3 + (UP + q0 + 2), 1)

                @block.gpsimd
                def _(pool):
                    def inner(g, m):
                        pool.wait_ge(f_silu, g * FGROUP + m + (made + 1))
                        pool.wait_ge(unit_free, up_unit(g, m, 1) + 3)
                        pool.tensor_tensor(val[:, :], gate[:, :], val[:, :], op=ALU.mult).then_inc(f_h, 1)
                        pool.wait_ge(f_hi, g * FGROUP + m + (made + 1))
                        pool.tensor_tensor(h_lo[:, bass.ds(m, 1), :], val[:, :],
                                           h_hi[:, bass.ds(m, 1), :].bitcast(F32), op=ALU.subtract).then_inc(f_lo, 1)

                    if layer == 0:
                        pool.sem_inc(f_h, 1)
                        pool.sem_inc(f_lo, 1)
                    with pool.Fori(0, 2) as g:
                        dn.take_lo(pool, DT, g * PAIRS + q0, 0)
                        dn.take_lo(pool, DT, g * PAIRS + (q0 + 1), 0)
                        with pool.Fori(1, FGROUP) as m:
                            dn.take_lo(pool, DT, up_pair(g, m, 0), 0)
                            inner(g, m + (-1))
                            dn.take_lo(pool, DT, up_pair(g, m, 1), 0)
                        inner(g, FGROUP - 1)
                        with pool.Fori(0, DT // 2) as i:
                            for s in range(2):
                                dn.take_lo(pool, FGROUP, g * PAIRS + i * 3 + (UP + q0 + s), s)
            Dense.q += 2 * 2 * PAIRS
            Dense.u += 2 * UNITS

    conv_ffn(0)

    s5 = ctx.enter_context(ExitStack())
    u_s5 = sb(s5, "u_s5", [P, DT, SEQ])
    K9 = L5 + 1
    rot = sb(s5, "rot", [P, 2, S5_PAIRS, N5])
    power = sb(s5, "power", [P, 2, K9, S5_PAIRS])
    b_bar = sb(s5, "b_bar", [P, 2, S5_PAIRS, 16])
    c_s5 = sb(s5, "c_s5", [P, 3, S5_PAIRS, 16])
    decay8 = sb(s5, "decay8", [P, S5_PAIRS])
    with ExitStack() as sc:
        xn_hi = sb(sc, "xn_hi_s", [P, DT, SEQ], F32R)
        xn_lo = sb(sc, "xn_lo_s", [P, DT, SEQ], F32R)
        norm("s", "o_norm_g", 0, xn_hi, xn_lo)
        dn = Dense(sc, "s")
        s_rows = sb(sc, "s_rows", [S5_PAIRS, 3, P])
        dt_rows = sb(sc, "dt_rows", [S5_PAIRS, 2])
        b_raw = sb(sc, "b_raw", [P, 2, S5_PAIRS, 16])
        c_raw = sb(sc, "c_raw", [P, DT, 2, 64])
        small = sb(sc, "small", [P, 20, S5_PAIRS])
        s_ps = ps(sc, "s_ps", [P, 3, S5_PAIRS])
        c_ps = ps(sc, "c_ps", [P, SEQ])
        w_in = io["o_w_in"].rearrange("a (k p) n -> (a p) k n", p=P)
        s_loaded, c_loaded, s_turned, c_turned, dt_wide = (
            sem(n) for n in ("s_loaded", "c_loaded", "s_turned", "c_turned", "dt_wide"))
        s_act, s_arg, c_kept = sem("s_act"), sem("s_arg"), sem("c_kept")
        q0, u0 = Dense.q // 2, Dense.u
        V = {n: small[:, k, :] for k, n in enumerate(
            "lre dt lr ang turns mag s2 h c2 cos sin zr den qre qim t1 t2 ck sk aim".split())}
        TWO_PI = 6.283185307179586
        TURN1 = 6.28125
        TURN2 = 0.0019340515136718750
        TURN3 = TWO_PI - TURN1 - TURN2
        ROUND = 12582912.0
        with nc.Block() as block:
            @block.sync
            def _(sp):
                for k, name in enumerate(("o_A_re", "o_A_im")):
                    sp.dma_start(s_rows[:, k, :], io[name].rearrange("a (r g) n -> (a r) (g n)", g=2)).then_inc(s_loaded, 16)
                sp.dma_start(dt_rows[:, :], io["o_log_dt"].rearrange("a (r g) -> (a r) g", g=2)).then_inc(s_loaded, 16)
                for k in range(2):
                    sp.dma_start(c_raw[:, :, k, :], io["o_C_re"].rearrange("a (t g) c n -> (a g c) t n", g=8)).then_inc(c_loaded, 16)
                for k, name in enumerate(("o_B_re", "o_B_im")):
                    b = io[name].rearrange("a (r g) n c -> (a g) n r c", g=2)
                    for g in range(2):
                        sp.dma_start(b_raw[g * 64:(g + 1) * 64, k, :, :], b[g, :, :, :]).then_inc(s_loaded, 16)
                with sp.Fori(0, DT // 2) as i:
                    for s in range(2):
                        dn.load(sp, w_in, DT, bass.ds(i * (2 * P) + s * P, P), i * 2 + (q0 + s), 0)
                sp.wait_ge(c_turned, 1)
                for k in range(2):
                    sp.dma_start(c_raw[:, :, k, :], io["o_C_im"].rearrange("a (t g) c n -> (a g c) t n", g=8)).then_inc(c_loaded, 16)

            @block.gpsimd
            def _(pool):
                with pool.Fori(0, DT // 2) as i:
                    for s in range(2):
                        dn.take_lo(pool, DT, i * 2 + (q0 + s), 0)

            @block.tensor
            def _(pe):
                pe.wait_ge(s_loaded, 7 * 16)
                pe.wait_ge(dt_wide, 1)
                for k in range(3):
                    last = nc.tensor.transpose(s_ps[:, k, :], s_rows[:, k, :], ident[0:S5_PAIRS, 0:S5_PAIRS])
                last.then_inc(s_turned, 1)

                def turn_c(n):
                    pe.wait_ge(c_loaded, 32 * (n + 1))
                    for t in range(DT):
                        last = nc.tensor.transpose(c_ps[:, t * P:(t + 1) * P],
                                                   c_raw[:, t, :, :].rearrange("p k n -> p (k n)"), ident[:, :])
                    last.then_inc(c_turned, 1)

                turn_c(0)
                with pe.Fori(0, DT // 2) as i:
                    for s in range(2):
                        dn.product(pe, DT, xn_hi, xn_lo, i * 2 + (u0 + s), s, i * 2 + (q0 + s), 0)
                pe.wait_ge(c_kept, 2)
                turn_c(1)

            @block.scalar
            def _(act):
                def keep_u(i, slot):
                    dn.wait_unit(act, i + q0, 1)
                    nc.scalar.copy(u_s5[:, bass.ds(i, 1), :].rearrange("p a (j n) -> p (a j) n", j=L5),
                                   dn.acc[slot][:, :].rearrange("p (n j) -> p j n", j=L5)).then_inc(unit_free, 1)

                act.wait_ge(s_arg, 1)
                nc.scalar.activation(V["dt"], V["dt"], ACT.Exp).then_inc(s_act, 1)
                act.wait_ge(s_arg, 2)
                nc.scalar.activation(V["mag"], V["lr"], ACT.Exp).then_inc(s_act, 1)
                act.wait_ge(s_arg, 3)
                nc.scalar.activation(V["s2"], V["h"], ACT.Sin).then_inc(s_act, 1)
                act.wait_ge(s_arg, 4)
                nc.scalar.activation(V["c2"], V["c2"], ACT.Sin).then_inc(s_act, 1)
                with act.Fori(0, DT // 2) as i:
                    for s in range(2):
                        dn.take_hi(act, DT, i * 2 + (q0 + s), 0)
                        keep_u(i * 2 + s, s)

            @block.vector
            def _(dve):
                link = Link(dve, "s5_setup")

                def mul(o, a, b, op=ALU.mult):
                    link.run(nc.vector.tensor_tensor(o, a, b, op))

                def affine(o, a, k1, k2=None, op0=ALU.mult, op1=ALU.add):
                    link.run(nc.vector.tensor_scalar(o, a, k1, k2, op0, op1) if k2 is not None
                             else nc.vector.tensor_scalar(o, a, k1, None, op0))

                def fused(o, a, k, b, op0=ALU.mult, op1=ALU.add):
                    link.run(nc.vector.scalar_tensor_tensor(out=o, in0=a, scalar=k, in1=b, op0=op0, op1=op1))

                def keep_c(n):
                    dve.wait_ge(c_turned, n + 1)
                    for g in range(2):
                        half = slice(g * 64, (g + 1) * 64)
                        src = c_ps[half, :].rearrange("p (r g c) -> p g r c", g=2, c=16)
                        nc.vector.tensor_copy(c_s5[half, n, :, :], src[:, g, :, :]).then_inc(c_kept, 1)

                dve.wait_ge(s_loaded, 7 * 16)
                nc.vector.tensor_copy(s_rows[:, 2, :].rearrange("p (g n) -> p g n", g=2),
                                      dt_rows[:, :].unsqueeze(2).to_broadcast([S5_PAIRS, 2, 64])).then_inc(dt_wide, 1)
                dve.wait_ge(s_turned, 1)
                affine(V["lre"], s_ps[:, 0, :], -1e-4, None, ALU.min)
                link.run(nc.vector.tensor_copy(V["aim"], s_ps[:, 1, :]))
                nc.vector.tensor_copy(V["dt"], s_ps[:, 2, :]).then_inc(s_arg, 1)
                dve.wait_ge(s_act, 1)
                mul(V["ang"], V["aim"], V["dt"])
                nc.vector.tensor_tensor(V["lr"], V["lre"], V["dt"], ALU.mult).then_inc(s_arg, 1)
                affine(V["turns"], V["ang"], 1 / TWO_PI, ROUND)
                affine(V["turns"], V["turns"], -ROUND, None, ALU.add)
                fused(V["ang"], V["turns"], -TURN1, V["ang"])
                fused(V["ang"], V["turns"], -TURN2, V["ang"])
                fused(V["ang"], V["turns"], -TURN3, V["ang"])
                dve.wait_ge(s_arg, 2)
                nc.vector.tensor_scalar(V["h"], V["ang"], 0.5, None, ALU.mult).then_inc(s_arg, 1)
                dve.wait_ge(s_arg, 3)
                fused(V["c2"], V["h"], -1.0, V["h"], ALU.mult, ALU.max)
                nc.vector.tensor_scalar(V["c2"], V["c2"], -1.0, TWO_PI / 4, ALU.mult, ALU.add).then_inc(s_arg, 1)
                dve.wait_ge(s_act, 4)
                fused(V["sin"], V["s2"], 2.0, V["c2"], ALU.mult, ALU.mult)
                mul(V["t1"], V["s2"], V["s2"])
                affine(V["cos"], V["t1"], -2.0, 1.0)
                link.run(nc.vector.memset(power[:, 0, 0, :], 1.0))
                link.run(nc.vector.memset(power[:, 1, 0, :], 0.0))
                a_re, a_im = power[:, 0, 1, :], power[:, 1, 1, :]
                mul(a_re, V["mag"], V["cos"])
                mul(a_im, V["mag"], V["sin"])
                for k in range(2, K9):
                    for part, op in ((0, ALU.subtract), (1, ALU.add)):
                        mul(V["t1"], power[:, 0, k - 1, :], (a_re, a_im)[part])
                        mul(V["t2"], power[:, 1, k - 1, :], (a_im, a_re)[part])
                        mul(power[:, part, k, :], V["t1"], V["t2"], op)
                mul(V["t1"], V["lre"], V["lre"])
                mul(V["t2"], V["aim"], V["aim"])
                mul(V["den"], V["t1"], V["t2"], ALU.add)
                link.run(nc.vector.reciprocal(V["den"], V["den"]))
                affine(V["zr"], a_re, -1.0, None, ALU.add)
                for q, x, y, op in ((V["qre"], V["zr"], a_im, ALU.add), (V["qim"], a_im, V["zr"], ALU.subtract)):
                    mul(V["t1"], x, V["lre"])
                    mul(V["t2"], y, V["aim"])
                    mul(V["t1"], V["t1"], V["t2"], op)
                    mul(q, V["t1"], V["den"])
                wide = [P, S5_PAIRS, 16]
                q_re, q_im = (V[n].unsqueeze(2).to_broadcast(wide) for n in ("qre", "qim"))
                tmp = rot[:, 1, 0:4, :].rearrange("p r n -> p (r n)").rearrange("p (r c) -> p r c", c=16)
                mul(b_bar[:, 0, :, :], b_raw[:, 0, :, :], q_re)
                mul(tmp, b_raw[:, 1, :, :], q_im)
                mul(b_bar[:, 0, :, :], b_bar[:, 0, :, :], tmp, ALU.subtract)
                mul(b_bar[:, 1, :, :], b_raw[:, 1, :, :], q_re)
                mul(tmp, b_raw[:, 0, :, :], q_im)
                mul(b_bar[:, 1, :, :], b_bar[:, 1, :, :], tmp, ALU.add)
                keep_c(0)
                mul(V["mag"], V["mag"], V["mag"])
                mul(V["mag"], V["mag"], V["mag"])
                mul(decay8[:, :], V["mag"], V["mag"])
                link.run(nc.vector.tensor_copy(V["ck"], V["cos"]))
                link.run(nc.vector.tensor_copy(V["sk"], V["sin"]))

                def square_turn():
                    mul(V["t1"], V["ck"], V["ck"])
                    mul(V["t2"], V["sk"], V["sk"])
                    fused(V["sk"], V["ck"], 2.0, V["sk"], ALU.mult, ALU.mult)
                    mul(V["ck"], V["t1"], V["t2"], ALU.subtract)

                for _ in range(3):
                    square_turn()
                link.run(nc.vector.memset(rot[:, 0, :, 0:1], 1.0))
                link.run(nc.vector.memset(rot[:, 1, :, 0:1], 0.0))
                n = 1
                while n < N5:
                    for lo in range(0, S5_PAIRS, 8):
                        r = slice(lo, lo + 8)
                        step = [P, 8, n]
                        ck, sk = (V[x][:, r].unsqueeze(2).to_broadcast(step) for x in ("ck", "sk"))
                        cos, sin = rot[:, 0, r, 0:n], rot[:, 1, r, 0:n]
                        new = [rot[:, k, r, n:2 * n] for k in range(2)]
                        part = b_raw[:, 0, :, :].rearrange("p r c -> p (r c)")[:, 0:8 * n].rearrange("p (r n) -> p r n", r=8)
                        for k, (x, y, op) in enumerate(((cos, sin, ALU.subtract), (sin, cos, ALU.add))):
                            mul(new[k], x, ck)
                            mul(part, y, sk)
                            mul(new[k], new[k], part, op)
                    n *= 2
                    if n < N5:
                        square_turn()
                keep_c(1)
                dve.wait_ge(c_kept, 4)
                affine(c_s5[:, 2, :, :], c_s5[:, 0, :, :], -1.0)
                link.close()
        Dense.q += 2 * DT
        Dense.u += DT

    with ExitStack() as sc:
        gx = sb(sc, "gx", [P, 2, L5, 4, 2, 16])
        hx = sb(sc, "hx", [P, 2, 2, K9, 4, 2, 16])
        g_in = sb(sc, "g_in", [P, L5, 2, P])
        k_fir = sb(sc, "k_fir", [P, L5, P])
        u_now = sb(sc, "u_now", [P, 2, L5, N5])
        m1 = sb(sc, "m1", [P, K9, 4, 16])
        m2 = sb(sc, "m2", [P, K9, 4, 16])
        m3 = sb(sc, "m3", [P, K9, 4, 16])
        m4 = sb(sc, "m4", [P, K9, 4, 16])
        first0 = sb(sc, "first0", [P, 4, N5])
        keep8 = sb(sc, "keep8", [P, 4, N5])
        f_hat = sb(sc, "f_hat", [P, 2, 4, N5])
        s_hat = sb(sc, "s_hat", [P, 2, 4, N5])
        r_tmp = sb(sc, "r_tmp", [P, 2, 4, N5])
        s_prev = sb(sc, "s_prev", [P, 2, 2, 4, N5])
        f_ps = ps(sc, "f_ps", [P, 4, 2, 2 * N5])
        y_ps = ps(sc, "y5_ps", [P, L5, N5])
        tk_ps = [ps(sc, f"tk_ps{k}", [P, HALF]) for k in range(2)]
        R5 = Rounds("s5", {
            "pool": {"m": 8, "gx": 4, "hx": 4},
            "pe": {"turn": 4, "k": 1, "f": 1, "fir": 1, "y": 1},
            "act": {"u": 1, "g": 4, "out": 1},
            "dve": {"keep8": 1, "k_kept": 5, "rin": 6, "scan": 2, "rout": 6},
        })
        s5_clear = sem("s5_clear")

        def make_pool(pool, i, s):
            def pw(part, n):
                return power[:, part, 0:n, bass.ds(i * 4, 4)].unsqueeze(3).to_broadcast([P, n, 4, 16])

            def over_k(t, n):
                return t[:, bass.ds(i * 4, 4), :].unsqueeze(1).to_broadcast([P, n, 4, 16])

            b_re, b_im = (over_k(b_bar[:, k, :, :], L5) for k in range(2))
            c_re, c_im, c_neg = (over_k(c_s5[:, k, :, :], K9) for k in range(3))
            R5.wait(pool, "gx", i, 4, back=1)
            R5.wait(pool, "hx", i, 4, back=1)
            for o, a, b in ((m1, pw(0, L5), b_re), (m2, pw(1, L5), b_im), (m3, pw(0, L5), b_im), (m4, pw(1, L5), b_re)):
                R5.up(pool.tensor_tensor(o[:, 0:L5, :, :], a, b, op=ALU.mult), "m")
            R5.wait(pool, "m", i, 4)
            R5.wait(pool, "turn", i, 4, back=1)
            R5.wait(pool, "k", i, 1, back=1)
            for part, (a, b, op) in enumerate(((m1, m2, ALU.subtract), (m3, m4, ALU.add))):
                for g in range(2):
                    half = slice(g * 64, (g + 1) * 64)
                    R5.up(pool.tensor_tensor(gx[half, part, :, :, g, :], a[half, 0:L5, :, :], b[half, 0:L5, :, :], op=op), "gx")
            R5.wait(pool, "gx", i, 4)
            for o, a, b in ((m1, c_re, pw(0, K9)), (m2, c_im, pw(1, K9)), (m3, c_neg, pw(1, K9)), (m4, c_im, pw(0, K9))):
                R5.up(pool.tensor_tensor(o[:, :, :, :], a, b, op=ALU.mult), "m")
            R5.wait(pool, "m", i, 8)
            R5.wait(pool, "y", i, 1, back=2)
            for part, (a, b) in enumerate(((m1, m2), (m3, m4))):
                for g in range(2):
                    half = slice(g * 64, (g + 1) * 64)
                    R5.up(pool.tensor_tensor(hx[half, s, part, :, :, g, :], a[half, :, :, :], b[half, :, :, :],
                                             op=ALU.subtract), "hx")

        def turn_pe(pe, i, s):
            R5.wait(pe, "gx", i, 4)
            for n in range(4):
                if n == 0:
                    R5.wait(pe, "g", i, 3, back=1)
                elif n == 1:
                    R5.wait(pe, "k_kept", i, 4, back=1)
                else:
                    R5.wait(pe, "g", i, n - 1)
                for x in range(4):
                    k, part = (4 * n + x) // 2, x % 2
                    last = nc.tensor.transpose(tk_ps[n % 2][:, x * P:(x + 1) * P],
                                               gx[:, part, k, :, :, :].rearrange("p q g c -> p (q g c)"), ident[:, :])
                R5.up(last, "turn")
            R5.wait(pe, "hx", i, 4)
            R5.wait(pe, "g", i, 4)
            for q in range(4):
                for part in range(2):
                    last = nc.tensor.matmul(tk_ps[1][32 * q:32 * q + 32, 0:L5 * 32],
                                            gx[:, part, 0, q, :, :].rearrange("p g c -> p (g c)"),
                                            hx[:, s, part, 0:L5, q, :, :].rearrange("p k g c -> p k (g c)"),
                                            start=part == 0, stop=part == 1)
            R5.up(last, "k")

        def turn_act(act, i, s):
            R5.wait(act, "y", i, 1, back=2)
            R5.up(nc.scalar.copy(u_now[:, s, :, :], u_s5[:, bass.ds(i, 1), :].rearrange("p a (j n) -> p (a j) n", j=L5)), "u")
            R5.wait(act, "f", i, 1, back=1)
            for n in range(4):
                R5.wait(act, "turn", i, n + 1)
                R5.up(nc.scalar.copy(g_in[:, 2 * n:2 * n + 2, :, :].rearrange("p k r c -> p (k r c)"),
                                     tk_ps[n % 2][:, :]), "g")

        def k_dve(dve, i, s):
            R5.wait(dve, "k", i)
            R5.wait(dve, "fir", i, 1, back=1)
            for q in range(4):
                rows = slice(32 * q, 32 * q + 32)
                R5.up(nc.vector.tensor_copy(k_fir[rows, :, 32 * q:32 * q + 32],
                                            tk_ps[1][rows, 0:L5 * 32].rearrange("p (d c) -> p d c", d=L5)), "k_kept")
            R5.wait(dve, "k_kept", i, 4)
            R5.up(nc.vector.scalar_tensor_tensor(out=k_fir[:, 0, :], in0=ident[:, :], scalar=col_at("o_D", i),
                                                 in1=k_fir[:, 0, :], op0=ALU.mult, op1=ALU.add), "k_kept")

        def states_pe(pe, i, s):
            R5.wait(pe, "g", i, 4)
            R5.wait(pe, "u", i)
            R5.wait(pe, "rin", i, 6, back=1)
            for tau in range(L5):
                for part in range(2):
                    for q in range(4):
                        rows = slice(32 * q, 32 * q + 32)
                        last = nc.tensor.matmul(f_ps[:, q, 0, part * N5:(part + 1) * N5], g_in[rows, L5 - 1 - tau, part, :],
                                                u_now[rows, s, tau, :], start=tau == 0 and part == 0,
                                                stop=tau == L5 - 1, skip_group_check=True)
            R5.up(last, "f")
            R5.wait(pe, "k_kept", i, 5)
            R5.wait(pe, "out", i, 1, back=1)
            for j in range(L5):
                for tau in range(j + 1):
                    last = nc.tensor.matmul(y_ps[:, j, :], k_fir[:, j - tau, :], u_now[:, s, tau, :],
                                            start=tau == 0 and j % 4 == 0, stop=False, skip_group_check=True)
            R5.up(last, "fir")

        def output_pe(pe, i, s):
            R5.wait(pe, "rout", i, 6)
            for j in range(L5):
                for part in range(2):
                    for q in range(4):
                        last = nc.tensor.matmul(y_ps[32 * q:32 * q + 32, j, :],
                                                hx[:, s, part, j + 1, q, :, :].rearrange("p g c -> p (g c)"),
                                                s_prev[:, s, part, q, :], start=False, stop=part == 1,
                                                skip_group_check=True)
            R5.up(last, "y")

        def output_act(act, i, s):
            act.wait_ge(s5_clear, 5)
            R5.wait(act, "y", i)
            R5.up(nc.scalar.activation(u_s5[:, bass.ds(i, 1), :].rearrange("p a (n j) -> p (a j) n", j=L5),
                                       y_ps[:, :, :], ACT.Gelu_apprx_tanh), "out")

        def scan_dve(dve, i, s):
            c_i, s_i = (rot[:, k, bass.ds(i * 4, 4), :] for k in range(2))
            R5.up(nc.vector.tensor_tensor(keep8[:, :, :], first0[:, :, :],
                                          decay8[:, bass.ds(i * 4, 4)].unsqueeze(2).to_broadcast([P, 4, N5]), ALU.mult), "keep8")
            R5.wait(dve, "f", i)

            f_re, f_im = (f_ps[:, :, 0, part * N5:(part + 1) * N5] for part in range(2))
            x, y = f_hat[:, 0, :, :], f_hat[:, 1, :, :]
            xt, yt = r_tmp[:, 0, :, :], r_tmp[:, 1, :, :]
            R5.wait(dve, "rout", i, 6, back=1)
            for o, a, t in ((x, f_re, c_i), (y, f_im, c_i), (xt, f_im, s_i), (yt, f_re, s_i)):
                R5.up(nc.vector.tensor_tensor(o, a, t, ALU.mult), "rin")
            R5.wait(dve, "rin", i, 3)
            R5.up(nc.vector.tensor_tensor(x, x, xt, ALU.add), "rin")
            R5.wait(dve, "rin", i, 4)
            R5.up(nc.vector.tensor_tensor(y, y, yt, ALU.subtract), "rin")
            R5.wait(dve, "keep8", i)
            for part in range(2):
                R5.wait(dve, "rin", i, 5 + part)
                R5.up(nc.vector.tensor_tensor_scan(
                    s_hat[:, part, :, :].rearrange("p q n -> p (q n)"), keep8[:, :, :].rearrange("p q n -> p (q n)"),
                    f_hat[:, part, :, :].rearrange("p q n -> p (q n)"), 0.0, ALU.mult, ALU.add), "scan")
            R5.wait(dve, "scan", i, 2)
            R5.wait(dve, "y", i, 1, back=2)
            past = slice(0, N5 - 1)
            sx, sy = s_hat[:, 0, :, past], s_hat[:, 1, :, past]
            px, py = s_prev[:, s, 0, :, 1:N5], s_prev[:, s, 1, :, 1:N5]
            for o, a, t in ((px, sx, c_i), (py, sy, c_i), (xt[:, :, past], sy, s_i), (yt[:, :, past], sx, s_i)):
                R5.up(nc.vector.tensor_tensor(o, a, t[:, :, past], ALU.mult), "rout")
            R5.wait(dve, "rout", i, 4)
            R5.up(nc.vector.tensor_tensor(px, px, xt[:, :, past], ALU.subtract), "rout")
            R5.up(nc.vector.tensor_tensor(py, py, yt[:, :, past], ALU.add), "rout")

        def pipelined(eng, before, work, after):
            def step(i, s, more):
                if work:
                    work(eng, i, s)
                if more:
                    before(eng, i + 1, 1 - s)
                if after:
                    after(eng, i, s)
            before(eng, 0, 0)
            with eng.Fori(0, DT // 2 - 1) as n:
                for s in range(2):
                    step(n * 2 + s, s, True)
            step(DT - 2, 0, True)
            step(DT - 1, 1, False)

        with nc.Block() as block:
            @block.gpsimd
            def _(pool):
                R5.start(pool, "pool")
                pool.memset(gx[:, :, :, :, :, :], 0.0).then_inc(s5_clear, 1)
                pool.memset(hx[:, :, :, :, :, :, :], 0.0).then_inc(s5_clear, 1)
                pool.wait_ge(s5_clear, 5)
                with pool.Fori(0, DT // 2) as n:
                    for s in range(2):
                        make_pool(pool, n * 2 + s, s)

            @block.vector
            def _(dve):
                R5.start(dve, "dve")
                nc.vector.memset(k_fir[:, :, :], 0.0).then_inc(s5_clear, 1)
                nc.vector.memset(first0[:, :, :], 1.0).then_inc(s5_clear, 1)
                nc.vector.memset(s_prev[:, :, :, :, 0:1], 0.0).then_inc(s5_clear, 1)
                dve.wait_ge(s5_clear, 5)
                nc.vector.memset(first0[:, :, 0:1], 0.0).then_inc(s5_clear, 1)
                dve.wait_ge(s5_clear, 6)
                pipelined(dve, k_dve, scan_dve, None)

            @block.tensor
            def _(pe):
                R5.start(pe, "pe")
                pipelined(pe, turn_pe, states_pe, output_pe)

            @block.scalar
            def _(act):
                R5.start(act, "act")
                pipelined(act, turn_act, None, output_act)


    with ExitStack() as sc:
        y_hi = sb(sc, "yg_hi", [P, DT, SEQ], F32R)
        y_lo = sb(sc, "yg_lo", [P, DT, SEQ], F32R)
        sig = sb(sc, "glu_sig", [P, 2, SEQ])
        dn = Dense(sc, "g")
        w_glu = io["o_w_glu"].rearrange("a (k p) n -> (a p) k n", p=P)
        yg_hi_done, yg_lo_done, glu_sig, glu_mul, glu_out = (
            sem(n) for n in ("yg_hi_done", "yg_lo_done", "glu_sig_done", "glu_mul", "glu_out"))
        q0, u0 = Dense.q // 2, Dense.u
        with nc.Block() as block:
            def cols(i, half):
                return bass.ds((i + (1 - half) * DT) * P, P)

            @block.sync
            def _(sp):
                with sp.Fori(0, DT) as i:
                    for half in range(2):
                        dn.load(sp, w_glu, DT, cols(i, half), i * 2 + (q0 + half), 0)

            @block.gpsimd
            def _(pool):
                with pool.Fori(0, DT) as i:
                    for half in range(2):
                        dn.take_lo(pool, DT, i * 2 + (q0 + half), 0)

            @block.scalar
            def _(act):
                for k in range(DT):
                    nc.scalar.copy(y_hi[:, k, :], u_s5[:, k, :]).then_inc(yg_hi_done, 1)
                with act.Fori(0, DT) as i:
                    for half in range(2):
                        dn.take_hi(act, DT, i * 2 + (q0 + half), 0)
                    dn.wait_unit(act, i * 2 + q0, 1)
                    act.wait_ge(glu_out, i + 1)
                    nc.scalar.activation(sig[:, 0, :], dn.acc[0][:, :], ACT.Sigmoid).then_inc(unit_free, 1)

            @block.tensor
            def _(pe):
                pe.wait_ge(yg_lo_done, DT)
                with pe.Fori(0, DT) as i:
                    for half in range(2):
                        dn.product(pe, DT, y_hi, y_lo, i * 2 + (u0 + half), half, i * 2 + (q0 + half), 0)

            @block.vector
            def _(dve):
                for k in range(DT):
                    dve.wait_ge(yg_hi_done, k + 1)
                    nc.vector.tensor_tensor(y_lo[:, k, :], u_s5[:, k, :], y_hi[:, k, :].bitcast(F32),
                                            ALU.subtract).then_inc(yg_lo_done, 1)
                dve.sem_inc(glu_out, 1)
                with dve.Fori(0, DT) as i:
                    dn.wait_unit(dve, i * 2 + (q0 + 1), 1)
                    dve.wait_ge(unit_free, i * 2 + (u0 + 3))
                    nc.vector.tensor_tensor(sig[:, 1, :], sig[:, 0, :], dn.acc[1][:, :], ALU.mult).then_inc(unit_free, 1)
                    dve.wait_ge(unit_free, i * 2 + (u0 + 4))
                    here = x_res[:, bass.ds(i, 1), :]
                    nc.vector.tensor_tensor(here, here, sig[:, 1, :], ALU.add).then_inc(glu_out, 1)
        Dense.q += 4 * DT
        Dense.u += 2 * DT
    s5.close()

    conv_ffn(1)

    norm("out", "final_norm_g", 0, None, None)
    with ExitStack() as sc:
        chan = sb(sc, "chan", [P, 2, SEQ])
        rows = sb(sc, "out_rows", [P, 2, SEQ])
        turned = [ps(sc, f"out_ps{s}", [P, SEQ]) for s in range(2)]
        o_copied, o_turned, o_kept = sem("o_copied"), sem("o_turned"), sem("o_kept")
        o_stored = [sem("o_stored0"), sem("o_stored1")]
        out_v = out.rearrange("b (k t) c -> (b t) k c", t=P)
        with nc.Block() as block:
            @block.scalar
            def _(act):
                act.sem_inc(o_copied, 1)
                with act.Fori(0, DT // 2) as n:
                    for s in range(2):
                        act.wait_ge(o_turned, n * 2 + (s + 1))
                        nc.scalar.copy(chan[:, s, :], x_res[:, bass.ds(n * 2 + s, 1), :]).then_inc(o_copied, 1)

            @block.tensor
            def _(pe):
                pe.sem_inc(o_turned, 2)
                with pe.Fori(0, DT // 2) as n:
                    for s in range(2):
                        pe.wait_ge(o_copied, n * 2 + (s + 2))
                        pe.wait_ge(o_kept, n * 2 + (s + 1))
                        for k in range(SEQ // P):
                            last = nc.tensor.transpose(turned[s][:, k * P:(k + 1) * P], chan[:, s, k * P:(k + 1) * P], ident[:, :])
                        last.then_inc(o_turned, 1)

            @block.vector
            def _(dve):
                dve.sem_inc(o_kept, 2)
                with dve.Fori(0, DT // 2) as n:
                    for s in range(2):
                        dve.wait_ge(o_turned, n * 2 + (s + 3))
                        dve.wait_ge(o_stored[s], n * 16 + 16)
                        nc.vector.tensor_copy(rows[:, s, :], turned[s][:, :]).then_inc(o_kept, 1)

            @block.sync
            def _(sp):
                for s in range(2):
                    sp.sem_inc(o_stored[s], 16)
                with sp.Fori(0, DT // 2) as n:
                    for s in range(2):
                        sp.wait_ge(o_kept, n * 2 + (s + 3))
                        sp.dma_start(out_v[:, :, bass.ds(n * (2 * P) + s * P, P)],
                                     rows[:, s, :].rearrange("p (k c) -> p k c", c=P)).then_inc(o_stored[s], 16)
                for s in range(2):
                    sp.wait_ge(o_stored[s], 16 + 16 * (DT // 2))
    ctx.close()


INPUTS = ["x", "e_norm_g", "e_w_in", "e_mu", "e_w0", "e_w2", "e_a0", "e_a2", "e_g2", "e_k_k", "e_k_a", "e_r_k",
          "e_ln_w", "e_ln_b", "e_conv_w", "e_conv_b", "e_gate_a_w", "e_gate_a_b", "e_gate_x_w", "e_gate_x_b",
          "e_lru_lambda", "e_w_out", "o_norm_g", "o_w_in", "o_A_re", "o_A_im", "o_log_dt", "o_B_re", "o_B_im",
          "o_C_re", "o_C_im", "o_D", "o_w_glu", "f_norm_g", "f_w_up", "f_conv_w", "f_conv_b", "f_w_down",
          "final_norm_g"]


def kernel(**inputs):
    import numpy as np
    import concourse.bacc as bacc
    from concourse.bass_utils import run_bass_kernel_spmd

    nc = bacc.Bacc("TRN2", target_bir_lowering=False, num_devices=1)
    arrays = {f"in_{n}": np.ascontiguousarray(inputs[n]) for n in INPUTS}
    io = {n: nc.dram_tensor(f"in_{n}", arrays[f"in_{n}"].shape, F32, kind="ExternalInput").ap() for n in INPUTS}
    out = nc.dram_tensor("out_0", (1, SEQ, D_MODEL), F32, kind="ExternalOutput").ap()
    trunk(nc, io, out)
    result = run_bass_kernel_spmd(nc, [arrays], core_ids=[0])
    return result.results[0]["out_0"]
```

```python
from contextlib import ExitStack

import concourse.bass as bass
from concourse import mybir

F32 = mybir.dt.float32
F32R = mybir.dt.float32r
ALU = mybir.AluOpType
ACT = mybir.ActivationFunctionType

P = 128
D_MODEL = 1024
SEQ = 1024
HALF = 512
DT = D_MODEL // P
RW = 512
RT = RW // P
HEAD = 64
HEADS = RW // HEAD
D_FF = 2816
FT = D_FF // P
FGROUP = FT // 2
NORM_EPS = 1e-6
GN_EPS = 64e-5
LRU_C = 8.0
EXP_MINUS_HALF = 0.6065306597126334
CH = 128
NCH = SEQ // CH
L5 = 8
N5 = SEQ // L5
S5_PAIRS = 32

ROWS0 = [("e_mu", 14), ("e_w0", 4), ("e_a0", 4), ("e_k_k", 4), ("e_k_a", 4), ("e_r_k", 4),
         ("e_ln_w", 4), ("e_ln_b", 4), ("e_conv_w", 16), ("e_conv_b", 4), ("e_gate_a_b", 4),
         ("e_gate_x_b", 4), ("e_lru_lambda", 4), ("e_norm_g", 8), ("o_norm_g", 8),
         ("f_norm_g", 16), ("final_norm_g", 8), ("o_D", 8)]
COL = {}
_at = 0
for _name, _rows in ROWS0:
    COL[_name] = _at
    _at += _rows
ROWS0_USED = _at
COL["f_conv_w"] = P
COL["f_conv_b"] = P + 2 * 3 * 2 * FT
PCOLS = COL["f_conv_b"] + 2 * 2 * FT


def flat(ap):
    names = "abcdef"[:len(ap.shape)]
    return ap.rearrange(f"{' '.join(names)} -> ({' '.join(names)})")


def trunk(nc, io, out):
    ctx = ExitStack()
    sems = {}

    def sem(name):
        if name not in sems:
            sems[name] = ctx.enter_context(nc.semaphore(name))
        return sems[name]

    def sb(scope, name, shape, dt=F32):
        return scope.enter_context(nc.sbuf_tensor(name, shape, dt))

    def ps(scope, name, shape):
        return scope.enter_context(nc.psum_tensor(name, shape, F32))

    class Link:

        def __init__(self, eng, name):
            self.eng, self.sem, self.n, self.loop = eng, sem(name), totals.get(name, 0), 0
            self.name = name

        def did(self, ins):
            ins.then_inc(self.sem, 1)
            self.n += 1

        def wait(self):
            self.eng.wait_ge(self.sem, self.loop + self.n)

        def run(self, ins):
            self.did(ins)
            self.wait()

        def enter(self, i, per):
            self.loop, self.start, self.per = i * per, self.n, per

        def leave(self, times):
            assert self.n - self.start == self.per, (self.name, self.n - self.start)
            self.loop, self.n = 0, self.start + self.per * times

        def close(self):
            totals[self.name] = self.n

    totals = {}

    class Rounds:

        def __init__(self, tag, raises):
            self.tag, self.raises = tag, raises
            self.per = {n: k for own in raises.values() for n, k in own.items()}

        def start(self, eng, own):
            for n, k in self.raises[own].items():
                eng.sem_inc(sem(f"{self.tag}_{n}"), 2 * k)

        def wait(self, eng, name, i, k=1, back=0):
            eng.wait_ge(sem(f"{self.tag}_{name}"), i * self.per[name] + ((2 - back) * self.per[name] + k))

        def up(self, ins, name):
            ins.then_inc(sem(f"{self.tag}_{name}"), 1)

    x_res = sb(ctx, "x_res", [P, DT, SEQ])
    prm = sb(ctx, "prm", [P, 4 * P])
    ident = sb(ctx, "ident", [P, P])

    def col(name, k=0):
        return prm[:, COL[name] + k:COL[name] + k + 1]

    def col_at(name, k):
        return prm[:, bass.ds(k + COL[name], 1)]

    with ExitStack() as sc:
        rows = sb(sc, "param_rows", [P, 4, P])
        stage = sb(sc, "x_stage", [P, 2, D_MODEL])
        turned = [ps(sc, f"turned{s}", [P, 2 * HALF]) for s in range(2)]
        turned_prm = ps(sc, "turned_prm", [P, 4, P])
        x_loaded = [sem("x_loaded0"), sem("x_loaded1")]
        prm_loaded, rows_clear, ident_ready = sem("prm_loaded"), sem("rows_clear"), sem("ident_ready")
        x_turned, x_kept, prm_turned = sem("x_turned"), sem("x_kept"), sem("prm_turned")
        n_prm = len(ROWS0) + 4
        x_rows = io["x"].rearrange("b (n t) d -> (b n) t d", t=P)
        with nc.Block() as block:
            @block.sync
            def _(sp):
                for s in range(2):
                    sp.dma_start(stage[:, s, :], x_rows[s, :, :]).then_inc(x_loaded[s], 16)
                with sp.Fori(1, SEQ // P // 2) as i:
                    for s in range(2):
                        sp.wait_ge(x_turned, i * 2 + s - 1)
                        sp.dma_start(stage[:, s, :], x_rows[bass.ds(i * 2 + s, 1), :, :]).then_inc(x_loaded[s], 16)

            @block.gpsimd
            def _(pool):
                pool.memset(ident[:, :], 0.0).then_inc(ident_ready, 1)
                pool.memset(rows[:, 0, :], 0.0).then_inc(rows_clear, 1)
                pool.memset(rows[:, 3, :], 0.0).then_inc(rows_clear, 1)
                pool.wait_ge(ident_ready, 1)
                pool.affine_select(out=ident[:, :], in_=ident[:, :], compare_op=ALU.not_equal, fill=1.0,
                                   base=0, pattern=[[-1, P]], channel_multiplier=1).then_inc(ident_ready, 1)

            @block.scalar
            def _(act):
                act.wait_ge(rows_clear, 2)
                for name, n in ROWS0:
                    act.dma_start(rows[COL[name]:COL[name] + n, 0, :],
                                  flat(io[name]).rearrange("(r p) -> r p", p=P)).then_inc(prm_loaded, 16)
                taps = flat(io["f_conv_w"]).rearrange("(r p) -> r p", p=P)
                for k in range(3):
                    n = min(P, taps.shape[0] - k * P)
                    act.dma_start(rows[0:n, 1 + k, :], taps[k * P:k * P + n, :]).then_inc(prm_loaded, 16)
                bias = flat(io["f_conv_b"]).rearrange("(r p) -> r p", p=P)
                at = COL["f_conv_b"] - 3 * P
                act.dma_start(rows[at:at + bias.shape[0], 3, :], bias).then_inc(prm_loaded, 16)
                act.wait_ge(prm_turned, 1)
                act.copy(prm[:, :], turned_prm[:, :, :]).then_inc(sem("prm_ready"), 1)

            @block.tensor
            def _(pe):
                pe.wait_ge(ident_ready, 2)
                with pe.Fori(0, SEQ // P // 2) as i:
                    for s in range(2):
                        pe.wait_ge(x_loaded[s], i * 16 + 16)
                        pe.wait_ge(x_kept, i * 2 + s + 1)
                        for c in range(DT):
                            last = nc.tensor.transpose(turned[s][:, c * P:(c + 1) * P],
                                                       stage[:, s, c * P:(c + 1) * P], ident[:, :])
                        last.then_inc(x_turned, 1)
                pe.wait_ge(prm_loaded, 16 * n_prm)
                for k in range(4):
                    last = nc.tensor.transpose(turned_prm[:, k, :], rows[:, k, :], ident[:, :])
                last.then_inc(prm_turned, 1)

            @block.vector
            def _(dve):
                dve.sem_inc(x_kept, 2)
                with dve.Fori(0, SEQ // P // 2) as i:
                    for s in range(2):
                        dve.wait_ge(x_turned, i * 2 + s + 1)
                        nc.vector.tensor_copy(x_res[:, :, bass.ds(i * (2 * P) + s * P, P)],
                                              turned[s][:, :].rearrange("p (c t) -> p c t", c=DT)).then_inc(x_kept, 1)

    def norm(tag, g_name, g_at, xn_hi, xn_lo):
        with ExitStack() as sc:
            sq = sb(sc, f"sq_{tag}", [P, 2, SEQ])
            rstd = sb(sc, f"rstd_{tag}", [P, SEQ])
            xn = sb(sc, f"xn_{tag}", [P, 2, SEQ])
            ones = sb(sc, f"ones_{tag}", [P, P])
            eps = sb(sc, f"eps_{tag}", [P, 1])
            total = ps(sc, f"total_{tag}", [P, SEQ])
            squared, summed, root, consts, inv, scaled, hi_done, lo_done = (
                sem("n_" + n) for n in ("squared", "summed", "root", "consts", "inv", "scaled", "hi", "lo"))
            before = totals.get("norms", 0)
            totals["norms"] = before + 1
            tiles = before * DT
            with nc.Block() as block:
                @block.scalar
                def _(act):
                    for c in range(DT):
                        if c >= 2:
                            act.wait_ge(summed, tiles + c - 1)
                        nc.scalar.activation(sq[:, c % 2, :], x_res[:, c, :], ACT.Square).then_inc(squared, 1)
                    act.wait_ge(summed, tiles + DT)
                    act.wait_ge(consts, 2 * before + 2)
                    nc.scalar.activation(rstd[:, :], total[:, :], ACT.Sqrt, scale=1.0 / D_MODEL, bias=eps[:, 0:1]).then_inc(root, 1)
                    for c in range(DT) if xn_hi else ():
                        act.wait_ge(scaled, tiles + c + 1)
                        nc.scalar.copy(xn_hi[:, c, :], xn[:, c % 2, :]).then_inc(hi_done, 1)

                @block.tensor
                def _(pe):
                    pe.wait_ge(consts, 2 * before + 2)
                    for c in range(DT):
                        pe.wait_ge(squared, tiles + c + 1)
                        for h in range(2):
                            last = nc.tensor.matmul(total[:, h * HALF:(h + 1) * HALF], ones[:, :],
                                                    sq[:, c % 2, h * HALF:(h + 1) * HALF],
                                                    start=c == 0, stop=c == DT - 1)
                        last.then_inc(summed, 1)

                @block.vector
                def _(dve):
                    nc.vector.memset(ones[:, :], 1.0).then_inc(consts, 1)
                    nc.vector.memset(eps[:, :], NORM_EPS).then_inc(consts, 1)
                    dve.wait_ge(root, before + 1)
                    nc.vector.reciprocal(rstd[:, :], rstd[:, :]).then_inc(inv, 1)
                    dve.wait_ge(inv, before + 1)
                    for c in range(DT):
                        if c >= 2 and xn_hi:
                            dve.wait_ge(lo_done, tiles + c - 1)
                        nc.vector.scalar_tensor_tensor(out=xn[:, c % 2, :] if xn_hi else x_res[:, c, :], in0=x_res[:, c, :],
                                                       scalar=col(g_name, g_at + c), in1=rstd[:, :],
                                                       op0=ALU.mult, op1=ALU.mult).then_inc(scaled, 1)

                @block.gpsimd
                def _(pool):
                    for c in range(DT) if xn_hi else ():
                        pool.wait_ge(hi_done, tiles + c + 1)
                        pool.tensor_tensor(xn_lo[:, c, :], xn[:, c % 2, :], xn_hi[:, c, :].bitcast(F32),
                                           op=ALU.subtract).then_inc(lo_done, 1)

    w_loaded = [sem("w_loaded0"), sem("w_loaded1")]
    w_hi_done, w_lo_done, w_used = sem("w_hi_done"), sem("w_lo_done"), sem("w_used")
    unit_free = sem("unit_free")
    KC = 4

    class Dense:

        q = 0
        u = 0

        def __init__(self, sc, tag):
            self.raw = sb(sc, f"w_raw_{tag}", [P, 2, KC, P])
            self.hi = sb(sc, f"w_hi_{tag}", [P, 2, KC, P], F32R)
            self.lo = sb(sc, f"w_lo_{tag}", [P, 2, KC, P], F32R)
            self.acc = [ps(sc, f"acc{s}_{tag}", [P, SEQ]) for s in range(2)]

        @staticmethod
        def chunks(kt):
            return [(k, min(KC, kt - k)) for k in range(0, kt, KC)]

        def load(self, sp, w, kt, n0, pair, par):
            for k, n in self.chunks(kt):
                sp.wait_ge(w_lo_done, pair * 2 + (par + 1))
                sp.dma_start(self.raw[:, par, 0:n, :], w[:, k:k + n, n0]).then_inc(w_loaded[par], 16)
                pair, par = (pair + 1, 0) if par else (pair, 1)

        def take_hi(self, act, kt, pair, par):
            for k, n in self.chunks(kt):
                act.wait_ge(w_loaded[par], pair * 16 + 16)
                act.wait_ge(w_used, pair * 2 + (par + 1))
                nc.scalar.copy(self.hi[:, par, 0:n, :], self.raw[:, par, 0:n, :]).then_inc(w_hi_done, 1)
                pair, par = (pair + 1, 0) if par else (pair, 1)

        def take_lo(self, pool, kt, pair, par):
            for k, n in self.chunks(kt):
                pool.wait_ge(w_hi_done, pair * 2 + (par + 1))
                pool.tensor_tensor(self.lo[:, par, 0:n, :], self.raw[:, par, 0:n, :],
                                   self.hi[:, par, 0:n, :].bitcast(F32), op=ALU.subtract).then_inc(w_lo_done, 1)
                pair, par = (pair + 1, 0) if par else (pair, 1)

        @staticmethod
        def wait_unit(eng, pair, par):
            eng.wait_ge(w_used, pair * 2 + (par + 3))

        def product(self, pe, kt, in_hi, in_lo, unit, slot, pair, par):
            pe.wait_ge(unit_free, unit + 1)
            acc = self.acc[slot]
            for k, n in self.chunks(kt):
                pe.wait_ge(w_lo_done, pair * 2 + (par + 3))
                for j in range(n):
                    for w, x in ((self.hi, in_hi), (self.hi, in_lo), (self.lo, in_hi)):
                        first = k + j == 0 and w is self.hi and x is in_hi
                        final = k + j == kt - 1 and w is self.lo
                        for h in range(2):
                            last = nc.tensor.matmul(acc[:, h * HALF:(h + 1) * HALF], w[:, par, j, :],
                                                    x[:, k + j, h * HALF:(h + 1) * HALF], start=first, stop=final)
                last.then_inc(w_used, 1)
                pair, par = (pair + 1, 0) if par else (pair, 1)

    def dense_credit_pool(pool):
        pool.sem_inc(w_lo_done, 2)

    def dense_credit_pe(pe):
        pe.sem_inc(w_used, 2)

    def dense_credit_dve(dve):
        dve.sem_inc(unit_free, 2)


    proj = ctx.enter_context(ExitStack())
    EV = 22
    p_even = sb(proj, "p_even", [P, EV, SEQ])
    w_in = io["e_w_in"].rearrange("a (k p) n -> (a p) k n", p=P)
    with ExitStack() as sc:
        xn_hi = sb(sc, "xn_hi_e", [P, DT, SEQ], F32R)
        xn_lo = sb(sc, "xn_lo_e", [P, DT, SEQ], F32R)
        norm("e", "e_norm_g", 0, xn_hi, xn_lo)
        dn = Dense(sc, "e")
        start_scale = sb(sc, "start_scale", [P, EV])
        start_bias = sb(sc, "start_bias", [P, EV])
        tables, started, spent = sem("e_tables"), sem("e_started"), sem("e_spent")
        with nc.Block() as block:
            @block.sync
            def _(sp):
                with sp.Fori(0, EV // 2) as i:
                    for s in range(2):
                        dn.load(sp, w_in, DT, bass.ds(i * (2 * P) + s * P, P), i * 2 + s, 0)

            @block.gpsimd
            def _(pool):
                dense_credit_pool(pool)
                with pool.Fori(0, EV // 2) as i:
                    for s in range(2):
                        dn.take_lo(pool, DT, i * 2 + s, 0)

            @block.tensor
            def _(pe):
                dense_credit_pe(pe)
                with pe.Fori(0, EV // 2) as i:
                    for s in range(2):
                        dn.product(pe, DT, xn_hi, xn_lo, i * 2 + s, s, i * 2 + s, 0)

            @block.scalar
            def _(act):
                def start_unit(u, slot):
                    act.wait_ge(w_used, u * 2 + 4)
                    nc.scalar.activation(p_even[:, bass.ds(u, 1), :], dn.acc[slot][:, :], ACT.Identity,
                                         scale=start_scale[:, bass.ds(u, 1)],
                                         bias=start_bias[:, bass.ds(u, 1)]).then_inc(started, 1)

                act.wait_ge(tables, 6)
                dn.take_hi(act, DT, 0, 0)
                dn.take_hi(act, DT, 1, 0)
                start_unit(0, 0)
                with act.Fori(1, EV // 2) as i:
                    for s in range(2):
                        dn.take_hi(act, DT, i * 2 + s, 0)
                        start_unit(i * 2 + (s - 1), 1 - s)
                start_unit(EV - 1, 1)

            @block.vector
            def _(dve):
                dense_credit_dve(dve)
                nc.vector.tensor_scalar(start_scale[:, 0:14], prm[:, COL["e_mu"]:COL["e_mu"] + 14],
                                        -1.0, 1.0, ALU.mult, ALU.add).then_inc(tables, 1)
                nc.vector.tensor_copy(start_scale[:, 14:18],
                                      prm[:, COL["e_conv_w"] + 12:COL["e_conv_w"] + 16]).then_inc(tables, 1)
                nc.vector.memset(start_scale[:, 18:22], 1.0).then_inc(tables, 1)
                nc.vector.memset(start_bias[:, 0:14], 0.0).then_inc(tables, 1)
                nc.vector.tensor_copy(start_bias[:, 14:18],
                                      prm[:, COL["e_conv_b"]:COL["e_conv_b"] + 4]).then_inc(tables, 1)
                nc.vector.memset(start_bias[:, 18:22], 0.0).then_inc(tables, 1)

                def tap(u, slot, scale, back):
                    here = p_even[:, bass.ds(u, 1), back:SEQ]
                    return nc.vector.scalar_tensor_tensor(out=here, in0=dn.acc[slot][:, 0:SEQ - back],
                                                          scalar=scale, in1=here, op0=ALU.mult, op1=ALU.add)

                with dve.Fori(0, 7) as i:
                    for s in range(2):
                        dve.wait_ge(started, i * 2 + s + 1)
                        tap(i * 2 + s, s, col_at("e_mu", i * 2 + s), 1).then_inc(unit_free, 1)
                with dve.Fori(0, 2) as i:
                    for s in range(2):
                        dve.wait_ge(started, i * 2 + (s + 15))
                        for back in (1, 2, 3):
                            ins = tap(i * 2 + (s + 14), s, col_at("e_conv_w", i * 2 + (s + 4 * (3 - back))), back)
                            if back < 3:
                                ins.then_inc(spent, 1)
                                dve.wait_ge(spent, i * 4 + (2 * s + back))
                        ins.then_inc(unit_free, 1)
                dve.wait_ge(unit_free, 2 + 18)
                with dve.Fori(18, EV) as i:
                    dve.wait_ge(started, i + 1)
                    dve.sem_inc(unit_free, 1)

    LEVELS = 7
    level_mask = sb(proj, "level_mask", [P, LEVELS, P])
    causal = sb(proj, "causal", [P, 2, P])
    head_ones = sb(proj, "head_ones", [P, P])
    centre = sb(proj, "centre", [P, P])
    scratch_w = p_even[:, 18:22, :]

    with ExitStack() as sc:
        gw = sb(sc, "gw", [P, 2, 4, P])
        same_block = sb(sc, "same_block", [P, LEVELS + 1, P])
        decay_c = sb(sc, "decay_c", [P, 4])
        lam_abs = sb(sc, "lam_abs", [P, 4])
        z = sb(sc, "lam_z", [P, 4])
        z2 = sb(sc, "lam_z2", [P, 4])
        den = sb(sc, "lam_den", [P, 4])
        poly = sb(sc, "lam_poly", [P, 4])
        g_r = sb(sc, "g_r", [P, 2, SEQ])
        g_i = sb(sc, "g_i", [P, 2, SEQ])
        a_t = sb(sc, "a_t", [P, 2, SEQ])
        th = sb(sc, "th", [P, 2, SEQ])
        g_psum = [ps(sc, f"g_psum{k}", [P, SEQ]) for k in range(4)]
        gw_clear, gw_loaded, lam_exp, decay_ready = sem("gw_clear"), sem("gw_loaded"), sem("lam_exp"), sem("decay_ready")
        lam_ready = sem("lam_ready")
        l_gates, l_sig, l_tanh, l_exp, l_arg, l_root, l_gelu, l_out = (
            sem("l_" + n) for n in ("gates", "sig", "tanh", "exp", "arg", "root", "gelu", "out"))
        masks_pool, masks_dve, l_gated, l_h, l_sq = sem("masks_pool"), sem("masks_dve"), sem("l_gated"), sem("l_h"), sem("l_sq")
        with nc.Block() as block:
            @block.gpsimd
            def _(pool):
                link = Link(pool, "masks_pool")
                link.run(pool.memset(same_block[:, :, :], 1.0))
                for k in range(LEVELS):
                    m = same_block[:, k, :].rearrange("p (b c) -> p b c", c=1 << k)
                    link.run(pool.affine_select(out=m, in_=m, compare_op=ALU.is_ge, fill=0.0, base=0,
                                                pattern=[[-(1 << k), P >> k], [0, 1 << k]], channel_multiplier=1))
                    link.run(pool.affine_select(out=m, in_=m, compare_op=ALU.is_ge, fill=0.0, base=(1 << k) - 1,
                                                pattern=[[1 << k, P >> k], [0, 1 << k]], channel_multiplier=-1))
                link.run(pool.memset(causal[:, :, :], 1.0))
                for k in range(2):
                    link.run(pool.affine_select(out=causal[:, k, :], in_=causal[:, k, :], compare_op=ALU.is_ge, fill=0.0,
                                                base=k - 1, pattern=[[1, P]], channel_multiplier=-1))
                link.close()

            @block.sync
            def _(sp):
                sp.wait_ge(gw_clear, 1)
                for g, name in enumerate(("e_gate_a_w", "e_gate_x_w")):
                    w = io[name].rearrange("a (c h) i j -> (a h) i c j", h=2)
                    for h in range(2):
                        sp.dma_start(gw[h * HEAD:(h + 1) * HEAD, g, :, h * HEAD:(h + 1) * HEAD],
                                     w[h, :, :, :]).then_inc(gw_loaded, 16)

            @block.tensor
            def _(pe):
                pe.wait_ge(gw_loaded, 64)
                for c in range(4):
                    if c >= 2:
                        pe.wait_ge(l_sig, 2 * (c - 1))
                    for g in range(2):
                        for h in range(2):
                            last = nc.tensor.matmul(g_psum[2 * (c % 2) + g][:, h * HALF:(h + 1) * HALF], gw[:, g, c, :],
                                                    p_even[:, 14 + c, h * HALF:(h + 1) * HALF], start=True, stop=True)
                    last.then_inc(l_gates, 1)

            @block.scalar
            def _(act):
                act.wait_ge(lam_ready, 1)
                nc.scalar.activation(lam_abs[:, :], lam_abs[:, :], ACT.Exp, scale=-1.0).then_inc(lam_exp, 1)
                act.wait_ge(decay_ready, 1)
                for c in range(4):
                    s = c % 2
                    act.wait_ge(l_gates, c + 1)
                    if c >= 2:
                        act.wait_ge(l_out, c - 1)
                    nc.scalar.activation(g_r[:, s, :], g_psum[2 * s][:, :], ACT.Sigmoid,
                                         bias=col("e_gate_a_b", c)).then_inc(l_sig, 1)
                    nc.scalar.activation(g_i[:, s, :], g_psum[2 * s + 1][:, :], ACT.Sigmoid,
                                         bias=col("e_gate_x_b", c)).then_inc(l_sig, 1)
                    act.wait_ge(l_sig, 2 * c + 1)
                    nc.scalar.activation(th[:, s, :], g_r[:, s, :], ACT.Tanh, scale=decay_c[:, c:c + 1]).then_inc(l_tanh, 1)
                    act.wait_ge(l_arg, 4 * c + 1)
                    nc.scalar.activation(a_t[:, s, :], a_t[:, s, :], ACT.Exp).then_inc(l_exp, 1)
                    act.wait_ge(l_arg, 4 * c + 3)
                    nc.scalar.activation(th[:, s, :], th[:, s, :], ACT.Sqrt).then_inc(l_root, 1)
                    nc.scalar.activation(p_even[:, 18 + c, :], p_even[:, 18 + c, :], ACT.Gelu_apprx_tanh).then_inc(l_gelu, 1)

            @block.vector
            def _(dve):
                nc.vector.memset(gw[:, :, :, :], 0.0).then_inc(gw_clear, 1)
                lam = prm[:, COL["e_lru_lambda"]:COL["e_lru_lambda"] + 4]
                nc.vector.scalar_tensor_tensor(out=lam_abs[:, :], in0=lam, scalar=-1.0, in1=lam, op0=ALU.mult,
                                               op1=ALU.max).then_inc(lam_ready, 1)
                dve.wait_ge(lam_exp, 1)
                link = Link(dve, "masks_dve")
                link.run(nc.vector.tensor_scalar(den[:, :], lam_abs[:, :], 2.0, None, ALU.add))
                link.run(nc.vector.reciprocal(den[:, :], den[:, :]))
                link.run(nc.vector.tensor_tensor(z[:, :], lam_abs[:, :], den[:, :], ALU.mult))
                link.run(nc.vector.tensor_tensor(z2[:, :], z[:, :], z[:, :], ALU.mult))
                link.run(nc.vector.memset(poly[:, :], 1.0 / 17))
                for k in range(15, 0, -2):
                    link.run(nc.vector.tensor_tensor(poly[:, :], poly[:, :], z2[:, :], ALU.mult))
                    link.run(nc.vector.tensor_scalar(poly[:, :], poly[:, :], 1.0 / k, None, ALU.add))
                link.run(nc.vector.tensor_tensor(poly[:, :], poly[:, :], z[:, :], ALU.mult))
                link.run(nc.vector.tensor_scalar(poly[:, :], poly[:, :], 2 * LRU_C, None, ALU.mult))
                link.run(nc.vector.tensor_scalar(den[:, :], lam, -LRU_C, 0.0, ALU.mult, ALU.max))
                nc.vector.tensor_tensor(decay_c[:, :], poly[:, :], den[:, :], ALU.add).then_inc(decay_ready, 1)
                dve.wait_ge(decay_ready, 1)
                for c in range(4):
                    s = c % 2
                    dve.wait_ge(l_sig, 2 * c + 2)
                    nc.vector.tensor_scalar(a_t[:, s, :], g_r[:, s, :], decay_c[:, c:c + 1], -1.0,
                                            ALU.mult, ALU.mult).then_inc(l_arg, 1)
                    nc.vector.tensor_tensor(g_i[:, s, :], g_i[:, s, :], p_even[:, 14 + c, :], ALU.mult).then_inc(l_gated, 1)
                    dve.wait_ge(l_exp, c + 1)
                    nc.vector.tensor_tensor(g_r[:, s, :], a_t[:, s, :], a_t[:, s, :], ALU.mult).then_inc(l_arg, 1)
                    dve.wait_ge(l_arg, 4 * c + 2)
                    dve.wait_ge(l_tanh, c + 1)
                    nc.vector.scalar_tensor_tensor(out=th[:, s, :], in0=g_r[:, s, :], scalar=1.0, in1=th[:, s, :],
                                                   op0=ALU.add, op1=ALU.mult).then_inc(l_arg, 1)
                    dve.wait_ge(l_gated, c + 1)
                    dve.wait_ge(l_root, c + 1)
                    nc.vector.tensor_tensor(g_i[:, s, :], g_i[:, s, :], th[:, s, :], ALU.mult).then_inc(l_arg, 1)
                    dve.wait_ge(l_arg, 4 * c + 4)
                    nc.vector.tensor_tensor_scan(g_r[:, s, :], a_t[:, s, :], g_i[:, s, :], 0.0, ALU.mult, ALU.add).then_inc(l_h, 1)
                    dve.wait_ge(l_h, c + 1)
                    dve.wait_ge(l_gelu, c + 1)
                    nc.vector.tensor_tensor(p_even[:, 14 + c, :], g_r[:, s, :], p_even[:, 18 + c, :], ALU.mult).then_inc(l_out, 1)
                dve.wait_ge(masks_pool, 1 + 2 * LEVELS + 3)
                link.run(nc.vector.tensor_copy(head_ones[:, :], same_block[:, 6, :]))
                for k in range(LEVELS):
                    link.run(nc.vector.tensor_tensor(level_mask[:, k, :], same_block[:, k + 1, :], same_block[:, k, :], ALU.subtract))
                below = same_block[:, 0, :]
                link.run(nc.vector.tensor_scalar(below, causal[:, 1, :], -1.0, 1.0, ALU.mult, ALU.add))
                for k in range(LEVELS):
                    link.run(nc.vector.tensor_tensor(level_mask[:, k, :], level_mask[:, k, :],
                                                     below if k else causal[:, 0, :], ALU.mult))
                link.run(nc.vector.scalar_tensor_tensor(out=centre[:, :], in0=head_ones[:, :], scalar=-1.0 / HEAD,
                                                        in1=ident[:, :], op0=ALU.mult, op1=ALU.add))
                link.close()

    with ExitStack() as sc:
        lora_w = sb(sc, "lora_w", [P, RW])
        lora_g = sb(sc, "lora_g", [P, RW])
        ones = sb(sc, "r_ones", [P, CH])
        lora_x = sb(sc, "lora_x", [P, CH])
        sig_g = sb(sc, "sig_g", [P, CH])
        names = ("decay", "logsum", "grow", "a", "kk", "ksq", "k2", "rk")
        flat_temps = p_even[:, 18:22, :].rearrange("p c t -> p (c t)")
        T = {n: flat_temps[:, HALF * k:HALF * (k + 1)].rearrange("p (i t) -> p i t", i=RT)
             for k, n in enumerate(names)}
        y_sq = T["ksq"]
        v_now = sb(sc, "v_now", [P, RT, CH])
        mid = sb(sc, "mid", [P, RT])
        norms = sb(sc, "norms", [HEADS, 2, CH])
        unscale = sb(sc, "unscale", [P, 1])
        zr = sb(sc, "zr", [P, 2, RT, 2, CH])
        k_t = sb(sc, "k_t", [P, 2, RT, CH])
        b_t = sb(sc, "b_t", [P, 2, RT, CH])
        mid_scale = sb(sc, "mid_scale", [P, 2, RT])
        end_scale = sb(sc, "end_scale", [P, 2, RT])
        by_token = sb(sc, "by_token", [P, 4, RW])
        a_b = [sb(sc, f"a_b{g}", [P, RT, 2, CH]) for g in range(2)]
        a_k = [sb(sc, f"a_k{g}", [P, RT, 2, CH]) for g in range(2)]
        a_zb = [sb(sc, f"a_zb{g}", [P, RT, CH], F32R) for g in range(2)]
        rounded = sb(sc, "rounded", [P, 6 * RT + 3, CH], F32R)
        EYE = 6 * RT + 1
        x_inv, x_inv_t, mx = ([rounded[:, 1 + (2 * k + g) * RT:1 + (2 * k + g + 1) * RT, :] for g in range(2)]
                              for k in range(3))
        eye = rounded[:, EYE, :]
        x_t = [sb(sc, f"x_t{g}", [P, RT, CH]) for g in range(2)]
        neg_eye = sb(sc, "neg_eye", [P, P], F32R)
        akv = sb(sc, "akv", [P, RW])
        sa = akv
        y_c = sb(sc, "y_c", [P, RT, CH])
        w_t = y_c
        head_in = sb(sc, "head_in", [P, RT, HEADS])
        head_out = sb(sc, "head_out", [HEADS, RT, P])
        state = sb(sc, "state", [P, RT, HEAD])
        state_mid = sb(sc, "state_mid", [P, RT, HEAD])
        prep_ps = [ps(sc, f"prep_ps{k}", [P, HALF]) for k in range(2)]
        m = [ps(sc, f"main_ps{k}", [P, SEQ]) for k in range(3)]
        banks = [(m[0][:, 0:HALF], m[0][:, HALF:SEQ], m[1][:, 0:HALF]),
                 (m[1][:, HALF:SEQ], m[2][:, 0:HALF], m[2][:, HALF:SEQ])]
        SUM_SCALE = 65536.0

        R7 = Rounds("r", {
            "act": {"lora_in": 3, "sigmoid": 2, "ksq": 1, "roots": 2, "g_kept": 1, "exps": 4, "turned_kept": 4,
                    "a_zb": 2, "x0": 7, "xt0": 6, "res0": 1, "akv": 1, "w_t": 1, "sa": 2, "y": 1, "y_sq": 2},
            "pe": {"lora": 3, "k_sum": 1, "k_wide": 1, "bonus_sum": 1, "turned": 4, "a_ps": 4, "mx_ps0": 6, "mx_ps1": 6,
                   "x_ps0": 13, "x_ps1": 13, "res_ps0": 2, "res_ps1": 2, "akv_ps": 1, "w_ps": 1, "sa_ps": 2, "s_ps": 1,
                   "y_ps": 1, "yc_ps": 1, "y_sum": 1, "y_wide": 1},
            "dve": {"biased": 2, "logsum": 4, "mids": 1, "k2": 2, "k_floor": 1, "y_floor": 1, "kk": 1, "zr": 2,
                    "ends": 1, "bonus": 1, "a_kept": 4, "first": 2, "mx0": 6, "mx1": 6, "x1": 7, "xt1": 6, "res1": 1,
                    "x_t0": 1, "x_t1": 1, "state_mid": 1, "state": 2, "gn": 1},
            "pool": {"v_now": 1, "kk_raw": 1, "centred": 2, "rk": 2, "bk": 3, "first_t": 2, "out": 4},
        })
        last_chunk = NCH - 1
        start, wait, up = R7.start, R7.wait, R7.up

        def per_channel(name):
            return prm[:, COL[name]:COL[name] + RT].unsqueeze(2).to_broadcast([P, RT, CH])

        def over_tokens(ap, n=CH):
            return ap.unsqueeze(2).to_broadcast([P, RT, n])

        def tokens(first, n, c):
            return p_even[:, first:first + n, bass.ds(c * CH, CH)]

        def tt(out_, a, b, op):
            return nc.vector.tensor_tensor(out_, a, b, op)

        def psum4(ap):
            return ap.rearrange("p (i t) -> p i t", i=RT)

        def product4(bank, lhs, rhs, begin=True, end=True):
            for i in range(RT):
                last = nc.tensor.matmul(bank[:, i * CH:(i + 1) * CH], lhs(i), rhs(i), start=begin, stop=end,
                                        skip_group_check=not (begin and end))
            return last

        def lora_pe(pe, c, k):
            if k == 0:
                wait(pe, "lora_in", c, 3)
                wait(pe, "turned_kept", c, 4, back=1)
            if k == 1:
                wait(pe, "turned_kept", c, 3, back=1)
            if k == 2:
                wait(pe, "biased", c, 1)
            w, x = ((lora_w[0:HEAD, :], lora_x[0:HEAD, :]), (lora_w[HEAD:P, :], lora_x[HEAD:P, :]),
                    (lora_g[:, :], sig_g[:, :]))[k]
            up(product4(prep_ps[k % 2], lambda i: w[:, i * P:(i + 1) * P], lambda i: x), "lora")

        def head_sums(bank, sq):
            for i in range(RT):
                last = nc.tensor.matmul(bank[0:HEADS, 0:CH], head_in[:, i, :], sq[:, i, :], start=i == 0, stop=i == RT - 1)
            return last

        def widen(bank, by_head):
            return product4(bank, lambda i: head_out[:, i, :], lambda i: by_head[:, :])

        def k_sum_pe(pe, c):
            wait(pe, "ksq", c)
            wait(pe, "biased", c, 2)
            up(head_sums(prep_ps[1], T["ksq"]), "k_sum")

        def bonus_pe(pe, c):
            wait(pe, "rk", c, 2)
            wait(pe, "g_kept", c)
            up(nc.tensor.matmul(prep_ps[0][:, :], head_ones[:, :], T["rk"], start=True, stop=True), "bonus_sum")

        def k_wide_pe(pe, c):
            wait(pe, "roots", c, 2)
            wait(pe, "gn", c, back=2)
            up(widen(prep_ps[1], norms[:, 0, :]), "k_wide")

        def centre_pe(pe, c):
            wait(pe, "y", c)
            if isinstance(c, int) and c == last_chunk:
                wait(pe, "gn", c, back=1)
            elif isinstance(c, int) and c == last_chunk - 1:
                wait(pe, "turned_kept", c + 1, 3)
            else:
                wait(pe, "k_floor", c + 2)
            up(nc.tensor.matmul(prep_ps[1][:, :], centre[:, :], y_c[:, :, :], start=True, stop=True), "yc_ps")

        def y_sum_pe(pe, c):
            wait(pe, "y_sq", c, 2)
            up(head_sums(prep_ps[1], y_sq[:, :, :]), "y_sum")

        def y_wide_pe(pe, c):
            wait(pe, "roots", c + 2, 2)
            up(widen(prep_ps[1], norms[:, 1, :]), "y_wide")

        def turn_pe(pe, c, s, n):
            src = (zr[:, s, :, 0, :], b_t[:, s, :, :], k_t[:, s, :, :], v_now[:, :, :])[n]
            if n == 0:
                wait(pe, "kk", c)
                wait(pe, "zr", c, 1)
            if n == 1:
                wait(pe, "bonus", c)
                wait(pe, "bk", c, 3)
            if n == 2:
                wait(pe, "turned_kept", c, 1)
            if n == 3:
                wait(pe, "turned_kept", c, 2)
                wait(pe, "v_now", c)
            bank = prep_ps[(n + 1) % 2]
            for i in range(RT):
                last = nc.tensor.transpose(bank[:, i * CH:(i + 1) * CH], src[:, i, :], ident[:, :])
            up(last, "turned")

        def scores_pe(pe, c, s, n):
            src, g = ((b_t, 0), (b_t, 1), (k_t, 0), (k_t, 1))[n]
            if n == 0:
                wait(pe, "zr", c, 2)
                wait(pe, "bk", c, 3)
                wait(pe, "w_t", c, back=1)
            if n == 1:
                wait(pe, "y", c, back=1)
                wait(pe, "sa", c, 2, back=1)
            if n == 2:
                wait(pe, "state", c, 1, back=1)
            if n == 3:
                wait(pe, "a_kept", c, 1)
            h = g * HEAD
            for i in range(RT):
                last = nc.tensor.matmul(m[n % 3][:, i * 2 * CH:(i + 1) * 2 * CH], src[h:h + HEAD, s, i, :],
                                        zr[h:h + HEAD, s, i, :, :], start=True, stop=True)
            up(last, "a_ps")

        def beside_zeros(bank, i, lhs, tile, **flags):
            rhs = rounded[:, tile:EYE + 2:EYE + 1 - tile, :] if i == 0 else rounded[:, 0:tile + 1:tile, :]
            at = max(i - 1, 0) * CH
            return nc.tensor.matmul(bank[:, at:at + 2 * CH], lhs, rhs, skip_group_check=True, **flags)

        def units(bank, lhs, rhs, **flags):
            return nc.tensor.matmul(bank, lhs, rhs, skip_group_check=True, **flags)

        eyes4 = eye.unsqueeze(1).to_broadcast([P, RT, CH])
        X_AT, XT_AT, MX_AT = ([1 + (2 * k + g) * RT for g in range(2)] for k in range(3))

        def level0_pe(pe, c):
            for g in range(2):
                wait(pe, "first", c, g + 1)
                wait(pe, "a_kept", c, 4 if g == 0 else 3)
                if g == 0:
                    units(banks[g][1], eye, eyes4, start=True, stop=False)
                for i in range(RT):
                    last = beside_zeros(banks[g][1], i, mx[g][:, i, :], EYE, start=g == 1 and i == 0, stop=i == RT - 1)
                up(last, f"x_ps{g}")

        def grow_pe(pe, c, k):
            for g in range(2):
                wait(pe, f"x{g}", c, k)
                if k == 1:
                    wait(pe, "a_zb", c, g + 1)
                for i in range(RT):
                    last = beside_zeros(banks[g][0], i, a_zb[g][:, i, :], X_AT[g] + i, start=i == 0, stop=i == RT - 1)
                up(last, f"mx_ps{g}")

        def add4(bank, lhs, rhs_at, old=None):
            if old is not None:
                units(bank, eye, old, start=True, stop=False)
            for i in range(RT):
                last = beside_zeros(bank, i, lhs[:, i, :], rhs_at + i, start=old is None and i == 0, stop=i == RT - 1)
            return last

        def close_pe(pe, c, k):
            for g in range(2):
                wait(pe, f"mx{g}", c, k)
                if k == 1:
                    wait(pe, "first_t", c, g + 1)
                else:
                    wait(pe, f"xt{g}", c, k - 1)
                up(add4(banks[g][1], x_inv_t[g], MX_AT[g], None if g else x_inv[g]), f"x_ps{g}")
                up(add4(banks[g][2], mx[g], XT_AT[g], None if g else x_inv_t[g]), f"x_ps{g}")

        def refine_pe(pe, c):
            for g in range(2):
                wait(pe, f"x{g}", c, LEVELS)
                units(banks[g][0], eye, eyes4, start=True, stop=False)
                units(banks[g][0], neg_eye[:, :], x_inv[g], start=False, stop=False)
                for i in range(RT):
                    last = units(banks[g][0][:, i * CH:(i + 1) * CH], a_b[g][:, i, 0, :],
                                 x_inv[g][:, i, :].bitcast(F32), start=False, stop=i == RT - 1)
                up(last, f"res_ps{g}")
            wait(pe, "akv", c, back=1)
            vt = by_token[:, 3, :]
            for h in range(HEADS):
                i, g = h // 2, h % 2
                last = nc.tensor.matmul(m[2][:, h * HEAD:(h + 1) * HEAD], a_k[g][:, i, 0, :],
                                        vt[:, h * HEAD:(h + 1) * HEAD], start=True, stop=True)
            up(last, "akv_ps")
            for g in range(2):
                wait(pe, f"res{g}", c)
                wait(pe, f"xt{g}", c, LEVELS - 1)
                up(add4(banks[g][2], mx[g], XT_AT[g]), f"res_ps{g}")

        def w_pe(pe, c):
            for g in range(2):
                wait(pe, f"x_t{g}", c)
                for i in range(RT):
                    h = 2 * i + g
                    last = nc.tensor.matmul(m[0][g * HEAD:(g + 1) * HEAD, HALF + i * CH:HALF + (i + 1) * CH],
                                            by_token[:, 0, h * HEAD:(h + 1) * HEAD], x_t[g][:, i, :],
                                            start=True, stop=True)
            up(last, "w_ps")

        def sa_pe(pe, c):
            wait(pe, "akv", c)
            wait(pe, "w_t", c)
            wait(pe, "state_mid", c)
            for g, bank in enumerate((m[1][:, 0:HALF], m[2][:, HALF:SEQ])):
                o = g * HEAD
                for i in range(RT):
                    h = 2 * i + g
                    dst = bank[:, i * HEAD:(i + 1) * HEAD]
                    nc.tensor.matmul(dst, x_t[g][:, i, :], akv[:, h * HEAD:(h + 1) * HEAD],
                                     start=True, stop=False)
                    last = nc.tensor.matmul(dst, w_t[o:o + HEAD, i, :], state_mid[o:o + HEAD, i, :],
                                            start=False, stop=True)
                up(last, "sa_ps")

        def tail_pe(pe, c, s):
            vt = by_token[:, 3, :]
            wait(pe, "sa", c, 2)
            for h in range(HEADS):
                i, g = h // 2, h % 2
                o = g * HEAD
                dst = m[2][o:o + HEAD, i * HEAD:(i + 1) * HEAD]
                cols = slice(h * HEAD, (h + 1) * HEAD)
                nc.tensor.matmul(dst, by_token[:, 1, cols], sa[:, cols], start=True, stop=False)
                last = nc.tensor.matmul(dst, by_token[:, 2, cols], vt[:, cols], start=False, stop=True)
            up(last, "s_ps")
            for h in range(HEADS):
                i, g = h // 2, h % 2
                o = g * HEAD
                dst = m[1][o:o + HEAD, HALF + i * CH:HALF + (i + 1) * CH]
                cols = slice(h * HEAD, (h + 1) * HEAD)
                nc.tensor.matmul(dst, state_mid[o:o + HEAD, i, :], zr[o:o + HEAD, s, i, 1, :], start=True, stop=False)
                nc.tensor.matmul(dst, sa[:, cols], a_b[g][:, i, 1, :], start=False, stop=False)
                last = nc.tensor.matmul(dst, vt[:, cols], a_k[g][:, i, 1, :], start=False, stop=True)
            up(last, "y_ps")

        def codes_act(act, c):
            wait(act, "lora", c, 3, back=1)
            up(nc.scalar.activation(lora_x[0:HEAD, :], p_even[0:HEAD, 12, bass.ds(c * CH, CH)], ACT.Tanh), "lora_in")
            up(nc.scalar.activation(lora_x[HEAD:P, :], p_even[HEAD:P, 12, bass.ds(c * CH, CH)], ACT.Copy), "lora_in")
            up(nc.scalar.activation(sig_g[:, :], p_even[:, 13, bass.ds(c * CH, CH)], ACT.Sigmoid), "lora_in")

        def sigmoids_act(act, c):
            wait(act, "biased", c, 1)
            up(nc.scalar.activation(T["decay"], T["decay"], ACT.Sigmoid), "sigmoid")
            wait(act, "biased", c, 2)
            up(nc.scalar.activation(T["a"], T["a"], ACT.Sigmoid), "sigmoid")

        def square_act(act, c):
            wait(act, "kk_raw", c)
            if not (isinstance(c, int) and c == 0):
                wait(act, "y_sum", c, back=3)
            up(nc.scalar.activation(T["ksq"], T["kk"], ACT.Square), "ksq")

        def gate_act(act, c):
            wait(act, "k2", c, 2)
            wait(act, "lora", c, 3)
            up(nc.scalar.activation(tokens(4, RT, c), psum4(prep_ps[0]), ACT.Copy), "g_kept")

        def exps_act(act, c, s, k):
            if k == 0:
                wait(act, "centred", c, 1)
                wait(act, "state_mid", c, back=2)
                up(nc.scalar.activation(mid_scale[:, s, :], mid[:, :], ACT.Exp, scale=-EXP_MINUS_HALF), "exps")
                up(nc.scalar.activation(T["grow"], T["logsum"], ACT.Exp, scale=EXP_MINUS_HALF), "exps")
            else:
                wait(act, "centred", c, 2)
                up(nc.scalar.activation(T["decay"], T["decay"], ACT.Exp, scale=-EXP_MINUS_HALF), "exps")
                up(nc.scalar.activation(T["logsum"], T["logsum"], ACT.Exp, scale=-EXP_MINUS_HALF), "exps")

        def roots_act(act, c, first=0, n=2):
            tile_ = norms[:, first:first + n, :]
            if first == 0:
                wait(act, "k_floor", c)
            if first + n == 2:
                wait(act, "y_floor", c, back=2)
            up(nc.scalar.activation(tile_, tile_, ACT.Ln, scale=SUM_SCALE), "roots")
            wait(act, "roots", c, 1)
            up(nc.scalar.activation(tile_, tile_, ACT.Exp, scale=-0.5, bias=unscale[0:HEADS, 0:1]), "roots")

        def centred_act(act, c, last=False):
            wait(act, "yc_ps", c)
            if not last:
                wait(act, "k_sum", c + 1)
            wait(act, "out", c, 4, back=1)
            up(nc.scalar.activation(y_c[:, :, :], psum4(prep_ps[1]), ACT.Copy), "y_sq")
            up(nc.scalar.activation(y_sq[:, :, :], psum4(prep_ps[1]), ACT.Square), "y_sq")

        def turn_act(act, c, n):
            wait(act, "turned", c, n + 1)
            wait(act, ("w_ps", "s_ps", "s_ps", "y_ps")[n], c, back=1)
            up(nc.scalar.copy(by_token[:, n, :], prep_ps[(n + 1) % 2][:, :]), "turned_kept")

        def a_zb_act(act, c):
            for g in range(2):
                wait(act, "a_kept", c, g + 1)
                wait(act, f"mx_ps{g}", c, LEVELS - 1, back=1)
                up(nc.scalar.copy(a_zb[g][:, :, :], a_b[g][:, :, 0, :]), "a_zb")

        def level_act(act, c, k):
            wait(act, "x_ps0", c, 2 * k if k else 1)
            up(nc.scalar.copy(x_inv[0][:, :, :], psum4(banks[0][1])), "x0")
            if k:
                wait(act, "x_ps0", c, 2 * k + 1)
                up(nc.scalar.copy(x_inv_t[0][:, :, :], psum4(banks[0][2])), "xt0")

        def tail_act(act, c):
            wait(act, "res_ps0", c, 1)
            up(nc.scalar.copy(mx[0][:, :, :], psum4(banks[0][0])), "res0")
            wait(act, "akv_ps", c)
            up(nc.scalar.copy(akv[:, :], m[2][:, 0:HALF]), "akv")
            wait(act, "w_ps", c)
            wait(act, "out", c, 4, back=1)
            up(nc.scalar.copy(w_t[:, :, :], psum4(m[0][:, HALF:SEQ])), "w_t")

        def sa_act(act, c):
            by_half = sa[:, :].rearrange("p (i g v) -> p g i v", g=2, v=HEAD)
            for g, bank in enumerate((m[1][:, 0:RT * HEAD], m[2][:, HALF:HALF + RT * HEAD])):
                wait(act, "sa_ps", c, g + 1)
                up(nc.scalar.copy(by_half[:, g, :, :], bank.rearrange("p (i v) -> p i v", i=RT)), "sa")

        def y_act(act, c):
            wait(act, "y_ps", c)
            up(nc.scalar.copy(y_c[:, :, :], psum4(m[1][:, HALF:SEQ])), "y")

        def biased_dve(dve, c):
            wait(dve, "lora", c, 1)
            wait(dve, "zr", c, 1, back=1)
            up(tt(T["decay"], psum4(prep_ps[0]), per_channel("e_w0"), ALU.add), "biased")
            wait(dve, "lora", c, 2)
            wait(dve, "bk", c, 2, back=1)
            up(tt(T["a"], psum4(prep_ps[1]), per_channel("e_a0"), ALU.add), "biased")

        def logsum_dve(dve, c):
            wait(dve, "sigmoid", c, 1)
            for i in range(RT):
                up(nc.vector.tensor_tensor_scan(T["logsum"][:, i, :], ones[:, :], T["decay"][:, i, :], 0.0,
                                                ALU.mult, ALU.add), "logsum")
            wait(dve, "logsum", c, RT)
            wait(dve, "exps", c, 1, back=1)
            up(nc.vector.tensor_copy(mid[:, :], T["logsum"][:, :, CH // 2 - 1]), "mids")

        def k2_dve(dve, c):
            wait(dve, "sigmoid", c, 2)
            wait(dve, "bk", c, 1, back=1)
            up(nc.vector.scalar_tensor_tensor(out=T["k2"], in0=T["a"], scalar=-1.0, in1=per_channel("e_k_a"),
                                              op0=ALU.add, op1=ALU.mult), "k2")
            wait(dve, "k2", c, 1)
            up(nc.vector.scalar_tensor_tensor(out=T["k2"], in0=T["k2"], scalar=1.0, in1=tokens(4, RT, c),
                                              op0=ALU.add, op1=ALU.mult), "k2")

        def floor_dve(dve, c):
            wait(dve, "k_sum", c)
            wait(dve, "k_wide", c, back=1)
            up(nc.vector.tensor_scalar(norms[:, 0, :], prep_ps[1][0:HEADS, 0:CH], 1e-24, None, ALU.max), "k_floor")

        def y_floor_dve(dve, c):
            wait(dve, "y_sum", c)
            wait(dve, "y_wide", c, back=1)
            up(nc.vector.tensor_scalar(norms[:, 1, :], prep_ps[1][0:HEADS, 0:CH], 1.0 / HEAD, GN_EPS,
                                       ALU.mult, ALU.add), "y_floor")

        def zr_dve(dve, c, s):
            wait(dve, "k_wide", c)
            up(tt(T["kk"], T["kk"], psum4(prep_ps[1]), ALU.mult), "kk")
            wait(dve, "kk", c)
            wait(dve, "exps", c, 4)
            wait(dve, "y_ps", c, back=2)
            up(nc.vector.scalar_tensor_tensor(out=zr[:, s, :, 0, :], in0=T["kk"], scalar=-1.0, in1=T["decay"],
                                              op0=ALU.mult, op1=ALU.mult), "zr")
            up(tt(zr[:, s, :, 1, :], tokens(0, RT, c), T["logsum"], ALU.mult), "zr")
            up(nc.vector.tensor_copy(end_scale[:, s, :], T["logsum"][:, :, CH - 1]), "ends")

        def bonus_dve(dve, c):
            wait(dve, "bonus_sum", c)
            wait(dve, "v_now", c)
            up(tt(tokens(8, RT, c), psum4(prep_ps[0]), v_now[:, :, :], ALU.mult), "bonus")

        def gn_dve(dve, c):
            wait(dve, "y_wide", c)
            up(tt(y_c[:, :, :], y_c[:, :, :], psum4(prep_ps[1]), ALU.mult), "gn")

        def scores_dve(dve, c):
            mask = causal[:, :, :].rearrange("p a t -> p (a t)").unsqueeze(1).to_broadcast([P, RT, 2 * CH])
            for n, dst in enumerate((a_b[0], a_b[1], a_k[0], a_k[1])):
                wait(dve, "a_ps", c, n + 1)
                if n == 0:
                    wait(dve, "y_ps", c, back=1)
                    wait(dve, "a_zb", c, 2, back=1)
                up(tt(dst[:, :, :, :].rearrange("p i a t -> p i (a t)"),
                      m[n % 3][:, :].rearrange("p (i a) -> p i a", i=RT), mask, ALU.mult), "a_kept")
                if n < 2:
                    wait(dve, "a_kept", c, n + 1)
                    wait(dve, f"res_ps{n}", c, 2, back=1)
                    up(tt(mx[n][:, :, :], a_b[n][:, :, 0, :], level_mask[:, 0, :].unsqueeze(1).to_broadcast([P, RT, CH]),
                          ALU.mult), "first")

        def mask_dve(dve, c, k):
            for g in range(2):
                wait(dve, f"mx_ps{g}", c, k)
                if k == 1:
                    wait(dve, "first_t", c, g + 1)
                up(tt(mx[g][:, :, :], psum4(banks[g][0]),
                      level_mask[:, k, :].unsqueeze(1).to_broadcast([P, RT, CH]), ALU.mult), f"mx{g}")

        def add_old(c, g_old, bank, name):
            up(tt(g_old, psum4(bank), g_old.bitcast(F32), ALU.add), name)

        def level0_dve(dve, c):
            wait(dve, "x_ps1", c, 1)
            up(tt(x_inv[1][:, :, :], psum4(banks[1][1]), ident[:, :].unsqueeze(1).to_broadcast([P, RT, CH]), ALU.add), "x1")

        def close_dve(dve, c, k):
            wait(dve, "x_ps1", c, 2 * k)
            add_old(c, x_inv[1][:, :, :], banks[1][1], "x1")
            wait(dve, "x_ps1", c, 2 * k + 1)
            add_old(c, x_inv_t[1][:, :, :], banks[1][2], "xt1")

        def mid_state_dve(dve, c, s):
            wait(dve, "exps", c, 1)
            wait(dve, "state", c, 2, back=1)
            wait(dve, "y_ps", c, back=1)
            up(tt(state_mid[:, :, :], state[:, :, :], over_tokens(mid_scale[:, s, :], HEAD), ALU.mult), "state_mid")

        def tail_dve(dve, c, s):
            wait(dve, "res_ps1", c, 1)
            up(nc.vector.tensor_copy(mx[1][:, :, :], psum4(banks[1][0])), "res1")
            for g in range(2):
                wait(dve, f"res_ps{g}", c, 2)
                up(tt(x_t[g][:, :, :], psum4(banks[g][2]), x_inv_t[g][:, :, :].bitcast(F32), ALU.add), f"x_t{g}")
            wait(dve, "s_ps", c)
            up(tt(state[:, :, :], state_mid[:, :, :], m[2][:, 0:RT * HEAD].rearrange("p (i v) -> p i v", i=RT),
                  ALU.add), "state")
            wait(dve, "state", c, 1)
            up(tt(state[:, :, :], state[:, :, :], over_tokens(end_scale[:, s, :], HEAD), ALU.mult), "state")

        def ptt(pool, o, a, b, op, name):
            up(pool.tensor_tensor(o, a, b, op=op), name)

        def v_pool(pool, c):
            wait(pool, "bonus", c, back=1)
            wait(pool, "turned", c, 4, back=1)
            up(pool.tensor_copy(v_now[:, :, :], tokens(8, RT, c)), "v_now")

        def raw_pool(pool, c):
            wait(pool, "zr", c, 1, back=1)
            wait(pool, "bk", c, 3, back=1)
            ptt(pool, T["kk"], tokens(4, RT, c), per_channel("e_k_k"), ALU.mult, "kk_raw")

        def centre_pool(pool, c):
            wait(pool, "mids", c)
            ptt(pool, T["logsum"], T["logsum"], over_tokens(mid[:, :]), ALU.subtract, "centred")
            wait(pool, "centred", c, 1)
            ptt(pool, T["decay"], T["logsum"], T["decay"], ALU.subtract, "centred")

        def rk_pool(pool, c):
            wait(pool, "k2", c, 2)
            wait(pool, "bonus_sum", c, back=1)
            ptt(pool, T["rk"], tokens(0, RT, c), T["k2"], ALU.mult, "rk")
            wait(pool, "rk", c, 1)
            ptt(pool, T["rk"], T["rk"], per_channel("e_r_k"), ALU.mult, "rk")

        def k_pool(pool, c, s):
            wait(pool, "exps", c, 2)
            wait(pool, "a_ps", c, 4, back=2)
            wait(pool, "turned", c, 3, back=2)
            ptt(pool, k_t[:, s, :, :], T["k2"], T["grow"], ALU.mult, "bk")

        def b_pool(pool, c, s):
            wait(pool, "kk", c)
            wait(pool, "zr", c, 1)
            ptt(pool, T["kk"], T["kk"], T["a"], ALU.mult, "bk")
            wait(pool, "bk", c, 2)
            ptt(pool, b_t[:, s, :, :], T["kk"], T["grow"], ALU.mult, "bk")

        def first_pool(pool, c):
            for g in range(2):
                wait(pool, "first", c, g + 1)
                wait(pool, f"x_t{g}", c, back=1)
                ptt(pool, x_inv_t[g][:, :, :], mx[g][:, :, :].bitcast(F32),
                    ident[:, :].unsqueeze(1).to_broadcast([P, RT, CH]), ALU.add, "first_t")

        def out_pool(pool, c):
            wait(pool, "gn", c)
            ptt(pool, y_c[:, :, :], y_c[:, :, :], per_channel("e_ln_w"), ALU.mult, "out")
            wait(pool, "out", c, 1)
            ptt(pool, y_c[:, :, :], y_c[:, :, :], per_channel("e_ln_b"), ALU.add, "out")
            wait(pool, "out", c, 2)
            ptt(pool, y_c[:, :, :], y_c[:, :, :], tokens(8, RT, c), ALU.add, "out")
            wait(pool, "out", c, 3)
            ptt(pool, tokens(0, RT, c), y_c[:, :, :], tokens(4, RT, c), ALU.mult, "out")

        def turn_of_pe(pe, c, s, more, late):
            turn_pe(pe, c, s, 2)
            turn_pe(pe, c, s, 3)
            for n in (1, 2, 3):
                scores_pe(pe, c, s, n)
            if more:
                lora_pe(pe, c + 1, 0)
                lora_pe(pe, c + 1, 1)
                k_sum_pe(pe, c + 1)
            level0_pe(pe, c)
            if late:
                centre_pe(pe, c - 1)
            for k in range(1, LEVELS):
                grow_pe(pe, c, k)
                if more and k == 1:
                    lora_pe(pe, c + 1, 2)
                if late and k == 2:
                    y_sum_pe(pe, c - 1)
                if late and k == 4:
                    y_wide_pe(pe, c - 1)
                if more and k == 5:
                    k_wide_pe(pe, c + 1)
                if more and k == 6:
                    bonus_pe(pe, c + 1)
                close_pe(pe, c, k)
            refine_pe(pe, c)
            if more:
                turn_pe(pe, c + 1, 1 - s, 0)
            w_pe(pe, c)
            if more:
                turn_pe(pe, c + 1, 1 - s, 1)
            sa_pe(pe, c)
            if more:
                scores_pe(pe, c + 1, 1 - s, 0)
            tail_pe(pe, c, s)

        def turn_of_act(act, c, s, more, late):
            turn_act(act, c, 2)
            turn_act(act, c, 3)
            if more:
                codes_act(act, c + 1)
                square_act(act, c + 1)
            a_zb_act(act, c)
            if more:
                sigmoids_act(act, c + 1)
            for k in range(LEVELS):
                level_act(act, c, k)
                if late and k == 0:
                    centred_act(act, c - 1)
                if k == 2:
                    if more:
                        gate_act(act, c + 1)
                        roots_act(act, c + 1, 0, 2 if late else 1)
                    else:
                        roots_act(act, c + 1, 1, 1)
                if more and k == 3:
                    exps_act(act, c + 1, 1 - s, 0)
                if more and k == 4:
                    exps_act(act, c + 1, 1 - s, 1)
            tail_act(act, c)
            if more:
                turn_act(act, c + 1, 0)
            sa_act(act, c)
            if more:
                turn_act(act, c + 1, 1)
            y_act(act, c)

        def turn_of_dve(dve, c, s, more, late):
            scores_dve(dve, c)
            if more:
                biased_dve(dve, c + 1)
                floor_dve(dve, c + 1)
            level0_dve(dve, c)
            for k in range(1, LEVELS):
                mask_dve(dve, c, k)
                if more and k == 1:
                    logsum_dve(dve, c + 1)
                if k == 2:
                    if late:
                        y_floor_dve(dve, c - 1)
                    if more:
                        k2_dve(dve, c + 1)
                if k == 3:
                    mid_state_dve(dve, c, s)
                if late and k == 4:
                    gn_dve(dve, c - 1)
                if more and k == 6:
                    bonus_dve(dve, c + 1)
                close_dve(dve, c, k)
                if more and k == 5:
                    zr_dve(dve, c + 1, 1 - s)
            tail_dve(dve, c, s)

        def turn_of_pool(pool, c, s, more, late):
            if more:
                raw_pool(pool, c + 1)
            first_pool(pool, c)
            if more:
                v_pool(pool, c + 1)
                centre_pool(pool, c + 1)
                rk_pool(pool, c + 1)
                k_pool(pool, c + 1, 1 - s)
            if late:
                out_pool(pool, c - 1)
            if more:
                b_pool(pool, c + 1, 1 - s)

        def all_turns(eng, turn_of):
            turn_of(eng, 0, 0, True, False)
            with eng.Fori(0, NCH // 2 - 1) as n:
                for k in (1, 2):
                    turn_of(eng, n * 2 + k, k % 2, True, True)
            turn_of(eng, NCH - 1, 1, False, True)

        lora_loaded, r_consts, eyes, selectors = sem("lora_loaded"), sem("r_consts"), sem("r_eyes"), sem("r_selectors")
        with nc.Block() as block:
            @block.sync
            def _(sp):
                sp.dma_start(lora_w[0:HEAD, :], io["e_w2"][0, :, :]).then_inc(lora_loaded, 16)
                sp.dma_start(lora_w[HEAD:P, :], io["e_a2"][0, :, :]).then_inc(lora_loaded, 16)
                sp.dma_start(lora_g[:, :], io["e_g2"][0, :, :]).then_inc(lora_loaded, 16)

            @block.scalar
            def _(act):
                start(act, "act")
                act.wait_ge(r_consts, 3)
                codes_act(act, 0)
                sigmoids_act(act, 0)
                square_act(act, 0)
                gate_act(act, 0)
                exps_act(act, 0, 0, 0)
                exps_act(act, 0, 0, 1)
                roots_act(act, 0, 0, 1)
                turn_act(act, 0, 0)
                turn_act(act, 0, 1)
                all_turns(act, turn_of_act)
                centred_act(act, last_chunk, True)
                roots_act(act, last_chunk + 2, 1, 1)

            @block.vector
            def _(dve):
                start(dve, "dve")
                nc.vector.memset(ones[:, :], 1.0).then_inc(r_consts, 1)
                nc.vector.memset(state[:, :, :], 0.0).then_inc(r_consts, 1)
                nc.vector.memset(unscale[:, :], 5.545177444479562).then_inc(r_consts, 1)
                nc.vector.tensor_copy(eye, ident[:, :]).then_inc(eyes, 1)
                for at in (0, EYE + 1):
                    nc.vector.tensor_scalar(rounded[:, at, :], ident[:, :], 0.0, None, ALU.mult).then_inc(eyes, 1)
                nc.vector.tensor_scalar(neg_eye[:, :], ident[:, :], -1.0, None, ALU.mult).then_inc(eyes, 1)
                dve.wait_ge(r_consts, 3)
                biased_dve(dve, 0)
                logsum_dve(dve, 0)
                k2_dve(dve, 0)
                floor_dve(dve, 0)
                bonus_dve(dve, 0)
                zr_dve(dve, 0, 0)
                all_turns(dve, turn_of_dve)
                y_floor_dve(dve, last_chunk)
                gn_dve(dve, last_chunk)

            @block.gpsimd
            def _(pool):
                start(pool, "pool")
                pool.memset(head_in[:, :, :], 0.0).then_inc(selectors, 1)
                pool.memset(head_out[:, :, :], 1.0).then_inc(selectors, 1)
                pool.wait_ge(selectors, 2)
                for i in range(RT):
                    pool.tensor_copy(head_in[:, i, 2 * i:2 * i + 2], head_ones[:, 0:P:HEAD]).then_inc(selectors, 1)
                by_row = head_out[:, :, :].rearrange("h i c -> h (i c)")
                pool.affine_select(out=by_row, in_=by_row, compare_op=ALU.is_ge, fill=0.0, base=0,
                                   pattern=[[1, RW]], channel_multiplier=-HEAD).then_inc(selectors, 1)
                pool.wait_ge(selectors, 2 + RT + 1)
                pool.affine_select(out=by_row, in_=by_row, compare_op=ALU.is_ge, fill=0.0, base=HEAD - 1,
                                   pattern=[[-1, RW]], channel_multiplier=HEAD).then_inc(selectors, 2)
                raw_pool(pool, 0)
                v_pool(pool, 0)
                centre_pool(pool, 0)
                rk_pool(pool, 0)
                k_pool(pool, 0, 0)
                b_pool(pool, 0, 0)
                all_turns(pool, turn_of_pool)
                out_pool(pool, last_chunk)

            @block.tensor
            def _(pe):
                start(pe, "pe")
                pe.wait_ge(lora_loaded, 48)
                pe.wait_ge(r_consts, 3)
                pe.wait_ge(eyes, 4)
                pe.wait_ge(selectors, 2 + RT + 3)
                for k in range(3):
                    lora_pe(pe, 0, k)
                k_sum_pe(pe, 0)
                bonus_pe(pe, 0)
                k_wide_pe(pe, 0)
                turn_pe(pe, 0, 0, 0)
                turn_pe(pe, 0, 0, 1)
                scores_pe(pe, 0, 0, 0)
                all_turns(pe, turn_of_pe)
                centre_pe(pe, last_chunk)
                y_sum_pe(pe, last_chunk)
                y_wide_pe(pe, last_chunk)

    Dense.q, Dense.u = 2 * EV, EV

    def residual_add_dve(dve, dn, c, slot, pair, par):
        dn.wait_unit(dve, pair, par)
        here = x_res[:, bass.ds(c, 1), :]
        nc.vector.tensor_tensor(here, here, dn.acc[slot][:, :], ALU.add).then_inc(unit_free, 1)

    with ExitStack() as sc:
        y_hi = sb(sc, "y_hi", [P, DT, SEQ], F32R)
        y_lo = sb(sc, "y_lo", [P, DT, SEQ], F32R)
        dn = Dense(sc, "o")
        w_out = io["e_w_out"].rearrange("a (k p) n -> (a p) k n", p=P)
        y_hi_done, y_lo_done = sem("y_hi_done"), sem("y_lo_done")
        y_tiles = (0, 1, 2, 3, 14, 15, 16, 17)
        q0, u0 = Dense.q // 2, Dense.u
        with nc.Block() as block:
            @block.sync
            def _(sp):
                with sp.Fori(0, DT // 2) as i:
                    for s in range(2):
                        dn.load(sp, w_out, DT, bass.ds(i * (2 * P) + s * P, P), i * 2 + (q0 + s), 0)

            @block.gpsimd
            def _(pool):
                with pool.Fori(0, DT // 2) as i:
                    for s in range(2):
                        dn.take_lo(pool, DT, i * 2 + (q0 + s), 0)

            @block.scalar
            def _(act):
                for k, tile in enumerate(y_tiles):
                    nc.scalar.copy(y_hi[:, k, :], p_even[:, tile, :]).then_inc(y_hi_done, 1)
                with act.Fori(0, DT // 2) as i:
                    for s in range(2):
                        dn.take_hi(act, DT, i * 2 + (q0 + s), 0)

            @block.tensor
            def _(pe):
                pe.wait_ge(y_lo_done, DT)
                with pe.Fori(0, DT // 2) as i:
                    for s in range(2):
                        dn.product(pe, DT, y_hi, y_lo, i * 2 + (u0 + s), s, i * 2 + (q0 + s), 0)

            @block.vector
            def _(dve):
                for k, tile in enumerate(y_tiles):
                    dve.wait_ge(y_hi_done, k + 1)
                    nc.vector.tensor_tensor(y_lo[:, k, :], p_even[:, tile, :], y_hi[:, k, :].bitcast(F32),
                                            ALU.subtract).then_inc(y_lo_done, 1)
                with dve.Fori(0, DT // 2) as i:
                    for s in range(2):
                        residual_add_dve(dve, dn, i * 2 + s, s, i * 2 + (q0 + s), 1)
        Dense.q += 2 * DT
        Dense.u += DT
    proj.close()

    def conv_ffn(layer):
        tag = f"f{layer}"
        with ExitStack() as sc:
            xn_hi = sb(sc, "xn_hi_" + tag, [P, DT, SEQ], F32R)
            xn_lo = sb(sc, "xn_lo_" + tag, [P, DT, SEQ], F32R)
            norm(tag, "f_norm_g", DT * layer, xn_hi, xn_lo)
            dn = Dense(sc, tag)
            h_hi = sb(sc, "h_hi_" + tag, [P, FGROUP, SEQ], F32R)
            h_lo = sb(sc, "h_lo_" + tag, [P, FGROUP, SEQ], F32R)
            gate = sb(sc, "gate_" + tag, [P, SEQ])
            val = sb(sc, "val_" + tag, [P, SEQ])
            w_up = io["f_w_up"][layer, :, :].rearrange("(k p) n -> p k n", p=P)
            w_down = io["f_w_down"][layer, :, :].rearrange("(g k p) n -> g p k n", g=2, p=P)
            f_start, f_tap, f_silu, f_h, f_hi, f_lo = (
                sem("f_" + n) for n in ("start", "tap", "silu", "h", "hi", "lo"))
            made = layer * FT
            UP = 2 * FGROUP
            PAIRS = UP + 3 * DT // 2
            UNITS = 2 * FGROUP + DT
            q0, u0 = Dense.q // 2, Dense.u
            taps, bias = COL["f_conv_w"] + layer * 3 * 2 * FT, COL["f_conv_b"] + layer * 2 * FT

            def param(first, tile):
                return prm[:, bass.ds(tile + first, 1)]

            def tile_of(g, m, half):
                return g * FGROUP + m + half * FT

            def up_cols(g, m, half):
                return bass.ds(g * (FGROUP * P) + m * P + half * D_FF, P)

            def up_pair(g, m, half):
                return g * PAIRS + m * 2 + (half + q0)

            def up_unit(g, m, half):
                return g * UNITS + m * 2 + (half + u0)

            with nc.Block() as block:
                @block.sync
                def _(sp):
                    with sp.Fori(0, 2) as g:
                        with sp.Fori(0, FGROUP) as m:
                            for half in range(2):
                                dn.load(sp, w_up, DT, up_cols(g, m, half), up_pair(g, m, half), 0)
                        with sp.Fori(0, DT // 2) as i:
                            for s in range(2):
                                dn.load(sp, w_down[bass.ds(g, 1), :, :, :].rearrange("g p k n -> (g p) k n"), FGROUP,
                                        bass.ds(i * (2 * P) + s * P, P), g * PAIRS + i * 3 + (UP + q0 + s), s)

                @block.tensor
                def _(pe):
                    with pe.Fori(0, 2) as g:
                        with pe.Fori(0, FGROUP) as m:
                            for half in range(2):
                                dn.product(pe, DT, xn_hi, xn_lo, up_unit(g, m, half), half, up_pair(g, m, half), 0)
                        with pe.Fori(0, DT // 2) as i:
                            for s in range(2):
                                pe.wait_ge(f_lo, g * FGROUP + (made + FGROUP + 1))
                                dn.product(pe, FGROUP, h_hi, h_lo, g * UNITS + i * 2 + (2 * FGROUP + u0 + s), s,
                                           g * PAIRS + i * 3 + (UP + q0 + s), s)

                @block.scalar
                def _(act):
                    def begin(g, m, half):
                        act.wait_ge(f_lo if half else f_h, g * FGROUP + m + (made + 1))
                        dn.wait_unit(act, up_pair(g, m, half), 1)
                        nc.scalar.activation((gate, val)[half][:, :], dn.acc[half][:, :], ACT.Identity,
                                             scale=param(taps + 2 * 2 * FT, tile_of(g, m, half)),
                                             bias=param(bias, tile_of(g, m, half))).then_inc(f_start, 1)

                    def silu(g, m):
                        act.wait_ge(unit_free, up_unit(g, m, 0) + 3)
                        nc.scalar.activation(gate[:, :], gate[:, :], ACT.Silu).then_inc(f_silu, 1)

                    def keep_hi(g, m):
                        act.wait_ge(f_h, g * FGROUP + m + (made + 2))
                        nc.scalar.copy(h_hi[:, bass.ds(m, 1), :], val[:, :]).then_inc(f_hi, 1)

                    with act.Fori(0, 2) as g:
                        dn.take_hi(act, DT, g * PAIRS + q0, 0)
                        dn.take_hi(act, DT, g * PAIRS + (q0 + 1), 0)
                        begin(g, 0, 0)
                        silu(g, 0)
                        with act.Fori(1, FGROUP) as m:
                            dn.take_hi(act, DT, up_pair(g, m, 0), 0)
                            begin(g, m + (-1), 1)
                            keep_hi(g, m + (-1))
                            dn.take_hi(act, DT, up_pair(g, m, 1), 0)
                            begin(g, m, 0)
                            silu(g, m)
                        begin(g, FGROUP - 1, 1)
                        keep_hi(g, FGROUP - 1)
                        with act.Fori(0, DT // 2) as i:
                            for s in range(2):
                                dn.take_hi(act, FGROUP, g * PAIRS + i * 3 + (UP + q0 + s), s)

                @block.vector
                def _(dve):
                    with dve.Fori(0, 2) as g:
                        with dve.Fori(0, FGROUP) as m:
                            for half in range(2):
                                n = g * (2 * FGROUP) + m * 2 + (half + 2 * made)
                                dve.wait_ge(f_start, n + 1)
                                for back in (1, 2):
                                    here = (gate, val)[half][:, back:SEQ]
                                    if back == 2:
                                        dve.wait_ge(f_tap, n + 1)
                                    nc.vector.scalar_tensor_tensor(
                                        out=here, in0=dn.acc[half][:, 0:SEQ - back],
                                        scalar=param(taps + (2 - back) * 2 * FT, tile_of(g, m, half)), in1=here,
                                        op0=ALU.mult, op1=ALU.add).then_inc(f_tap if back == 1 else unit_free, 1)
                        with dve.Fori(0, DT // 2) as i:
                            residual_add_dve(dve, dn, i * 2, 0, g * PAIRS + i * 3 + (UP + q0 + 1), 0)
                            residual_add_dve(dve, dn, i * 2 + 1, 1, g * PAIRS + i * 3 + (UP + q0 + 2), 1)

                @block.gpsimd
                def _(pool):
                    def inner(g, m):
                        pool.wait_ge(f_silu, g * FGROUP + m + (made + 1))
                        pool.wait_ge(unit_free, up_unit(g, m, 1) + 3)
                        pool.tensor_tensor(val[:, :], gate[:, :], val[:, :], op=ALU.mult).then_inc(f_h, 1)
                        pool.wait_ge(f_hi, g * FGROUP + m + (made + 1))
                        pool.tensor_tensor(h_lo[:, bass.ds(m, 1), :], val[:, :],
                                           h_hi[:, bass.ds(m, 1), :].bitcast(F32), op=ALU.subtract).then_inc(f_lo, 1)

                    if layer == 0:
                        pool.sem_inc(f_h, 1)
                        pool.sem_inc(f_lo, 1)
                    with pool.Fori(0, 2) as g:
                        dn.take_lo(pool, DT, g * PAIRS + q0, 0)
                        dn.take_lo(pool, DT, g * PAIRS + (q0 + 1), 0)
                        with pool.Fori(1, FGROUP) as m:
                            dn.take_lo(pool, DT, up_pair(g, m, 0), 0)
                            inner(g, m + (-1))
                            dn.take_lo(pool, DT, up_pair(g, m, 1), 0)
                        inner(g, FGROUP - 1)
                        with pool.Fori(0, DT // 2) as i:
                            for s in range(2):
                                dn.take_lo(pool, FGROUP, g * PAIRS + i * 3 + (UP + q0 + s), s)
            Dense.q += 2 * 2 * PAIRS
            Dense.u += 2 * UNITS

    conv_ffn(0)

    s5 = ctx.enter_context(ExitStack())
    u_s5 = sb(s5, "u_s5", [P, DT, SEQ])
    K9 = L5 + 1
    rot = sb(s5, "rot", [P, 2, S5_PAIRS, N5])
    power = sb(s5, "power", [P, 2, K9, S5_PAIRS])
    b_bar = sb(s5, "b_bar", [P, 2, S5_PAIRS, 16])
    c_s5 = sb(s5, "c_s5", [P, 3, S5_PAIRS, 16])
    decay8 = sb(s5, "decay8", [P, S5_PAIRS])
    with ExitStack() as sc:
        xn_hi = sb(sc, "xn_hi_s", [P, DT, SEQ], F32R)
        xn_lo = sb(sc, "xn_lo_s", [P, DT, SEQ], F32R)
        norm("s", "o_norm_g", 0, xn_hi, xn_lo)
        dn = Dense(sc, "s")
        s_rows = sb(sc, "s_rows", [S5_PAIRS, 3, P])
        dt_rows = sb(sc, "dt_rows", [S5_PAIRS, 2])
        b_raw = sb(sc, "b_raw", [P, 2, S5_PAIRS, 16])
        c_raw = sb(sc, "c_raw", [P, DT, 2, 64])
        small = sb(sc, "small", [P, 20, S5_PAIRS])
        s_ps = ps(sc, "s_ps", [P, 3, S5_PAIRS])
        c_ps = ps(sc, "c_ps", [P, SEQ])
        w_in = io["o_w_in"].rearrange("a (k p) n -> (a p) k n", p=P)
        s_loaded, c_loaded, s_turned, c_turned, dt_wide = (
            sem(n) for n in ("s_loaded", "c_loaded", "s_turned", "c_turned", "dt_wide"))
        s_act, s_arg, c_kept = sem("s_act"), sem("s_arg"), sem("c_kept")
        q0, u0 = Dense.q // 2, Dense.u
        V = {n: small[:, k, :] for k, n in enumerate(
            "lre dt lr ang turns mag s2 h c2 cos sin zr den qre qim t1 t2 ck sk aim".split())}
        TWO_PI = 6.283185307179586
        TURN1 = 6.28125
        TURN2 = 0.0019340515136718750
        TURN3 = TWO_PI - TURN1 - TURN2
        ROUND = 12582912.0
        with nc.Block() as block:
            @block.sync
            def _(sp):
                for k, name in enumerate(("o_A_re", "o_A_im")):
                    sp.dma_start(s_rows[:, k, :], io[name].rearrange("a (r g) n -> (a r) (g n)", g=2)).then_inc(s_loaded, 16)
                sp.dma_start(dt_rows[:, :], io["o_log_dt"].rearrange("a (r g) -> (a r) g", g=2)).then_inc(s_loaded, 16)
                for k in range(2):
                    sp.dma_start(c_raw[:, :, k, :], io["o_C_re"].rearrange("a (t g) c n -> (a g c) t n", g=8)).then_inc(c_loaded, 16)
                for k, name in enumerate(("o_B_re", "o_B_im")):
                    b = io[name].rearrange("a (r g) n c -> (a g) n r c", g=2)
                    for g in range(2):
                        sp.dma_start(b_raw[g * 64:(g + 1) * 64, k, :, :], b[g, :, :, :]).then_inc(s_loaded, 16)
                with sp.Fori(0, DT // 2) as i:
                    for s in range(2):
                        dn.load(sp, w_in, DT, bass.ds(i * (2 * P) + s * P, P), i * 2 + (q0 + s), 0)
                sp.wait_ge(c_turned, 1)
                for k in range(2):
                    sp.dma_start(c_raw[:, :, k, :], io["o_C_im"].rearrange("a (t g) c n -> (a g c) t n", g=8)).then_inc(c_loaded, 16)

            @block.gpsimd
            def _(pool):
                with pool.Fori(0, DT // 2) as i:
                    for s in range(2):
                        dn.take_lo(pool, DT, i * 2 + (q0 + s), 0)

            @block.tensor
            def _(pe):
                pe.wait_ge(s_loaded, 7 * 16)
                pe.wait_ge(dt_wide, 1)
                for k in range(3):
                    last = nc.tensor.transpose(s_ps[:, k, :], s_rows[:, k, :], ident[0:S5_PAIRS, 0:S5_PAIRS])
                last.then_inc(s_turned, 1)

                def turn_c(n):
                    pe.wait_ge(c_loaded, 32 * (n + 1))
                    for t in range(DT):
                        last = nc.tensor.transpose(c_ps[:, t * P:(t + 1) * P],
                                                   c_raw[:, t, :, :].rearrange("p k n -> p (k n)"), ident[:, :])
                    last.then_inc(c_turned, 1)

                turn_c(0)
                with pe.Fori(0, DT // 2) as i:
                    for s in range(2):
                        dn.product(pe, DT, xn_hi, xn_lo, i * 2 + (u0 + s), s, i * 2 + (q0 + s), 0)
                pe.wait_ge(c_kept, 2)
                turn_c(1)

            @block.scalar
            def _(act):
                def keep_u(i, slot):
                    dn.wait_unit(act, i + q0, 1)
                    nc.scalar.copy(u_s5[:, bass.ds(i, 1), :].rearrange("p a (j n) -> p (a j) n", j=L5),
                                   dn.acc[slot][:, :].rearrange("p (n j) -> p j n", j=L5)).then_inc(unit_free, 1)

                act.wait_ge(s_arg, 1)
                nc.scalar.activation(V["dt"], V["dt"], ACT.Exp).then_inc(s_act, 1)
                act.wait_ge(s_arg, 2)
                nc.scalar.activation(V["mag"], V["lr"], ACT.Exp).then_inc(s_act, 1)
                act.wait_ge(s_arg, 3)
                nc.scalar.activation(V["s2"], V["h"], ACT.Sin).then_inc(s_act, 1)
                act.wait_ge(s_arg, 4)
                nc.scalar.activation(V["c2"], V["c2"], ACT.Sin).then_inc(s_act, 1)
                with act.Fori(0, DT // 2) as i:
                    for s in range(2):
                        dn.take_hi(act, DT, i * 2 + (q0 + s), 0)
                        keep_u(i * 2 + s, s)

            @block.vector
            def _(dve):
                link = Link(dve, "s5_setup")

                def mul(o, a, b, op=ALU.mult):
                    link.run(nc.vector.tensor_tensor(o, a, b, op))

                def affine(o, a, k1, k2=None, op0=ALU.mult, op1=ALU.add):
                    link.run(nc.vector.tensor_scalar(o, a, k1, k2, op0, op1) if k2 is not None
                             else nc.vector.tensor_scalar(o, a, k1, None, op0))

                def fused(o, a, k, b, op0=ALU.mult, op1=ALU.add):
                    link.run(nc.vector.scalar_tensor_tensor(out=o, in0=a, scalar=k, in1=b, op0=op0, op1=op1))

                def keep_c(n):
                    dve.wait_ge(c_turned, n + 1)
                    for g in range(2):
                        half = slice(g * 64, (g + 1) * 64)
                        src = c_ps[half, :].rearrange("p (r g c) -> p g r c", g=2, c=16)
                        nc.vector.tensor_copy(c_s5[half, n, :, :], src[:, g, :, :]).then_inc(c_kept, 1)

                dve.wait_ge(s_loaded, 7 * 16)
                nc.vector.tensor_copy(s_rows[:, 2, :].rearrange("p (g n) -> p g n", g=2),
                                      dt_rows[:, :].unsqueeze(2).to_broadcast([S5_PAIRS, 2, 64])).then_inc(dt_wide, 1)
                dve.wait_ge(s_turned, 1)
                affine(V["lre"], s_ps[:, 0, :], -1e-4, None, ALU.min)
                link.run(nc.vector.tensor_copy(V["aim"], s_ps[:, 1, :]))
                nc.vector.tensor_copy(V["dt"], s_ps[:, 2, :]).then_inc(s_arg, 1)
                dve.wait_ge(s_act, 1)
                mul(V["ang"], V["aim"], V["dt"])
                nc.vector.tensor_tensor(V["lr"], V["lre"], V["dt"], ALU.mult).then_inc(s_arg, 1)
                affine(V["turns"], V["ang"], 1 / TWO_PI, ROUND)
                affine(V["turns"], V["turns"], -ROUND, None, ALU.add)
                fused(V["ang"], V["turns"], -TURN1, V["ang"])
                fused(V["ang"], V["turns"], -TURN2, V["ang"])
                fused(V["ang"], V["turns"], -TURN3, V["ang"])
                dve.wait_ge(s_arg, 2)
                nc.vector.tensor_scalar(V["h"], V["ang"], 0.5, None, ALU.mult).then_inc(s_arg, 1)
                dve.wait_ge(s_arg, 3)
                fused(V["c2"], V["h"], -1.0, V["h"], ALU.mult, ALU.max)
                nc.vector.tensor_scalar(V["c2"], V["c2"], -1.0, TWO_PI / 4, ALU.mult, ALU.add).then_inc(s_arg, 1)
                dve.wait_ge(s_act, 4)
                fused(V["sin"], V["s2"], 2.0, V["c2"], ALU.mult, ALU.mult)
                mul(V["t1"], V["s2"], V["s2"])
                affine(V["cos"], V["t1"], -2.0, 1.0)
                link.run(nc.vector.memset(power[:, 0, 0, :], 1.0))
                link.run(nc.vector.memset(power[:, 1, 0, :], 0.0))
                a_re, a_im = power[:, 0, 1, :], power[:, 1, 1, :]
                mul(a_re, V["mag"], V["cos"])
                mul(a_im, V["mag"], V["sin"])
                for k in range(2, K9):
                    for part, op in ((0, ALU.subtract), (1, ALU.add)):
                        mul(V["t1"], power[:, 0, k - 1, :], (a_re, a_im)[part])
                        mul(V["t2"], power[:, 1, k - 1, :], (a_im, a_re)[part])
                        mul(power[:, part, k, :], V["t1"], V["t2"], op)
                mul(V["t1"], V["lre"], V["lre"])
                mul(V["t2"], V["aim"], V["aim"])
                mul(V["den"], V["t1"], V["t2"], ALU.add)
                link.run(nc.vector.reciprocal(V["den"], V["den"]))
                affine(V["zr"], a_re, -1.0, None, ALU.add)
                for q, x, y, op in ((V["qre"], V["zr"], a_im, ALU.add), (V["qim"], a_im, V["zr"], ALU.subtract)):
                    mul(V["t1"], x, V["lre"])
                    mul(V["t2"], y, V["aim"])
                    mul(V["t1"], V["t1"], V["t2"], op)
                    mul(q, V["t1"], V["den"])
                wide = [P, S5_PAIRS, 16]
                q_re, q_im = (V[n].unsqueeze(2).to_broadcast(wide) for n in ("qre", "qim"))
                tmp = rot[:, 1, 0:4, :].rearrange("p r n -> p (r n)").rearrange("p (r c) -> p r c", c=16)
                mul(b_bar[:, 0, :, :], b_raw[:, 0, :, :], q_re)
                mul(tmp, b_raw[:, 1, :, :], q_im)
                mul(b_bar[:, 0, :, :], b_bar[:, 0, :, :], tmp, ALU.subtract)
                mul(b_bar[:, 1, :, :], b_raw[:, 1, :, :], q_re)
                mul(tmp, b_raw[:, 0, :, :], q_im)
                mul(b_bar[:, 1, :, :], b_bar[:, 1, :, :], tmp, ALU.add)
                keep_c(0)
                mul(V["mag"], V["mag"], V["mag"])
                mul(V["mag"], V["mag"], V["mag"])
                mul(decay8[:, :], V["mag"], V["mag"])
                link.run(nc.vector.tensor_copy(V["ck"], V["cos"]))
                link.run(nc.vector.tensor_copy(V["sk"], V["sin"]))

                def square_turn():
                    mul(V["t1"], V["ck"], V["ck"])
                    mul(V["t2"], V["sk"], V["sk"])
                    fused(V["sk"], V["ck"], 2.0, V["sk"], ALU.mult, ALU.mult)
                    mul(V["ck"], V["t1"], V["t2"], ALU.subtract)

                for _ in range(3):
                    square_turn()
                link.run(nc.vector.memset(rot[:, 0, :, 0:1], 1.0))
                link.run(nc.vector.memset(rot[:, 1, :, 0:1], 0.0))
                n = 1
                while n < N5:
                    for lo in range(0, S5_PAIRS, 8):
                        r = slice(lo, lo + 8)
                        step = [P, 8, n]
                        ck, sk = (V[x][:, r].unsqueeze(2).to_broadcast(step) for x in ("ck", "sk"))
                        cos, sin = rot[:, 0, r, 0:n], rot[:, 1, r, 0:n]
                        new = [rot[:, k, r, n:2 * n] for k in range(2)]
                        part = b_raw[:, 0, :, :].rearrange("p r c -> p (r c)")[:, 0:8 * n].rearrange("p (r n) -> p r n", r=8)
                        for k, (x, y, op) in enumerate(((cos, sin, ALU.subtract), (sin, cos, ALU.add))):
                            mul(new[k], x, ck)
                            mul(part, y, sk)
                            mul(new[k], new[k], part, op)
                    n *= 2
                    if n < N5:
                        square_turn()
                keep_c(1)
                dve.wait_ge(c_kept, 4)
                affine(c_s5[:, 2, :, :], c_s5[:, 0, :, :], -1.0)
                link.close()
        Dense.q += 2 * DT
        Dense.u += DT

    with ExitStack() as sc:
        gx = sb(sc, "gx", [P, 2, L5, 4, 2, 16])
        hx = sb(sc, "hx", [P, 2, 2, K9, 4, 2, 16])
        g_in = sb(sc, "g_in", [P, L5, 2, P])
        k_fir = sb(sc, "k_fir", [P, L5, P])
        u_now = sb(sc, "u_now", [P, 2, L5, N5])
        m1 = sb(sc, "m1", [P, K9, 4, 16])
        m2 = sb(sc, "m2", [P, K9, 4, 16])
        m3 = sb(sc, "m3", [P, K9, 4, 16])
        m4 = sb(sc, "m4", [P, K9, 4, 16])
        first0 = sb(sc, "first0", [P, 4, N5])
        keep8 = sb(sc, "keep8", [P, 4, N5])
        f_hat = sb(sc, "f_hat", [P, 2, 4, N5])
        s_hat = sb(sc, "s_hat", [P, 2, 4, N5])
        r_tmp = sb(sc, "r_tmp", [P, 2, 4, N5])
        s_prev = sb(sc, "s_prev", [P, 2, 2, 4, N5])
        f_ps = ps(sc, "f_ps", [P, 4, 2, 2 * N5])
        y_ps = ps(sc, "y5_ps", [P, L5, N5])
        tk_ps = [ps(sc, f"tk_ps{k}", [P, HALF]) for k in range(2)]
        R5 = Rounds("s5", {
            "pool": {"m": 8, "gx": 4, "hx": 4},
            "pe": {"turn": 4, "k": 1, "f": 1, "fir": 1, "y": 1},
            "act": {"u": 1, "g": 4, "out": 1},
            "dve": {"keep8": 1, "k_kept": 5, "rin": 6, "scan": 2, "rout": 6},
        })
        s5_clear = sem("s5_clear")

        def make_pool(pool, i, s):
            def pw(part, n):
                return power[:, part, 0:n, bass.ds(i * 4, 4)].unsqueeze(3).to_broadcast([P, n, 4, 16])

            def over_k(t, n):
                return t[:, bass.ds(i * 4, 4), :].unsqueeze(1).to_broadcast([P, n, 4, 16])

            b_re, b_im = (over_k(b_bar[:, k, :, :], L5) for k in range(2))
            c_re, c_im, c_neg = (over_k(c_s5[:, k, :, :], K9) for k in range(3))
            R5.wait(pool, "gx", i, 4, back=1)
            R5.wait(pool, "hx", i, 4, back=1)
            for o, a, b in ((m1, pw(0, L5), b_re), (m2, pw(1, L5), b_im), (m3, pw(0, L5), b_im), (m4, pw(1, L5), b_re)):
                R5.up(pool.tensor_tensor(o[:, 0:L5, :, :], a, b, op=ALU.mult), "m")
            R5.wait(pool, "m", i, 4)
            R5.wait(pool, "turn", i, 4, back=1)
            R5.wait(pool, "k", i, 1, back=1)
            for part, (a, b, op) in enumerate(((m1, m2, ALU.subtract), (m3, m4, ALU.add))):
                for g in range(2):
                    half = slice(g * 64, (g + 1) * 64)
                    R5.up(pool.tensor_tensor(gx[half, part, :, :, g, :], a[half, 0:L5, :, :], b[half, 0:L5, :, :], op=op), "gx")
            R5.wait(pool, "gx", i, 4)
            for o, a, b in ((m1, c_re, pw(0, K9)), (m2, c_im, pw(1, K9)), (m3, c_neg, pw(1, K9)), (m4, c_im, pw(0, K9))):
                R5.up(pool.tensor_tensor(o[:, :, :, :], a, b, op=ALU.mult), "m")
            R5.wait(pool, "m", i, 8)
            R5.wait(pool, "y", i, 1, back=2)
            for part, (a, b) in enumerate(((m1, m2), (m3, m4))):
                for g in range(2):
                    half = slice(g * 64, (g + 1) * 64)
                    R5.up(pool.tensor_tensor(hx[half, s, part, :, :, g, :], a[half, :, :, :], b[half, :, :, :],
                                             op=ALU.subtract), "hx")

        def turn_pe(pe, i, s):
            R5.wait(pe, "gx", i, 4)
            for n in range(4):
                if n == 0:
                    R5.wait(pe, "g", i, 3, back=1)
                elif n == 1:
                    R5.wait(pe, "k_kept", i, 4, back=1)
                else:
                    R5.wait(pe, "g", i, n - 1)
                for x in range(4):
                    k, part = (4 * n + x) // 2, x % 2
                    last = nc.tensor.transpose(tk_ps[n % 2][:, x * P:(x + 1) * P],
                                               gx[:, part, k, :, :, :].rearrange("p q g c -> p (q g c)"), ident[:, :])
                R5.up(last, "turn")
            R5.wait(pe, "hx", i, 4)
            R5.wait(pe, "g", i, 4)
            for q in range(4):
                for part in range(2):
                    last = nc.tensor.matmul(tk_ps[1][32 * q:32 * q + 32, 0:L5 * 32],
                                            gx[:, part, 0, q, :, :].rearrange("p g c -> p (g c)"),
                                            hx[:, s, part, 0:L5, q, :, :].rearrange("p k g c -> p k (g c)"),
                                            start=part == 0, stop=part == 1)
            R5.up(last, "k")

        def turn_act(act, i, s):
            R5.wait(act, "y", i, 1, back=2)
            R5.up(nc.scalar.copy(u_now[:, s, :, :], u_s5[:, bass.ds(i, 1), :].rearrange("p a (j n) -> p (a j) n", j=L5)), "u")
            R5.wait(act, "f", i, 1, back=1)
            for n in range(4):
                R5.wait(act, "turn", i, n + 1)
                R5.up(nc.scalar.copy(g_in[:, 2 * n:2 * n + 2, :, :].rearrange("p k r c -> p (k r c)"),
                                     tk_ps[n % 2][:, :]), "g")

        def k_dve(dve, i, s):
            R5.wait(dve, "k", i)
            R5.wait(dve, "fir", i, 1, back=1)
            for q in range(4):
                rows = slice(32 * q, 32 * q + 32)
                R5.up(nc.vector.tensor_copy(k_fir[rows, :, 32 * q:32 * q + 32],
                                            tk_ps[1][rows, 0:L5 * 32].rearrange("p (d c) -> p d c", d=L5)), "k_kept")
            R5.wait(dve, "k_kept", i, 4)
            R5.up(nc.vector.scalar_tensor_tensor(out=k_fir[:, 0, :], in0=ident[:, :], scalar=col_at("o_D", i),
                                                 in1=k_fir[:, 0, :], op0=ALU.mult, op1=ALU.add), "k_kept")

        def states_pe(pe, i, s):
            R5.wait(pe, "g", i, 4)
            R5.wait(pe, "u", i)
            R5.wait(pe, "rin", i, 6, back=1)
            for tau in range(L5):
                for part in range(2):
                    for q in range(4):
                        rows = slice(32 * q, 32 * q + 32)
                        last = nc.tensor.matmul(f_ps[:, q, 0, part * N5:(part + 1) * N5], g_in[rows, L5 - 1 - tau, part, :],
                                                u_now[rows, s, tau, :], start=tau == 0 and part == 0,
                                                stop=tau == L5 - 1, skip_group_check=True)
            R5.up(last, "f")
            R5.wait(pe, "k_kept", i, 5)
            R5.wait(pe, "out", i, 1, back=1)
            for j in range(L5):
                for tau in range(j + 1):
                    last = nc.tensor.matmul(y_ps[:, j, :], k_fir[:, j - tau, :], u_now[:, s, tau, :],
                                            start=tau == 0 and j % 4 == 0, stop=False, skip_group_check=True)
            R5.up(last, "fir")

        def output_pe(pe, i, s):
            R5.wait(pe, "rout", i, 6)
            for j in range(L5):
                for part in range(2):
                    for q in range(4):
                        last = nc.tensor.matmul(y_ps[32 * q:32 * q + 32, j, :],
                                                hx[:, s, part, j + 1, q, :, :].rearrange("p g c -> p (g c)"),
                                                s_prev[:, s, part, q, :], start=False, stop=part == 1,
                                                skip_group_check=True)
            R5.up(last, "y")

        def output_act(act, i, s):
            act.wait_ge(s5_clear, 5)
            R5.wait(act, "y", i)
            R5.up(nc.scalar.activation(u_s5[:, bass.ds(i, 1), :].rearrange("p a (n j) -> p (a j) n", j=L5),
                                       y_ps[:, :, :], ACT.Gelu_apprx_tanh), "out")

        def scan_dve(dve, i, s):
            c_i, s_i = (rot[:, k, bass.ds(i * 4, 4), :] for k in range(2))
            R5.up(nc.vector.tensor_tensor(keep8[:, :, :], first0[:, :, :],
                                          decay8[:, bass.ds(i * 4, 4)].unsqueeze(2).to_broadcast([P, 4, N5]), ALU.mult), "keep8")
            R5.wait(dve, "f", i)

            f_re, f_im = (f_ps[:, :, 0, part * N5:(part + 1) * N5] for part in range(2))
            x, y = f_hat[:, 0, :, :], f_hat[:, 1, :, :]
            xt, yt = r_tmp[:, 0, :, :], r_tmp[:, 1, :, :]
            R5.wait(dve, "rout", i, 6, back=1)
            for o, a, t in ((x, f_re, c_i), (y, f_im, c_i), (xt, f_im, s_i), (yt, f_re, s_i)):
                R5.up(nc.vector.tensor_tensor(o, a, t, ALU.mult), "rin")
            R5.wait(dve, "rin", i, 3)
            R5.up(nc.vector.tensor_tensor(x, x, xt, ALU.add), "rin")
            R5.wait(dve, "rin", i, 4)
            R5.up(nc.vector.tensor_tensor(y, y, yt, ALU.subtract), "rin")
            R5.wait(dve, "keep8", i)
            for part in range(2):
                R5.wait(dve, "rin", i, 5 + part)
                R5.up(nc.vector.tensor_tensor_scan(
                    s_hat[:, part, :, :].rearrange("p q n -> p (q n)"), keep8[:, :, :].rearrange("p q n -> p (q n)"),
                    f_hat[:, part, :, :].rearrange("p q n -> p (q n)"), 0.0, ALU.mult, ALU.add), "scan")
            R5.wait(dve, "scan", i, 2)
            R5.wait(dve, "y", i, 1, back=2)
            past = slice(0, N5 - 1)
            sx, sy = s_hat[:, 0, :, past], s_hat[:, 1, :, past]
            px, py = s_prev[:, s, 0, :, 1:N5], s_prev[:, s, 1, :, 1:N5]
            for o, a, t in ((px, sx, c_i), (py, sy, c_i), (xt[:, :, past], sy, s_i), (yt[:, :, past], sx, s_i)):
                R5.up(nc.vector.tensor_tensor(o, a, t[:, :, past], ALU.mult), "rout")
            R5.wait(dve, "rout", i, 4)
            R5.up(nc.vector.tensor_tensor(px, px, xt[:, :, past], ALU.subtract), "rout")
            R5.up(nc.vector.tensor_tensor(py, py, yt[:, :, past], ALU.add), "rout")

        def pipelined(eng, before, work, after):
            def step(i, s, more):
                if work:
                    work(eng, i, s)
                if more:
                    before(eng, i + 1, 1 - s)
                if after:
                    after(eng, i, s)
            before(eng, 0, 0)
            with eng.Fori(0, DT // 2 - 1) as n:
                for s in range(2):
                    step(n * 2 + s, s, True)
            step(DT - 2, 0, True)
            step(DT - 1, 1, False)

        with nc.Block() as block:
            @block.gpsimd
            def _(pool):
                R5.start(pool, "pool")
                pool.memset(gx[:, :, :, :, :, :], 0.0).then_inc(s5_clear, 1)
                pool.memset(hx[:, :, :, :, :, :, :], 0.0).then_inc(s5_clear, 1)
                pool.wait_ge(s5_clear, 5)
                with pool.Fori(0, DT // 2) as n:
                    for s in range(2):
                        make_pool(pool, n * 2 + s, s)

            @block.vector
            def _(dve):
                R5.start(dve, "dve")
                nc.vector.memset(k_fir[:, :, :], 0.0).then_inc(s5_clear, 1)
                nc.vector.memset(first0[:, :, :], 1.0).then_inc(s5_clear, 1)
                nc.vector.memset(s_prev[:, :, :, :, 0:1], 0.0).then_inc(s5_clear, 1)
                dve.wait_ge(s5_clear, 5)
                nc.vector.memset(first0[:, :, 0:1], 0.0).then_inc(s5_clear, 1)
                dve.wait_ge(s5_clear, 6)
                pipelined(dve, k_dve, scan_dve, None)

            @block.tensor
            def _(pe):
                R5.start(pe, "pe")
                pipelined(pe, turn_pe, states_pe, output_pe)

            @block.scalar
            def _(act):
                R5.start(act, "act")
                pipelined(act, turn_act, None, output_act)


    with ExitStack() as sc:
        y_hi = sb(sc, "yg_hi", [P, DT, SEQ], F32R)
        y_lo = sb(sc, "yg_lo", [P, DT, SEQ], F32R)
        sig = sb(sc, "glu_sig", [P, 2, SEQ])
        dn = Dense(sc, "g")
        w_glu = io["o_w_glu"].rearrange("a (k p) n -> (a p) k n", p=P)
        yg_hi_done, yg_lo_done, glu_sig, glu_mul, glu_out = (
            sem(n) for n in ("yg_hi_done", "yg_lo_done", "glu_sig_done", "glu_mul", "glu_out"))
        q0, u0 = Dense.q // 2, Dense.u
        with nc.Block() as block:
            def cols(i, half):
                return bass.ds((i + (1 - half) * DT) * P, P)

            @block.sync
            def _(sp):
                with sp.Fori(0, DT) as i:
                    for half in range(2):
                        dn.load(sp, w_glu, DT, cols(i, half), i * 2 + (q0 + half), 0)

            @block.gpsimd
            def _(pool):
                with pool.Fori(0, DT) as i:
                    for half in range(2):
                        dn.take_lo(pool, DT, i * 2 + (q0 + half), 0)

            @block.scalar
            def _(act):
                for k in range(DT):
                    nc.scalar.copy(y_hi[:, k, :], u_s5[:, k, :]).then_inc(yg_hi_done, 1)
                with act.Fori(0, DT) as i:
                    for half in range(2):
                        dn.take_hi(act, DT, i * 2 + (q0 + half), 0)
                    dn.wait_unit(act, i * 2 + q0, 1)
                    act.wait_ge(glu_out, i + 1)
                    nc.scalar.activation(sig[:, 0, :], dn.acc[0][:, :], ACT.Sigmoid).then_inc(unit_free, 1)

            @block.tensor
            def _(pe):
                pe.wait_ge(yg_lo_done, DT)
                with pe.Fori(0, DT) as i:
                    for half in range(2):
                        dn.product(pe, DT, y_hi, y_lo, i * 2 + (u0 + half), half, i * 2 + (q0 + half), 0)

            @block.vector
            def _(dve):
                for k in range(DT):
                    dve.wait_ge(yg_hi_done, k + 1)
                    nc.vector.tensor_tensor(y_lo[:, k, :], u_s5[:, k, :], y_hi[:, k, :].bitcast(F32),
                                            ALU.subtract).then_inc(yg_lo_done, 1)
                dve.sem_inc(glu_out, 1)
                with dve.Fori(0, DT) as i:
                    dn.wait_unit(dve, i * 2 + (q0 + 1), 1)
                    dve.wait_ge(unit_free, i * 2 + (u0 + 3))
                    nc.vector.tensor_tensor(sig[:, 1, :], sig[:, 0, :], dn.acc[1][:, :], ALU.mult).then_inc(unit_free, 1)
                    dve.wait_ge(unit_free, i * 2 + (u0 + 4))
                    here = x_res[:, bass.ds(i, 1), :]
                    nc.vector.tensor_tensor(here, here, sig[:, 1, :], ALU.add).then_inc(glu_out, 1)
        Dense.q += 4 * DT
        Dense.u += 2 * DT
    s5.close()

    conv_ffn(1)

    norm("out", "final_norm_g", 0, None, None)
    with ExitStack() as sc:
        chan = sb(sc, "chan", [P, 2, SEQ])
        rows = sb(sc, "out_rows", [P, 2, SEQ])
        turned = [ps(sc, f"out_ps{s}", [P, SEQ]) for s in range(2)]
        o_copied, o_turned, o_kept = sem("o_copied"), sem("o_turned"), sem("o_kept")
        o_stored = [sem("o_stored0"), sem("o_stored1")]
        out_v = out.rearrange("b (k t) c -> (b t) k c", t=P)
        with nc.Block() as block:
            @block.scalar
            def _(act):
                act.sem_inc(o_copied, 1)
                with act.Fori(0, DT // 2) as n:
                    for s in range(2):
                        act.wait_ge(o_turned, n * 2 + (s + 1))
                        nc.scalar.copy(chan[:, s, :], x_res[:, bass.ds(n * 2 + s, 1), :]).then_inc(o_copied, 1)

            @block.tensor
            def _(pe):
                pe.sem_inc(o_turned, 2)
                with pe.Fori(0, DT // 2) as n:
                    for s in range(2):
                        pe.wait_ge(o_copied, n * 2 + (s + 2))
                        pe.wait_ge(o_kept, n * 2 + (s + 1))
                        for k in range(SEQ // P):
                            last = nc.tensor.transpose(turned[s][:, k * P:(k + 1) * P], chan[:, s, k * P:(k + 1) * P], ident[:, :])
                        last.then_inc(o_turned, 1)

            @block.vector
            def _(dve):
                dve.sem_inc(o_kept, 2)
                with dve.Fori(0, DT // 2) as n:
                    for s in range(2):
                        dve.wait_ge(o_turned, n * 2 + (s + 3))
                        dve.wait_ge(o_stored[s], n * 16 + 16)
                        nc.vector.tensor_copy(rows[:, s, :], turned[s][:, :]).then_inc(o_kept, 1)

            @block.sync
            def _(sp):
                for s in range(2):
                    sp.sem_inc(o_stored[s], 16)
                with sp.Fori(0, DT // 2) as n:
                    for s in range(2):
                        sp.wait_ge(o_kept, n * 2 + (s + 3))
                        sp.dma_start(out_v[:, :, bass.ds(n * (2 * P) + s * P, P)],
                                     rows[:, s, :].rearrange("p (k c) -> p k c", c=P)).then_inc(o_stored[s], 16)
                for s in range(2):
                    sp.wait_ge(o_stored[s], 16 + 16 * (DT // 2))
    ctx.close()


INPUTS = ["x", "e_norm_g", "e_w_in", "e_mu", "e_w0", "e_w2", "e_a0", "e_a2", "e_g2", "e_k_k", "e_k_a", "e_r_k",
          "e_ln_w", "e_ln_b", "e_conv_w", "e_conv_b", "e_gate_a_w", "e_gate_a_b", "e_gate_x_w", "e_gate_x_b",
          "e_lru_lambda", "e_w_out", "o_norm_g", "o_w_in", "o_A_re", "o_A_im", "o_log_dt", "o_B_re", "o_B_im",
          "o_C_re", "o_C_im", "o_D", "o_w_glu", "f_norm_g", "f_w_up", "f_conv_w", "f_conv_b", "f_w_down",
          "final_norm_g"]


def kernel(**inputs):
    import numpy as np
    import concourse.bacc as bacc
    from concourse.bass_utils import run_bass_kernel_spmd

    nc = bacc.Bacc("TRN2", target_bir_lowering=False, num_devices=1)
    arrays = {f"in_{n}": np.ascontiguousarray(inputs[n]) for n in INPUTS}
    io = {n: nc.dram_tensor(f"in_{n}", arrays[f"in_{n}"].shape, F32, kind="ExternalInput").ap() for n in INPUTS}
    out = nc.dram_tensor("out_0", (1, SEQ, D_MODEL), F32, kind="ExternalOutput").ap()
    trunk(nc, io, out)
    result = run_bass_kernel_spmd(nc, [arrays], core_ids=[0])
    return result.results[0]["out_0"]
```

```python
from contextlib import ExitStack

import concourse.bass as bass
from concourse import mybir

F32 = mybir.dt.float32
F32R = mybir.dt.float32r
ALU = mybir.AluOpType
ACT = mybir.ActivationFunctionType

P = 128
D_MODEL = 1024
SEQ = 1024
HALF = 512
DT = D_MODEL // P
RW = 512
RT = RW // P
HEAD = 64
HEADS = RW // HEAD
D_FF = 2816
FT = D_FF // P
FGROUP = FT // 2
NORM_EPS = 1e-6
GN_EPS = 64e-5
LRU_C = 8.0
EXP_MINUS_HALF = 0.6065306597126334
CH = 128
NCH = SEQ // CH
L5 = 8
N5 = SEQ // L5
S5_PAIRS = 32

ROWS0 = [("e_mu", 14), ("e_w0", 4), ("e_a0", 4), ("e_k_k", 4), ("e_k_a", 4), ("e_r_k", 4),
         ("e_ln_w", 4), ("e_ln_b", 4), ("e_conv_w", 16), ("e_conv_b", 4), ("e_gate_a_b", 4),
         ("e_gate_x_b", 4), ("e_lru_lambda", 4), ("e_norm_g", 8), ("o_norm_g", 8),
         ("f_norm_g", 16), ("final_norm_g", 8), ("o_D", 8)]
COL = {}
_at = 0
for _name, _rows in ROWS0:
    COL[_name] = _at
    _at += _rows
ROWS0_USED = _at
COL["f_conv_w"] = P
COL["f_conv_b"] = P + 2 * 3 * 2 * FT
PCOLS = COL["f_conv_b"] + 2 * 2 * FT


def flat(ap):
    names = "abcdef"[:len(ap.shape)]
    return ap.rearrange(f"{' '.join(names)} -> ({' '.join(names)})")


def trunk(nc, io, out):
    ctx = ExitStack()
    sems = {}

    def sem(name):
        if name not in sems:
            sems[name] = ctx.enter_context(nc.semaphore(name))
        return sems[name]

    def sb(scope, name, shape, dt=F32):
        return scope.enter_context(nc.sbuf_tensor(name, shape, dt))

    def ps(scope, name, shape):
        return scope.enter_context(nc.psum_tensor(name, shape, F32))

    class Link:

        def __init__(self, eng, name):
            self.eng, self.sem, self.n, self.loop = eng, sem(name), totals.get(name, 0), 0
            self.name = name

        def did(self, ins):
            ins.then_inc(self.sem, 1)
            self.n += 1

        def wait(self):
            self.eng.wait_ge(self.sem, self.loop + self.n)

        def run(self, ins):
            self.did(ins)
            self.wait()

        def enter(self, i, per):
            self.loop, self.start, self.per = i * per, self.n, per

        def leave(self, times):
            assert self.n - self.start == self.per, (self.name, self.n - self.start)
            self.loop, self.n = 0, self.start + self.per * times

        def close(self):
            totals[self.name] = self.n

    totals = {}

    class Rounds:

        def __init__(self, tag, raises):
            self.tag, self.raises = tag, raises
            self.per = {n: k for own in raises.values() for n, k in own.items()}

        def start(self, eng, own):
            for n, k in self.raises[own].items():
                eng.sem_inc(sem(f"{self.tag}_{n}"), 2 * k)

        def wait(self, eng, name, i, k=1, back=0):
            eng.wait_ge(sem(f"{self.tag}_{name}"), i * self.per[name] + ((2 - back) * self.per[name] + k))

        def up(self, ins, name):
            ins.then_inc(sem(f"{self.tag}_{name}"), 1)

    x_res = sb(ctx, "x_res", [P, DT, SEQ])
    prm = sb(ctx, "prm", [P, 4 * P])
    ident = sb(ctx, "ident", [P, P])
    pick = sb(ctx, "pick", [P, 2 * DT - 1])
    ones_row = sb(ctx, "ones_row", [SEQ // P, P])
    norm_eps = sb(ctx, "norm_eps", [P, 1])

    def col(name, k=0):
        return prm[:, COL[name] + k:COL[name] + k + 1]

    def col_at(name, k):
        return prm[:, bass.ds(k + COL[name], 1)]

    with ExitStack() as sc:
        rows = sb(sc, "param_rows", [P, 4, P])
        stage = sb(sc, "x_stage", [P, 2, D_MODEL])
        turned = [ps(sc, f"turned{s}", [P, 2 * HALF]) for s in range(2)]
        turned_prm = ps(sc, "turned_prm", [P, 4, P])
        x_loaded = [sem("x_loaded0"), sem("x_loaded1")]
        prm_loaded, rows_clear, ident_ready = sem("prm_loaded"), sem("rows_clear"), sem("ident_ready")
        x_turned, x_kept, prm_turned = sem("x_turned"), sem("x_kept"), sem("prm_turned")
        n_prm = len(ROWS0) + 4
        x_rows = io["x"].rearrange("b (n t) d -> (b n) t d", t=P)
        with nc.Block() as block:
            @block.sync
            def _(sp):
                for s in range(2):
                    sp.dma_start(stage[:, s, :], x_rows[s, :, :]).then_inc(x_loaded[s], 16)
                with sp.Fori(1, SEQ // P // 2) as i:
                    for s in range(2):
                        sp.wait_ge(x_turned, i * 2 + s - 1)
                        sp.dma_start(stage[:, s, :], x_rows[bass.ds(i * 2 + s, 1), :, :]).then_inc(x_loaded[s], 16)

            @block.gpsimd
            def _(pool):
                pool.memset(ident[:, :], 0.0).then_inc(ident_ready, 1)
                pool.memset(rows[:, 0, :], 0.0).then_inc(rows_clear, 1)
                pool.memset(rows[:, 3, :], 0.0).then_inc(rows_clear, 1)
                pool.wait_ge(ident_ready, 1)
                pool.affine_select(out=ident[:, :], in_=ident[:, :], compare_op=ALU.not_equal, fill=1.0,
                                   base=0, pattern=[[-1, P]], channel_multiplier=1).then_inc(ident_ready, 1)

            @block.scalar
            def _(act):
                act.wait_ge(rows_clear, 2)
                for name, n in ROWS0:
                    act.dma_start(rows[COL[name]:COL[name] + n, 0, :],
                                  flat(io[name]).rearrange("(r p) -> r p", p=P)).then_inc(prm_loaded, 16)
                taps = flat(io["f_conv_w"]).rearrange("(r p) -> r p", p=P)
                for k in range(3):
                    n = min(P, taps.shape[0] - k * P)
                    act.dma_start(rows[0:n, 1 + k, :], taps[k * P:k * P + n, :]).then_inc(prm_loaded, 16)
                bias = flat(io["f_conv_b"]).rearrange("(r p) -> r p", p=P)
                at = COL["f_conv_b"] - 3 * P
                act.dma_start(rows[at:at + bias.shape[0], 3, :], bias).then_inc(prm_loaded, 16)
                act.wait_ge(prm_turned, 1)
                act.copy(prm[:, :], turned_prm[:, :, :]).then_inc(sem("prm_ready"), 1)

            @block.tensor
            def _(pe):
                pe.wait_ge(ident_ready, 2)
                with pe.Fori(0, SEQ // P // 2) as i:
                    for s in range(2):
                        pe.wait_ge(x_loaded[s], i * 16 + 16)
                        pe.wait_ge(x_kept, i * 2 + s + 1)
                        for c in range(DT):
                            last = nc.tensor.transpose(turned[s][:, c * P:(c + 1) * P],
                                                       stage[:, s, c * P:(c + 1) * P], ident[:, :])
                        last.then_inc(x_turned, 1)
                pe.wait_ge(prm_loaded, 16 * n_prm)
                for k in range(4):
                    last = nc.tensor.transpose(turned_prm[:, k, :], rows[:, k, :], ident[:, :])
                last.then_inc(prm_turned, 1)

            @block.vector
            def _(dve):
                dve.sem_inc(x_kept, 2)
                nc.vector.memset(pick[:, :], 0.0).then_inc(sem("norm_consts"), 1)
                nc.vector.memset(ones_row[:, :], 1.0).then_inc(sem("norm_consts"), 1)
                nc.vector.memset(norm_eps[:, :], NORM_EPS).then_inc(sem("norm_consts"), 1)
                dve.wait_ge(sem("norm_consts"), 3)
                nc.vector.memset(pick[:, DT - 1:DT], 1.0).then_inc(sem("norm_consts"), 1)
                with dve.Fori(0, SEQ // P // 2) as i:
                    for s in range(2):
                        dve.wait_ge(x_turned, i * 2 + s + 1)
                        nc.vector.tensor_copy(x_res[:, :, bass.ds(i * (2 * P) + s * P, P)],
                                              turned[s][:, :].rearrange("p (c t) -> p c t", c=DT)).then_inc(x_kept, 1)

    TB = SEQ // P
    n_squared, n_added, n_summed, n_root, n_inv, n_spread, n_wide, n_scaled, n_hi, n_lo_even, n_lo_odd = (
        sem("n_" + n) for n in "squared added summed root inv spread wide scaled hi lo_even lo_odd".split())

    class Norm:

        count = 0

        def __init__(self, sc, tag, g_name, g_at, scratch, xn_hi=None, xn_lo=None):
            self.g_name, self.g_at, self.hi, self.lo = g_name, g_at, xn_hi, xn_lo
            if scratch is not None:
                self.use(scratch)
            self.rstd_rows = sb(sc, f"rstd_rows_{tag}", [TB, P])
            self.sums = ps(sc, f"sums_{tag}", [TB, P])
            self.rstd = ps(sc, f"rstd_{tag}", [P, SEQ])
            self.n = Norm.count
            Norm.count += 1

        def use(self, scratch):
            self.sq, self.xn = scratch[:, 0:4, :], scratch[:, 4:8, :]

        def squares_act(self, act):
            for c in range(DT):
                if c >= 4:
                    act.wait_ge(n_summed, self.n * 4 + c // 2 - 1)
                nc.scalar.activation(self.sq[:, c % 4, :], x_res[:, c, :], ACT.Square).then_inc(n_squared, 1)

        def root_act(self, act):
            act.wait_ge(n_summed, self.n * 4 + 4)
            nc.scalar.activation(self.rstd_rows[:, :], self.sums[:, :], ACT.Sqrt, scale=1.0 / D_MODEL,
                                 bias=norm_eps[0:TB, 0:1]).then_inc(n_root, 1)

        def hi_act(self, act):
            for c in range(DT):
                act.wait_ge(n_scaled, self.n * DT + c + 1)
                nc.scalar.copy(self.hi[:, c, :], self.xn[:, c % 4, :]).then_inc(n_hi, 1)

        def sums_dve(self, dve):
            for j in range(4):
                at = 2 * (j % 2)
                dve.wait_ge(n_squared, self.n * DT + 2 * j + 2)
                nc.vector.tensor_tensor(self.sq[:, at, :], self.sq[:, at, :], self.sq[:, at + 1, :],
                                        ALU.add).then_inc(n_added, 1)
            dve.wait_ge(n_root, self.n + 1)
            nc.vector.reciprocal(self.rstd_rows[:, :], self.rstd_rows[:, :]).then_inc(n_inv, 1)
            dve.wait_ge(n_inv, self.n + 1)
            shape = [TB, TB, P]
            nc.vector.tensor_tensor(self.sq[0:TB, 0, :].rearrange("b (k t) -> b k t", t=P),
                                    self.rstd_rows[:, :].unsqueeze(1).to_broadcast(shape),
                                    ident[0:TB, 0:TB].unsqueeze(2).to_broadcast(shape), ALU.mult).then_inc(n_spread, 1)
            dve.wait_ge(n_wide, self.n + 1)

        def scaled_dve(self, src, dst, g):
            nc.vector.scalar_tensor_tensor(out=dst, in0=src, scalar=g, in1=self.rstd[:, :],
                                           op0=ALU.mult, op1=ALU.mult).then_inc(n_scaled, 1)

        def parts_dve(self, dve):
            def lo(c):
                dve.wait_ge(n_hi, self.n * DT + c + 1)
                nc.vector.tensor_tensor(self.lo[:, c, :], self.xn[:, c % 4, :], self.hi[:, c, :].bitcast(F32),
                                        ALU.subtract).then_inc(n_lo_even, 1)

            for c in range(DT):
                if c >= 4 and c % 2 == 0:
                    dve.wait_ge(n_lo_even, self.n * 4 + c // 2 - 1)
                elif c >= 4:
                    dve.wait_ge(n_lo_odd, self.n * 4 + c // 2 - 1)
                self.scaled_dve(x_res[:, c, :], self.xn[:, c % 4, :], col(self.g_name, self.g_at + c))
                if c % 2 == 1:
                    lo(c - 1)

        def lo_pool(self, pool):
            for c in range(1, DT, 2):
                pool.wait_ge(n_hi, self.n * DT + c + 1)
                pool.tensor_tensor(self.lo[:, c, :], self.xn[:, c % 4, :], self.hi[:, c, :].bitcast(F32),
                                   op=ALU.subtract).then_inc(n_lo_odd, 1)

        def sums_pe(self, pe):
            pe.wait_ge(sem("norm_consts"), 4)
            for j in range(4):
                pe.wait_ge(n_added, self.n * 4 + j + 1)
                for b in range(TB):
                    last = nc.tensor.matmul(self.sums[:, :], pick[:, DT - 1 - b:2 * DT - 1 - b],
                                            self.sq[:, 2 * (j % 2), b * P:(b + 1) * P],
                                            start=j == 0 and b == 0, stop=j == 3 and b == TB - 1)
                last.then_inc(n_summed, 1)
            pe.wait_ge(n_spread, self.n + 1)
            for h in range(2):
                last = nc.tensor.matmul(self.rstd[:, h * HALF:(h + 1) * HALF], ones_row[:, :],
                                        self.sq[0:TB, 0, h * HALF:(h + 1) * HALF], start=True, stop=True)
            last.then_inc(n_wide, 1)

        def wait_tile(self, pe, k):
            sem_, n = (n_lo_odd, k // 2 + 1) if k % 2 else (n_lo_even, k // 2 + 1)
            pe.wait_ge(sem_, self.n * 4 + n)

    w_loaded = [sem("w_loaded0"), sem("w_loaded1")]
    w_hi_done, w_lo_done, w_used = sem("w_hi_done"), sem("w_lo_done"), sem("w_used")
    unit_free = sem("unit_free")
    KC = 4

    class Dense:

        q = 0
        u = 0

        def __init__(self, sc, tag):
            self.raw = sb(sc, f"w_raw_{tag}", [P, 2, KC, P])
            self.hi = sb(sc, f"w_hi_{tag}", [P, 2, KC, P], F32R)
            self.lo = sb(sc, f"w_lo_{tag}", [P, 2, KC, P], F32R)
            self.acc = [ps(sc, f"acc{s}_{tag}", [P, SEQ]) for s in range(2)]

        @staticmethod
        def chunks(kt):
            return [(k, min(KC, kt - k)) for k in range(0, kt, KC)]

        def load(self, sp, w, kt, n0, pair, par):
            for k, n in self.chunks(kt):
                sp.wait_ge(w_lo_done, pair * 2 + (par + 1))
                sp.dma_start(self.raw[:, par, 0:n, :], w[:, k:k + n, n0]).then_inc(w_loaded[par], 16)
                pair, par = (pair + 1, 0) if par else (pair, 1)

        def take_hi(self, act, kt, pair, par, first=0, end=None):
            pair, par = ((pair + (first + par) // 2), (first + par) % 2) if first else (pair, par)
            for k, n in self.chunks(kt)[first:end]:
                act.wait_ge(w_loaded[par], pair * 16 + 16)
                act.wait_ge(w_used, pair * 2 + (par + 1))
                nc.scalar.copy(self.hi[:, par, 0:n, :], self.raw[:, par, 0:n, :]).then_inc(w_hi_done, 1)
                pair, par = (pair + 1, 0) if par else (pair, 1)

        def take_lo(self, pool, kt, pair, par):
            for k, n in self.chunks(kt):
                pool.wait_ge(w_hi_done, pair * 2 + (par + 1))
                pool.tensor_tensor(self.lo[:, par, 0:n, :], self.raw[:, par, 0:n, :],
                                   self.hi[:, par, 0:n, :].bitcast(F32), op=ALU.subtract).then_inc(w_lo_done, 1)
                pair, par = (pair + 1, 0) if par else (pair, 1)

        @staticmethod
        def wait_unit(eng, pair, par):
            eng.wait_ge(w_used, pair * 2 + (par + 3))

        def product(self, pe, kt, in_hi, in_lo, unit, slot, pair, par, wait_tile=None):
            pe.wait_ge(unit_free, unit + 1)
            acc = self.acc[slot]
            for k, n in self.chunks(kt):
                pe.wait_ge(w_lo_done, pair * 2 + (par + 3))
                for j in range(n):
                    if wait_tile:
                        wait_tile(pe, k + j)
                    for w, x in ((self.hi, in_hi), (self.hi, in_lo), (self.lo, in_hi)):
                        first = k + j == 0 and w is self.hi and x is in_hi
                        final = k + j == kt - 1 and w is self.lo
                        for h in range(2):
                            last = nc.tensor.matmul(acc[:, h * HALF:(h + 1) * HALF], w[:, par, j, :],
                                                    x[:, k + j, h * HALF:(h + 1) * HALF], start=first, stop=final)
                last.then_inc(w_used, 1)
                pair, par = (pair + 1, 0) if par else (pair, 1)

    def dense_credit_pool(pool):
        pool.sem_inc(w_lo_done, 2)

    def dense_credit_pe(pe):
        pe.sem_inc(w_used, 2)

    def dense_credit_dve(dve):
        dve.sem_inc(unit_free, 2)


    proj = ctx.enter_context(ExitStack())
    EV = 22
    p_even = sb(proj, "p_even", [P, EV, SEQ])
    w_in = io["e_w_in"].rearrange("a (k p) n -> (a p) k n", p=P)
    with ExitStack() as sc:
        xn_hi = sb(sc, "xn_hi_e", [P, DT, SEQ], F32R)
        xn_lo = sb(sc, "xn_lo_e", [P, DT, SEQ], F32R)
        nm = Norm(sc, "e", "e_norm_g", 0, p_even[:, 14:22, :], xn_hi, xn_lo)
        dn = Dense(sc, "e")
        start_scale = sb(sc, "start_scale", [P, EV])
        start_bias = sb(sc, "start_bias", [P, EV])
        tables, started, spent = sem("e_tables"), sem("e_started"), sem("e_spent")
        with nc.Block() as block:
            @block.sync
            def _(sp):
                with sp.Fori(0, EV // 2) as i:
                    for s in range(2):
                        dn.load(sp, w_in, DT, bass.ds(i * (2 * P) + s * P, P), i * 2 + s, 0)

            @block.gpsimd
            def _(pool):
                dense_credit_pool(pool)
                dn.take_lo(pool, DT, 0, 0)
                nm.lo_pool(pool)
                dn.take_lo(pool, DT, 1, 0)
                with pool.Fori(1, EV // 2) as i:
                    for s in range(2):
                        dn.take_lo(pool, DT, i * 2 + s, 0)

            @block.tensor
            def _(pe):
                dense_credit_pe(pe)
                nm.sums_pe(pe)
                with pe.Fori(0, EV // 2) as i:
                    for s in range(2):
                        dn.product(pe, DT, xn_hi, xn_lo, i * 2 + s, s, i * 2 + s, 0, nm.wait_tile)

            @block.scalar
            def _(act):
                def start_unit(u, slot):
                    act.wait_ge(w_used, u * 2 + 4)
                    nc.scalar.activation(p_even[:, bass.ds(u, 1), :], dn.acc[slot][:, :], ACT.Identity,
                                         scale=start_scale[:, bass.ds(u, 1)],
                                         bias=start_bias[:, bass.ds(u, 1)]).then_inc(started, 1)

                nm.squares_act(act)
                act.wait_ge(tables, 6)
                dn.take_hi(act, DT, 0, 0)
                nm.root_act(act)
                nm.hi_act(act)
                dn.take_hi(act, DT, 1, 0)
                start_unit(0, 0)
                with act.Fori(1, EV // 2) as i:
                    for s in range(2):
                        dn.take_hi(act, DT, i * 2 + s, 0)
                        start_unit(i * 2 + (s - 1), 1 - s)
                start_unit(EV - 1, 1)

            @block.vector
            def _(dve):
                dense_credit_dve(dve)
                nc.vector.tensor_scalar(start_scale[:, 0:14], prm[:, COL["e_mu"]:COL["e_mu"] + 14],
                                        -1.0, 1.0, ALU.mult, ALU.add).then_inc(tables, 1)
                nc.vector.tensor_copy(start_scale[:, 14:18],
                                      prm[:, COL["e_conv_w"] + 12:COL["e_conv_w"] + 16]).then_inc(tables, 1)
                nc.vector.memset(start_scale[:, 18:22], 1.0).then_inc(tables, 1)
                nc.vector.memset(start_bias[:, 0:14], 0.0).then_inc(tables, 1)
                nc.vector.tensor_copy(start_bias[:, 14:18],
                                      prm[:, COL["e_conv_b"]:COL["e_conv_b"] + 4]).then_inc(tables, 1)
                nc.vector.memset(start_bias[:, 18:22], 0.0).then_inc(tables, 1)
                nm.sums_dve(dve)
                nm.parts_dve(dve)

                def tap(u, slot, scale, back):
                    here = p_even[:, bass.ds(u, 1), back:SEQ]
                    return nc.vector.scalar_tensor_tensor(out=here, in0=dn.acc[slot][:, 0:SEQ - back],
                                                          scalar=scale, in1=here, op0=ALU.mult, op1=ALU.add)

                with dve.Fori(0, 7) as i:
                    for s in range(2):
                        dve.wait_ge(started, i * 2 + s + 1)
                        tap(i * 2 + s, s, col_at("e_mu", i * 2 + s), 1).then_inc(unit_free, 1)
                with dve.Fori(0, 2) as i:
                    for s in range(2):
                        dve.wait_ge(started, i * 2 + (s + 15))
                        for back in (1, 2, 3):
                            ins = tap(i * 2 + (s + 14), s, col_at("e_conv_w", i * 2 + (s + 4 * (3 - back))), back)
                            if back < 3:
                                ins.then_inc(spent, 1)
                                dve.wait_ge(spent, i * 4 + (2 * s + back))
                        ins.then_inc(unit_free, 1)
                dve.wait_ge(unit_free, 2 + 18)
                with dve.Fori(18, EV) as i:
                    dve.wait_ge(started, i + 1)
                    dve.sem_inc(unit_free, 1)

    LEVELS = 7
    level_mask = sb(proj, "level_mask", [P, LEVELS, P])
    causal = sb(proj, "causal", [P, 2, P])
    head_ones = sb(proj, "head_ones", [P, P])
    centre = sb(proj, "centre", [P, P])
    scratch_w = p_even[:, 18:22, :]

    with ExitStack() as sc:
        gw = sb(sc, "gw", [P, 2, 4, P])
        same_block = sb(sc, "same_block", [P, LEVELS + 1, P])
        decay_c = sb(sc, "decay_c", [P, 4])
        lam_abs = sb(sc, "lam_abs", [P, 4])
        z = sb(sc, "lam_z", [P, 4])
        z2 = sb(sc, "lam_z2", [P, 4])
        den = sb(sc, "lam_den", [P, 4])
        poly = sb(sc, "lam_poly", [P, 4])
        g_r = sb(sc, "g_r", [P, 2, SEQ])
        g_i = sb(sc, "g_i", [P, 2, SEQ])
        a_t = sb(sc, "a_t", [P, 2, SEQ])
        th = sb(sc, "th", [P, 2, SEQ])
        g_psum = [ps(sc, f"g_psum{k}", [P, SEQ]) for k in range(4)]
        gw_clear, gw_loaded, lam_exp, decay_ready = sem("gw_clear"), sem("gw_loaded"), sem("lam_exp"), sem("decay_ready")
        lam_ready = sem("lam_ready")
        l_gates, l_sig, l_tanh, l_exp, l_arg, l_root, l_gelu, l_out = (
            sem("l_" + n) for n in ("gates", "sig", "tanh", "exp", "arg", "root", "gelu", "out"))
        masks_pool, masks_dve, l_gated, l_h, l_sq = sem("masks_pool"), sem("masks_dve"), sem("l_gated"), sem("l_h"), sem("l_sq")
        with nc.Block() as block:
            @block.gpsimd
            def _(pool):
                link = Link(pool, "masks_pool")
                link.run(pool.memset(same_block[:, :, :], 1.0))
                for k in range(LEVELS):
                    m = same_block[:, k, :].rearrange("p (b c) -> p b c", c=1 << k)
                    link.run(pool.affine_select(out=m, in_=m, compare_op=ALU.is_ge, fill=0.0, base=0,
                                                pattern=[[-(1 << k), P >> k], [0, 1 << k]], channel_multiplier=1))
                    link.run(pool.affine_select(out=m, in_=m, compare_op=ALU.is_ge, fill=0.0, base=(1 << k) - 1,
                                                pattern=[[1 << k, P >> k], [0, 1 << k]], channel_multiplier=-1))
                link.run(pool.memset(causal[:, :, :], 1.0))
                for k in range(2):
                    link.run(pool.affine_select(out=causal[:, k, :], in_=causal[:, k, :], compare_op=ALU.is_ge, fill=0.0,
                                                base=k - 1, pattern=[[1, P]], channel_multiplier=-1))
                link.close()

            @block.sync
            def _(sp):
                sp.wait_ge(gw_clear, 1)
                for g, name in enumerate(("e_gate_a_w", "e_gate_x_w")):
                    w = io[name].rearrange("a (c h) i j -> (a h) i c j", h=2)
                    for h in range(2):
                        sp.dma_start(gw[h * HEAD:(h + 1) * HEAD, g, :, h * HEAD:(h + 1) * HEAD],
                                     w[h, :, :, :]).then_inc(gw_loaded, 16)

            @block.tensor
            def _(pe):
                pe.wait_ge(gw_loaded, 64)
                for c in range(4):
                    if c >= 2:
                        pe.wait_ge(l_sig, 2 * (c - 1))
                    for g in range(2):
                        for h in range(2):
                            last = nc.tensor.matmul(g_psum[2 * (c % 2) + g][:, h * HALF:(h + 1) * HALF], gw[:, g, c, :],
                                                    p_even[:, 14 + c, h * HALF:(h + 1) * HALF], start=True, stop=True)
                    last.then_inc(l_gates, 1)

            @block.scalar
            def _(act):
                act.wait_ge(lam_ready, 1)
                nc.scalar.activation(lam_abs[:, :], lam_abs[:, :], ACT.Exp, scale=-1.0).then_inc(lam_exp, 1)
                for c in range(4):
                    nc.scalar.activation(p_even[:, 18 + c, :], p_even[:, 18 + c, :], ACT.Gelu_apprx_tanh).then_inc(l_gelu, 1)
                act.wait_ge(decay_ready, 1)
                for p in range(2):
                    for s in range(2):
                        c = 2 * p + s
                        act.wait_ge(l_gates, c + 1)
                        if p:
                            act.wait_ge(l_out, s + 1)
                        nc.scalar.activation(g_r[:, s, :], g_psum[2 * s][:, :], ACT.Sigmoid,
                                             bias=col("e_gate_a_b", c)).then_inc(l_sig, 1)
                        nc.scalar.activation(g_i[:, s, :], g_psum[2 * s + 1][:, :], ACT.Sigmoid,
                                             bias=col("e_gate_x_b", c)).then_inc(l_sig, 1)
                        act.wait_ge(l_sig, 2 * c + 1)
                        nc.scalar.activation(th[:, s, :], g_r[:, s, :], ACT.Tanh, scale=decay_c[:, c:c + 1]).then_inc(l_tanh, 1)
                    for s in range(2):
                        act.wait_ge(l_arg, 8 * p + s + 1)
                        nc.scalar.activation(a_t[:, s, :], a_t[:, s, :], ACT.Exp).then_inc(l_exp, 1)
                    for s in range(2):
                        act.wait_ge(l_arg, 8 * p + 2 * s + 4)
                        nc.scalar.activation(th[:, s, :], th[:, s, :], ACT.Sqrt).then_inc(l_root, 1)

            @block.vector
            def _(dve):
                nc.vector.memset(gw[:, :, :, :], 0.0).then_inc(gw_clear, 1)
                lam = prm[:, COL["e_lru_lambda"]:COL["e_lru_lambda"] + 4]
                nc.vector.scalar_tensor_tensor(out=lam_abs[:, :], in0=lam, scalar=-1.0, in1=lam, op0=ALU.mult,
                                               op1=ALU.max).then_inc(lam_ready, 1)
                dve.wait_ge(lam_exp, 1)
                link = Link(dve, "masks_dve")
                link.run(nc.vector.tensor_scalar(den[:, :], lam_abs[:, :], 2.0, None, ALU.add))
                link.run(nc.vector.reciprocal(den[:, :], den[:, :]))
                link.run(nc.vector.tensor_tensor(z[:, :], lam_abs[:, :], den[:, :], ALU.mult))
                link.run(nc.vector.tensor_tensor(z2[:, :], z[:, :], z[:, :], ALU.mult))
                link.run(nc.vector.memset(poly[:, :], 1.0 / 17))
                for k in range(15, 0, -2):
                    link.run(nc.vector.tensor_tensor(poly[:, :], poly[:, :], z2[:, :], ALU.mult))
                    link.run(nc.vector.tensor_scalar(poly[:, :], poly[:, :], 1.0 / k, None, ALU.add))
                link.run(nc.vector.tensor_tensor(poly[:, :], poly[:, :], z[:, :], ALU.mult))
                link.run(nc.vector.tensor_scalar(poly[:, :], poly[:, :], 2 * LRU_C, None, ALU.mult))
                link.run(nc.vector.tensor_scalar(den[:, :], lam, -LRU_C, 0.0, ALU.mult, ALU.max))
                nc.vector.tensor_tensor(decay_c[:, :], poly[:, :], den[:, :], ALU.add).then_inc(decay_ready, 1)
                dve.wait_ge(decay_ready, 1)
                dve.wait_ge(masks_pool, 1 + 2 * LEVELS + 3)
                link.run(nc.vector.tensor_copy(head_ones[:, :], same_block[:, 6, :]))
                for k in range(LEVELS):
                    link.run(nc.vector.tensor_tensor(level_mask[:, k, :], same_block[:, k + 1, :], same_block[:, k, :], ALU.subtract))
                below = same_block[:, 0, :]
                link.run(nc.vector.tensor_scalar(below, causal[:, 1, :], -1.0, 1.0, ALU.mult, ALU.add))
                for k in range(LEVELS):
                    link.run(nc.vector.tensor_tensor(level_mask[:, k, :], level_mask[:, k, :],
                                                     below if k else causal[:, 0, :], ALU.mult))
                link.run(nc.vector.scalar_tensor_tensor(out=centre[:, :], in0=head_ones[:, :], scalar=-1.0 / HEAD,
                                                        in1=ident[:, :], op0=ALU.mult, op1=ALU.add))
                for p in range(2):
                    for s in range(2):
                        c = 2 * p + s
                        dve.wait_ge(l_sig, 2 * c + 2)
                        nc.vector.tensor_scalar(a_t[:, s, :], g_r[:, s, :], decay_c[:, c:c + 1], -1.0,
                                                ALU.mult, ALU.mult).then_inc(l_arg, 1)
                        nc.vector.tensor_tensor(g_i[:, s, :], g_i[:, s, :], p_even[:, 14 + c, :], ALU.mult).then_inc(l_gated, 1)
                    for s in range(2):
                        c = 2 * p + s
                        dve.wait_ge(l_exp, c + 1)
                        dve.wait_ge(l_tanh, c + 1)
                        nc.vector.tensor_tensor(g_r[:, s, :], a_t[:, s, :], a_t[:, s, :], ALU.mult).then_inc(l_arg, 1)
                        dve.wait_ge(l_arg, 8 * p + 2 * s + 3)
                        nc.vector.scalar_tensor_tensor(out=th[:, s, :], in0=g_r[:, s, :], scalar=1.0, in1=th[:, s, :],
                                                       op0=ALU.add, op1=ALU.mult).then_inc(l_arg, 1)
                    for s in range(2):
                        c = 2 * p + s
                        dve.wait_ge(l_gated, c + 1)
                        dve.wait_ge(l_root, c + 1)
                        nc.vector.tensor_tensor(g_i[:, s, :], g_i[:, s, :], th[:, s, :], ALU.mult).then_inc(l_arg, 1)
                        dve.wait_ge(l_arg, 8 * p + s + 7)
                        nc.vector.tensor_tensor_scan(g_r[:, s, :], a_t[:, s, :], g_i[:, s, :], 0.0, ALU.mult, ALU.add).then_inc(l_h, 1)
                        dve.wait_ge(l_h, c + 1)
                        dve.wait_ge(l_gelu, c + 1)
                        nc.vector.tensor_tensor(p_even[:, 14 + c, :], g_r[:, s, :], p_even[:, 18 + c, :], ALU.mult).then_inc(l_out, 1)
                link.close()

    with ExitStack() as sc:
        lora_w = sb(sc, "lora_w", [P, RW])
        lora_g = sb(sc, "lora_g", [P, RW])
        ones = sb(sc, "r_ones", [P, CH])
        lora_x = sb(sc, "lora_x", [P, CH])
        sig_g = sb(sc, "sig_g", [P, CH])
        names = ("decay", "logsum", "grow", "a", "kk", "ksq", "k2", "rk")
        flat_temps = p_even[:, 18:22, :].rearrange("p c t -> p (c t)")
        T = {n: flat_temps[:, HALF * k:HALF * (k + 1)].rearrange("p (i t) -> p i t", i=RT)
             for k, n in enumerate(names)}
        y_sq = T["ksq"]
        v_now = sb(sc, "v_now", [P, RT, CH])
        mid = sb(sc, "mid", [P, RT])
        norms = sb(sc, "norms", [HEADS, 2, CH])
        unscale = sb(sc, "unscale", [P, 1])
        zr = sb(sc, "zr", [P, 2, RT, 2, CH])
        k_t = sb(sc, "k_t", [P, 2, RT, CH])
        b_t = sb(sc, "b_t", [P, 2, RT, CH])
        mid_scale = sb(sc, "mid_scale", [P, 2, RT])
        end_scale = sb(sc, "end_scale", [P, 2, RT])
        by_token = sb(sc, "by_token", [P, 4, RW])
        a_b = [sb(sc, f"a_b{g}", [P, RT, 2, CH]) for g in range(2)]
        a_k = [sb(sc, f"a_k{g}", [P, RT, 2, CH]) for g in range(2)]
        a_zb = [sb(sc, f"a_zb{g}", [P, RT, CH], F32R) for g in range(2)]
        rounded = sb(sc, "rounded", [P, 6 * RT + 3, CH], F32R)
        EYE = 6 * RT + 1
        x_inv, x_inv_t, mx = ([rounded[:, 1 + (2 * k + g) * RT:1 + (2 * k + g + 1) * RT, :] for g in range(2)]
                              for k in range(3))
        eye = rounded[:, EYE, :]
        x_t = [sb(sc, f"x_t{g}", [P, RT, CH]) for g in range(2)]
        neg_eye = sb(sc, "neg_eye", [P, P], F32R)
        akv = sb(sc, "akv", [P, RW])
        sa = akv
        y_c = sb(sc, "y_c", [P, RT, CH])
        w_t = y_c
        head_in = sb(sc, "head_in", [P, RT, HEADS])
        head_out = sb(sc, "head_out", [HEADS, RT, P])
        state = sb(sc, "state", [P, RT, HEAD])
        state_mid = sb(sc, "state_mid", [P, RT, HEAD])
        prep_ps = [ps(sc, f"prep_ps{k}", [P, HALF]) for k in range(2)]
        m = [ps(sc, f"main_ps{k}", [P, SEQ]) for k in range(3)]
        banks = [(m[0][:, 0:HALF], m[0][:, HALF:SEQ], m[1][:, 0:HALF]),
                 (m[1][:, HALF:SEQ], m[2][:, 0:HALF], m[2][:, HALF:SEQ])]
        SUM_SCALE = 65536.0

        R7 = Rounds("r", {
            "act": {"lora_in": 3, "sigmoid": 2, "ksq": 1, "roots": 2, "g_kept": 1, "exps": 4, "turned_kept": 4,
                    "a_zb": 2, "x0": 7, "xt0": 6, "res0": 1, "akv": 1, "w_t": 1, "sa": 2, "y": 1, "y_sq": 2},
            "pe": {"lora": 3, "k_sum": 1, "k_wide": 1, "bonus_sum": 1, "turned": 4, "a_ps": 4, "mx_ps0": 6, "mx_ps1": 6,
                   "x_ps0": 13, "x_ps1": 13, "res_ps0": 2, "res_ps1": 2, "akv_ps": 1, "w_ps": 1, "sa_ps": 2, "s_ps": 1,
                   "y_ps": 1, "yc_ps": 1, "y_sum": 1, "y_wide": 1},
            "dve": {"biased": 2, "logsum": 4, "mids": 1, "k2": 2, "k_floor": 1, "y_floor": 1, "kk": 1, "zr": 2,
                    "ends": 1, "bonus": 1, "a_kept": 4, "first": 2, "mx0": 6, "mx1": 6, "x1": 7, "xt1": 6, "res1": 1,
                    "x_t0": 1, "x_t1": 1, "state_mid": 1, "state": 2, "gn": 1},
            "pool": {"v_now": 1, "kk_raw": 1, "centred": 2, "rk": 2, "bk": 3, "first_t": 2, "out": 4},
        })
        last_chunk = NCH - 1
        start, wait, up = R7.start, R7.wait, R7.up

        def per_channel(name):
            return prm[:, COL[name]:COL[name] + RT].unsqueeze(2).to_broadcast([P, RT, CH])

        def over_tokens(ap, n=CH):
            return ap.unsqueeze(2).to_broadcast([P, RT, n])

        def tokens(first, n, c):
            return p_even[:, first:first + n, bass.ds(c * CH, CH)]

        def tt(out_, a, b, op):
            return nc.vector.tensor_tensor(out_, a, b, op)

        def psum4(ap):
            return ap.rearrange("p (i t) -> p i t", i=RT)

        def product4(bank, lhs, rhs, begin=True, end=True):
            for i in range(RT):
                last = nc.tensor.matmul(bank[:, i * CH:(i + 1) * CH], lhs(i), rhs(i), start=begin, stop=end,
                                        skip_group_check=not (begin and end))
            return last

        def lora_pe(pe, c, k):
            if k == 0:
                wait(pe, "lora_in", c, 3)
                wait(pe, "turned_kept", c, 4, back=1)
            if k == 1:
                wait(pe, "turned_kept", c, 3, back=1)
            if k == 2:
                wait(pe, "biased", c, 1)
            w, x = ((lora_w[0:HEAD, :], lora_x[0:HEAD, :]), (lora_w[HEAD:P, :], lora_x[HEAD:P, :]),
                    (lora_g[:, :], sig_g[:, :]))[k]
            up(product4(prep_ps[k % 2], lambda i: w[:, i * P:(i + 1) * P], lambda i: x), "lora")

        def head_sums(bank, sq):
            for i in range(RT):
                last = nc.tensor.matmul(bank[0:HEADS, 0:CH], head_in[:, i, :], sq[:, i, :], start=i == 0, stop=i == RT - 1)
            return last

        def widen(bank, by_head):
            return product4(bank, lambda i: head_out[:, i, :], lambda i: by_head[:, :])

        def k_sum_pe(pe, c):
            wait(pe, "ksq", c)
            wait(pe, "biased", c, 2)
            up(head_sums(prep_ps[1], T["ksq"]), "k_sum")

        def bonus_pe(pe, c):
            wait(pe, "rk", c, 2)
            wait(pe, "g_kept", c)
            up(nc.tensor.matmul(prep_ps[0][:, :], head_ones[:, :], T["rk"], start=True, stop=True), "bonus_sum")

        def k_wide_pe(pe, c):
            wait(pe, "roots", c, 2)
            wait(pe, "gn", c, back=2)
            up(widen(prep_ps[1], norms[:, 0, :]), "k_wide")

        def centre_pe(pe, c):
            wait(pe, "y", c)
            if isinstance(c, int) and c == last_chunk:
                wait(pe, "gn", c, back=1)
            elif isinstance(c, int) and c == last_chunk - 1:
                wait(pe, "turned_kept", c + 1, 3)
            else:
                wait(pe, "k_floor", c + 2)
            up(nc.tensor.matmul(prep_ps[1][:, :], centre[:, :], y_c[:, :, :], start=True, stop=True), "yc_ps")

        def y_sum_pe(pe, c):
            wait(pe, "y_sq", c, 2)
            up(head_sums(prep_ps[1], y_sq[:, :, :]), "y_sum")

        def y_wide_pe(pe, c):
            wait(pe, "roots", c + 2, 2)
            up(widen(prep_ps[1], norms[:, 1, :]), "y_wide")

        def turn_pe(pe, c, s, n):
            src = (zr[:, s, :, 0, :], b_t[:, s, :, :], k_t[:, s, :, :], v_now[:, :, :])[n]
            if n == 0:
                wait(pe, "kk", c)
                wait(pe, "zr", c, 1)
            if n == 1:
                wait(pe, "bonus", c)
                wait(pe, "bk", c, 3)
            if n == 2:
                wait(pe, "turned_kept", c, 1)
            if n == 3:
                wait(pe, "turned_kept", c, 2)
                wait(pe, "v_now", c)
            bank = prep_ps[(n + 1) % 2]
            for i in range(RT):
                last = nc.tensor.transpose(bank[:, i * CH:(i + 1) * CH], src[:, i, :], ident[:, :])
            up(last, "turned")

        def scores_pe(pe, c, s, n):
            src, g = ((b_t, 0), (b_t, 1), (k_t, 0), (k_t, 1))[n]
            if n == 0:
                wait(pe, "zr", c, 2)
                wait(pe, "bk", c, 3)
                wait(pe, "w_t", c, back=1)
            if n == 1:
                wait(pe, "y", c, back=1)
                wait(pe, "sa", c, 2, back=1)
            if n == 2:
                wait(pe, "state", c, 1, back=1)
            if n == 3:
                wait(pe, "a_kept", c, 1)
            h = g * HEAD
            for i in range(RT):
                last = nc.tensor.matmul(m[n % 3][:, i * 2 * CH:(i + 1) * 2 * CH], src[h:h + HEAD, s, i, :],
                                        zr[h:h + HEAD, s, i, :, :], start=True, stop=True)
            up(last, "a_ps")

        def beside_zeros(bank, i, lhs, tile, **flags):
            rhs = rounded[:, tile:EYE + 2:EYE + 1 - tile, :] if i == 0 else rounded[:, 0:tile + 1:tile, :]
            at = max(i - 1, 0) * CH
            return nc.tensor.matmul(bank[:, at:at + 2 * CH], lhs, rhs, skip_group_check=True, **flags)

        def units(bank, lhs, rhs, **flags):
            return nc.tensor.matmul(bank, lhs, rhs, skip_group_check=True, **flags)

        eyes4 = eye.unsqueeze(1).to_broadcast([P, RT, CH])
        X_AT, XT_AT, MX_AT = ([1 + (2 * k + g) * RT for g in range(2)] for k in range(3))

        def level0_pe(pe, c):
            for g in range(2):
                wait(pe, "first", c, g + 1)
                wait(pe, "a_kept", c, 4 if g == 0 else 3)
                if g == 0:
                    units(banks[g][1], eye, eyes4, start=True, stop=False)
                for i in range(RT):
                    last = beside_zeros(banks[g][1], i, mx[g][:, i, :], EYE, start=g == 1 and i == 0, stop=i == RT - 1)
                up(last, f"x_ps{g}")

        def grow_pe(pe, c, k):
            for g in range(2):
                wait(pe, f"x{g}", c, k)
                if k == 1:
                    wait(pe, "a_zb", c, g + 1)
                for i in range(RT):
                    last = beside_zeros(banks[g][0], i, a_zb[g][:, i, :], X_AT[g] + i, start=i == 0, stop=i == RT - 1)
                up(last, f"mx_ps{g}")

        def add4(bank, lhs, rhs_at, old=None):
            if old is not None:
                units(bank, eye, old, start=True, stop=False)
            for i in range(RT):
                last = beside_zeros(bank, i, lhs[:, i, :], rhs_at + i, start=old is None and i == 0, stop=i == RT - 1)
            return last

        def close_pe(pe, c, k):
            for g in range(2):
                wait(pe, f"mx{g}", c, k)
                if k == 1:
                    wait(pe, "first_t", c, g + 1)
                else:
                    wait(pe, f"xt{g}", c, k - 1)
                up(add4(banks[g][1], x_inv_t[g], MX_AT[g], None if g else x_inv[g]), f"x_ps{g}")
                up(add4(banks[g][2], mx[g], XT_AT[g], None if g else x_inv_t[g]), f"x_ps{g}")

        def refine_pe(pe, c):
            for g in range(2):
                wait(pe, f"x{g}", c, LEVELS)
                units(banks[g][0], eye, eyes4, start=True, stop=False)
                units(banks[g][0], neg_eye[:, :], x_inv[g], start=False, stop=False)
                for i in range(RT):
                    last = units(banks[g][0][:, i * CH:(i + 1) * CH], a_b[g][:, i, 0, :],
                                 x_inv[g][:, i, :].bitcast(F32), start=False, stop=i == RT - 1)
                up(last, f"res_ps{g}")
            wait(pe, "akv", c, back=1)
            vt = by_token[:, 3, :]
            for h in range(HEADS):
                i, g = h // 2, h % 2
                last = nc.tensor.matmul(m[2][:, h * HEAD:(h + 1) * HEAD], a_k[g][:, i, 0, :],
                                        vt[:, h * HEAD:(h + 1) * HEAD], start=True, stop=True)
            up(last, "akv_ps")
            for g in range(2):
                wait(pe, f"res{g}", c)
                wait(pe, f"xt{g}", c, LEVELS - 1)
                up(add4(banks[g][2], mx[g], XT_AT[g]), f"res_ps{g}")

        def w_pe(pe, c):
            for g in range(2):
                wait(pe, f"x_t{g}", c)
                for i in range(RT):
                    h = 2 * i + g
                    last = nc.tensor.matmul(m[0][g * HEAD:(g + 1) * HEAD, HALF + i * CH:HALF + (i + 1) * CH],
                                            by_token[:, 0, h * HEAD:(h + 1) * HEAD], x_t[g][:, i, :],
                                            start=True, stop=True)
            up(last, "w_ps")

        def sa_pe(pe, c):
            wait(pe, "akv", c)
            wait(pe, "w_t", c)
            wait(pe, "state_mid", c)
            for g, bank in enumerate((m[1][:, 0:HALF], m[2][:, HALF:SEQ])):
                o = g * HEAD
                for i in range(RT):
                    h = 2 * i + g
                    dst = bank[:, i * HEAD:(i + 1) * HEAD]
                    nc.tensor.matmul(dst, x_t[g][:, i, :], akv[:, h * HEAD:(h + 1) * HEAD],
                                     start=True, stop=False)
                    last = nc.tensor.matmul(dst, w_t[o:o + HEAD, i, :], state_mid[o:o + HEAD, i, :],
                                            start=False, stop=True)
                up(last, "sa_ps")

        def tail_pe(pe, c, s):
            vt = by_token[:, 3, :]
            wait(pe, "sa", c, 2)
            for h in range(HEADS):
                i, g = h // 2, h % 2
                o = g * HEAD
                dst = m[2][o:o + HEAD, i * HEAD:(i + 1) * HEAD]
                cols = slice(h * HEAD, (h + 1) * HEAD)
                nc.tensor.matmul(dst, by_token[:, 1, cols], sa[:, cols], start=True, stop=False)
                last = nc.tensor.matmul(dst, by_token[:, 2, cols], vt[:, cols], start=False, stop=True)
            up(last, "s_ps")
            for h in range(HEADS):
                i, g = h // 2, h % 2
                o = g * HEAD
                dst = m[1][o:o + HEAD, HALF + i * CH:HALF + (i + 1) * CH]
                cols = slice(h * HEAD, (h + 1) * HEAD)
                nc.tensor.matmul(dst, state_mid[o:o + HEAD, i, :], zr[o:o + HEAD, s, i, 1, :], start=True, stop=False)
                nc.tensor.matmul(dst, sa[:, cols], a_b[g][:, i, 1, :], start=False, stop=False)
                last = nc.tensor.matmul(dst, vt[:, cols], a_k[g][:, i, 1, :], start=False, stop=True)
            up(last, "y_ps")

        def codes_act(act, c):
            wait(act, "lora", c, 3, back=1)
            up(nc.scalar.activation(lora_x[0:HEAD, :], p_even[0:HEAD, 12, bass.ds(c * CH, CH)], ACT.Tanh), "lora_in")
            up(nc.scalar.activation(lora_x[HEAD:P, :], p_even[HEAD:P, 12, bass.ds(c * CH, CH)], ACT.Copy), "lora_in")
            up(nc.scalar.activation(sig_g[:, :], p_even[:, 13, bass.ds(c * CH, CH)], ACT.Sigmoid), "lora_in")

        def sigmoids_act(act, c):
            wait(act, "biased", c, 1)
            up(nc.scalar.activation(T["decay"], T["decay"], ACT.Sigmoid), "sigmoid")
            wait(act, "biased", c, 2)
            up(nc.scalar.activation(T["a"], T["a"], ACT.Sigmoid), "sigmoid")

        def square_act(act, c):
            wait(act, "kk_raw", c)
            if not (isinstance(c, int) and c == 0):
                wait(act, "y_sum", c, back=3)
            up(nc.scalar.activation(T["ksq"], T["kk"], ACT.Square), "ksq")

        def gate_act(act, c):
            wait(act, "k2", c, 2)
            wait(act, "lora", c, 3)
            up(nc.scalar.activation(tokens(4, RT, c), psum4(prep_ps[0]), ACT.Copy), "g_kept")

        def exps_act(act, c, s, k):
            if k == 0:
                wait(act, "centred", c, 1)
                wait(act, "state_mid", c, back=2)
                up(nc.scalar.activation(mid_scale[:, s, :], mid[:, :], ACT.Exp, scale=-EXP_MINUS_HALF), "exps")
                up(nc.scalar.activation(T["grow"], T["logsum"], ACT.Exp, scale=EXP_MINUS_HALF), "exps")
            else:
                wait(act, "centred", c, 2)
                up(nc.scalar.activation(T["decay"], T["decay"], ACT.Exp, scale=-EXP_MINUS_HALF), "exps")
                up(nc.scalar.activation(T["logsum"], T["logsum"], ACT.Exp, scale=-EXP_MINUS_HALF), "exps")

        def roots_act(act, c, first=0, n=2):
            tile_ = norms[:, first:first + n, :]
            if first == 0:
                wait(act, "k_floor", c)
            if first + n == 2:
                wait(act, "y_floor", c, back=2)
            up(nc.scalar.activation(tile_, tile_, ACT.Ln, scale=SUM_SCALE), "roots")
            wait(act, "roots", c, 1)
            up(nc.scalar.activation(tile_, tile_, ACT.Exp, scale=-0.5, bias=unscale[0:HEADS, 0:1]), "roots")

        def centred_act(act, c, last=False):
            wait(act, "yc_ps", c)
            if not last:
                wait(act, "k_sum", c + 1)
            wait(act, "out", c, 4, back=1)
            up(nc.scalar.activation(y_c[:, :, :], psum4(prep_ps[1]), ACT.Copy), "y_sq")
            up(nc.scalar.activation(y_sq[:, :, :], psum4(prep_ps[1]), ACT.Square), "y_sq")

        def turn_act(act, c, n):
            wait(act, "turned", c, n + 1)
            wait(act, ("w_ps", "s_ps", "s_ps", "y_ps")[n], c, back=1)
            up(nc.scalar.copy(by_token[:, n, :], prep_ps[(n + 1) % 2][:, :]), "turned_kept")

        def a_zb_act(act, c):
            for g in range(2):
                wait(act, "a_kept", c, g + 1)
                wait(act, f"mx_ps{g}", c, LEVELS - 1, back=1)
                up(nc.scalar.copy(a_zb[g][:, :, :], a_b[g][:, :, 0, :]), "a_zb")

        def level_act(act, c, k):
            wait(act, "x_ps0", c, 2 * k if k else 1)
            up(nc.scalar.copy(x_inv[0][:, :, :], psum4(banks[0][1])), "x0")
            if k:
                wait(act, "x_ps0", c, 2 * k + 1)
                up(nc.scalar.copy(x_inv_t[0][:, :, :], psum4(banks[0][2])), "xt0")

        def tail_act(act, c):
            wait(act, "res_ps0", c, 1)
            up(nc.scalar.copy(mx[0][:, :, :], psum4(banks[0][0])), "res0")
            wait(act, "akv_ps", c)
            up(nc.scalar.copy(akv[:, :], m[2][:, 0:HALF]), "akv")
            wait(act, "w_ps", c)
            wait(act, "out", c, 4, back=1)
            up(nc.scalar.copy(w_t[:, :, :], psum4(m[0][:, HALF:SEQ])), "w_t")

        def sa_act(act, c):
            by_half = sa[:, :].rearrange("p (i g v) -> p g i v", g=2, v=HEAD)
            for g, bank in enumerate((m[1][:, 0:RT * HEAD], m[2][:, HALF:HALF + RT * HEAD])):
                wait(act, "sa_ps", c, g + 1)
                up(nc.scalar.copy(by_half[:, g, :, :], bank.rearrange("p (i v) -> p i v", i=RT)), "sa")

        def y_act(act, c):
            wait(act, "y_ps", c)
            up(nc.scalar.copy(y_c[:, :, :], psum4(m[1][:, HALF:SEQ])), "y")

        def biased_dve(dve, c):
            wait(dve, "lora", c, 1)
            wait(dve, "zr", c, 1, back=1)
            up(tt(T["decay"], psum4(prep_ps[0]), per_channel("e_w0"), ALU.add), "biased")
            wait(dve, "lora", c, 2)
            wait(dve, "bk", c, 2, back=1)
            up(tt(T["a"], psum4(prep_ps[1]), per_channel("e_a0"), ALU.add), "biased")

        def logsum_dve(dve, c):
            wait(dve, "sigmoid", c, 1)
            for i in range(RT):
                up(nc.vector.tensor_tensor_scan(T["logsum"][:, i, :], ones[:, :], T["decay"][:, i, :], 0.0,
                                                ALU.mult, ALU.add), "logsum")
            wait(dve, "logsum", c, RT)
            wait(dve, "exps", c, 1, back=1)
            up(nc.vector.tensor_copy(mid[:, :], T["logsum"][:, :, CH // 2 - 1]), "mids")

        def k2_dve(dve, c):
            wait(dve, "sigmoid", c, 2)
            wait(dve, "bk", c, 1, back=1)
            up(nc.vector.scalar_tensor_tensor(out=T["k2"], in0=T["a"], scalar=-1.0, in1=per_channel("e_k_a"),
                                              op0=ALU.add, op1=ALU.mult), "k2")
            wait(dve, "k2", c, 1)
            up(nc.vector.scalar_tensor_tensor(out=T["k2"], in0=T["k2"], scalar=1.0, in1=tokens(4, RT, c),
                                              op0=ALU.add, op1=ALU.mult), "k2")

        def floor_dve(dve, c):
            wait(dve, "k_sum", c)
            wait(dve, "k_wide", c, back=1)
            up(nc.vector.tensor_scalar(norms[:, 0, :], prep_ps[1][0:HEADS, 0:CH], 1e-24, None, ALU.max), "k_floor")

        def y_floor_dve(dve, c):
            wait(dve, "y_sum", c)
            wait(dve, "y_wide", c, back=1)
            up(nc.vector.tensor_scalar(norms[:, 1, :], prep_ps[1][0:HEADS, 0:CH], 1.0 / HEAD, GN_EPS,
                                       ALU.mult, ALU.add), "y_floor")

        def zr_dve(dve, c, s):
            wait(dve, "k_wide", c)
            up(tt(T["kk"], T["kk"], psum4(prep_ps[1]), ALU.mult), "kk")
            wait(dve, "kk", c)
            wait(dve, "exps", c, 4)
            wait(dve, "y_ps", c, back=2)
            up(nc.vector.scalar_tensor_tensor(out=zr[:, s, :, 0, :], in0=T["kk"], scalar=-1.0, in1=T["decay"],
                                              op0=ALU.mult, op1=ALU.mult), "zr")

        def r_dve(dve, c, s):
            wait(dve, "exps", c, 4)
            wait(dve, "y_ps", c, back=2)
            up(tt(zr[:, s, :, 1, :], tokens(0, RT, c), T["logsum"], ALU.mult), "zr")
            up(nc.vector.tensor_copy(end_scale[:, s, :], T["logsum"][:, :, CH - 1]), "ends")

        def bonus_dve(dve, c):
            wait(dve, "bonus_sum", c)
            wait(dve, "v_now", c)
            up(tt(tokens(8, RT, c), psum4(prep_ps[0]), v_now[:, :, :], ALU.mult), "bonus")

        def gn_dve(dve, c):
            wait(dve, "y_wide", c)
            up(tt(y_c[:, :, :], y_c[:, :, :], psum4(prep_ps[1]), ALU.mult), "gn")

        def scores_dve(dve, c):
            mask = causal[:, :, :].rearrange("p a t -> p (a t)").unsqueeze(1).to_broadcast([P, RT, 2 * CH])
            for n, dst in enumerate((a_b[0], a_b[1], a_k[0], a_k[1])):
                wait(dve, "a_ps", c, n + 1)
                if n == 0:
                    wait(dve, "y_ps", c, back=1)
                    wait(dve, "a_zb", c, 2, back=1)
                up(tt(dst[:, :, :, :].rearrange("p i a t -> p i (a t)"),
                      m[n % 3][:, :].rearrange("p (i a) -> p i a", i=RT), mask, ALU.mult), "a_kept")
                if n < 2:
                    wait(dve, "a_kept", c, n + 1)
                    wait(dve, f"res_ps{n}", c, 2, back=1)
                    up(tt(mx[n][:, :, :], a_b[n][:, :, 0, :], level_mask[:, 0, :].unsqueeze(1).to_broadcast([P, RT, CH]),
                          ALU.mult), "first")

        def mask_dve(dve, c, k):
            for g in range(2):
                wait(dve, f"mx_ps{g}", c, k)
                if k == 1:
                    wait(dve, "first_t", c, g + 1)
                up(tt(mx[g][:, :, :], psum4(banks[g][0]),
                      level_mask[:, k, :].unsqueeze(1).to_broadcast([P, RT, CH]), ALU.mult), f"mx{g}")

        def add_old(c, g_old, bank, name):
            up(tt(g_old, psum4(bank), g_old.bitcast(F32), ALU.add), name)

        def level0_dve(dve, c):
            wait(dve, "x_ps1", c, 1)
            up(tt(x_inv[1][:, :, :], psum4(banks[1][1]), ident[:, :].unsqueeze(1).to_broadcast([P, RT, CH]), ALU.add), "x1")

        def close_dve(dve, c, k):
            wait(dve, "x_ps1", c, 2 * k)
            add_old(c, x_inv[1][:, :, :], banks[1][1], "x1")
            wait(dve, "x_ps1", c, 2 * k + 1)
            add_old(c, x_inv_t[1][:, :, :], banks[1][2], "xt1")

        def mid_state_dve(dve, c, s):
            wait(dve, "exps", c, 1)
            wait(dve, "state", c, 2, back=1)
            wait(dve, "y_ps", c, back=1)
            up(tt(state_mid[:, :, :], state[:, :, :], over_tokens(mid_scale[:, s, :], HEAD), ALU.mult), "state_mid")

        def tail_dve(dve, c, s, more):
            wait(dve, "res_ps1", c, 1)
            up(nc.vector.tensor_copy(mx[1][:, :, :], psum4(banks[1][0])), "res1")
            if more:
                bonus_dve(dve, c + 1)
            for g in range(2):
                wait(dve, f"res_ps{g}", c, 2)
                up(tt(x_t[g][:, :, :], psum4(banks[g][2]), x_inv_t[g][:, :, :].bitcast(F32), ALU.add), f"x_t{g}")
            wait(dve, "s_ps", c)
            up(tt(state[:, :, :], state_mid[:, :, :], m[2][:, 0:RT * HEAD].rearrange("p (i v) -> p i v", i=RT),
                  ALU.add), "state")
            wait(dve, "state", c, 1)
            up(tt(state[:, :, :], state[:, :, :], over_tokens(end_scale[:, s, :], HEAD), ALU.mult), "state")

        def ptt(pool, o, a, b, op, name):
            up(pool.tensor_tensor(o, a, b, op=op), name)

        def v_pool(pool, c):
            wait(pool, "bonus", c, back=1)
            wait(pool, "turned", c, 4, back=1)
            up(pool.tensor_copy(v_now[:, :, :], tokens(8, RT, c)), "v_now")

        def raw_pool(pool, c):
            wait(pool, "zr", c, 1, back=1)
            wait(pool, "bk", c, 3, back=1)
            ptt(pool, T["kk"], tokens(4, RT, c), per_channel("e_k_k"), ALU.mult, "kk_raw")

        def centre_pool(pool, c):
            wait(pool, "mids", c)
            ptt(pool, T["logsum"], T["logsum"], over_tokens(mid[:, :]), ALU.subtract, "centred")
            wait(pool, "centred", c, 1)
            ptt(pool, T["decay"], T["logsum"], T["decay"], ALU.subtract, "centred")

        def rk_pool(pool, c):
            wait(pool, "k2", c, 2)
            wait(pool, "bonus_sum", c, back=1)
            ptt(pool, T["rk"], tokens(0, RT, c), T["k2"], ALU.mult, "rk")
            wait(pool, "rk", c, 1)
            ptt(pool, T["rk"], T["rk"], per_channel("e_r_k"), ALU.mult, "rk")

        def k_pool(pool, c, s):
            wait(pool, "exps", c, 2)
            wait(pool, "a_ps", c, 4, back=2)
            wait(pool, "turned", c, 3, back=2)
            ptt(pool, k_t[:, s, :, :], T["k2"], T["grow"], ALU.mult, "bk")

        def b_pool(pool, c, s):
            wait(pool, "kk", c)
            wait(pool, "zr", c, 1)
            ptt(pool, T["kk"], T["kk"], T["a"], ALU.mult, "bk")
            wait(pool, "bk", c, 2)
            ptt(pool, b_t[:, s, :, :], T["kk"], T["grow"], ALU.mult, "bk")

        def first_pool(pool, c):
            for g in range(2):
                wait(pool, "first", c, g + 1)
                wait(pool, f"x_t{g}", c, back=1)
                ptt(pool, x_inv_t[g][:, :, :], mx[g][:, :, :].bitcast(F32),
                    ident[:, :].unsqueeze(1).to_broadcast([P, RT, CH]), ALU.add, "first_t")

        def out_pool(pool, c):
            wait(pool, "gn", c)
            ptt(pool, y_c[:, :, :], y_c[:, :, :], per_channel("e_ln_w"), ALU.mult, "out")
            wait(pool, "out", c, 1)
            ptt(pool, y_c[:, :, :], y_c[:, :, :], per_channel("e_ln_b"), ALU.add, "out")
            wait(pool, "out", c, 2)
            ptt(pool, y_c[:, :, :], y_c[:, :, :], tokens(8, RT, c), ALU.add, "out")
            wait(pool, "out", c, 3)
            ptt(pool, tokens(0, RT, c), y_c[:, :, :], tokens(4, RT, c), ALU.mult, "out")

        def turn_of_pe(pe, c, s, more, late):
            turn_pe(pe, c, s, 2)
            turn_pe(pe, c, s, 3)
            for n in (1, 2, 3):
                scores_pe(pe, c, s, n)
            if more:
                lora_pe(pe, c + 1, 0)
                lora_pe(pe, c + 1, 1)
                k_sum_pe(pe, c + 1)
            level0_pe(pe, c)
            if late:
                centre_pe(pe, c - 1)
            for k in range(1, LEVELS):
                grow_pe(pe, c, k)
                if more and k == 1:
                    lora_pe(pe, c + 1, 2)
                if late and k == 2:
                    y_sum_pe(pe, c - 1)
                if late and k == 4:
                    y_wide_pe(pe, c - 1)
                if more and k == 5:
                    k_wide_pe(pe, c + 1)
                if more and k == 6:
                    bonus_pe(pe, c + 1)
                close_pe(pe, c, k)
            refine_pe(pe, c)
            if more:
                turn_pe(pe, c + 1, 1 - s, 0)
            w_pe(pe, c)
            if more:
                turn_pe(pe, c + 1, 1 - s, 1)
            sa_pe(pe, c)
            if more:
                scores_pe(pe, c + 1, 1 - s, 0)
            tail_pe(pe, c, s)

        def turn_of_act(act, c, s, more, late):
            turn_act(act, c, 2)
            turn_act(act, c, 3)
            if more:
                codes_act(act, c + 1)
                square_act(act, c + 1)
            a_zb_act(act, c)
            if more:
                sigmoids_act(act, c + 1)
            for k in range(LEVELS):
                level_act(act, c, k)
                if late and k == 0:
                    centred_act(act, c - 1)
                if k == 2:
                    if more:
                        gate_act(act, c + 1)
                        roots_act(act, c + 1, 0, 2 if late else 1)
                    else:
                        roots_act(act, c + 1, 1, 1)
                if more and k == 3:
                    exps_act(act, c + 1, 1 - s, 0)
                if more and k == 4:
                    exps_act(act, c + 1, 1 - s, 1)
            tail_act(act, c)
            if more:
                turn_act(act, c + 1, 0)
            sa_act(act, c)
            if more:
                turn_act(act, c + 1, 1)
            y_act(act, c)

        def turn_of_dve(dve, c, s, more, late):
            scores_dve(dve, c)
            if more:
                biased_dve(dve, c + 1)
                floor_dve(dve, c + 1)
            level0_dve(dve, c)
            for k in range(1, LEVELS):
                mask_dve(dve, c, k)
                if more and k == 1:
                    logsum_dve(dve, c + 1)
                if k == 2:
                    if late:
                        y_floor_dve(dve, c - 1)
                    if more:
                        k2_dve(dve, c + 1)
                if k == 3:
                    mid_state_dve(dve, c, s)
                if late and k == 4:
                    gn_dve(dve, c - 1)
                if more and k == 5:
                    zr_dve(dve, c + 1, 1 - s)
                if more and k == 6:
                    r_dve(dve, c + 1, 1 - s)
                close_dve(dve, c, k)
            tail_dve(dve, c, s, more)

        def turn_of_pool(pool, c, s, more, late):
            if more:
                raw_pool(pool, c + 1)
            first_pool(pool, c)
            if more:
                v_pool(pool, c + 1)
                centre_pool(pool, c + 1)
                rk_pool(pool, c + 1)
                k_pool(pool, c + 1, 1 - s)
            if late:
                out_pool(pool, c - 1)
            if more:
                b_pool(pool, c + 1, 1 - s)

        def all_turns(eng, turn_of):
            turn_of(eng, 0, 0, True, False)
            with eng.Fori(0, NCH // 2 - 1) as n:
                for k in (1, 2):
                    turn_of(eng, n * 2 + k, k % 2, True, True)
            turn_of(eng, NCH - 1, 1, False, True)

        lora_loaded, r_consts, eyes, selectors = sem("lora_loaded"), sem("r_consts"), sem("r_eyes"), sem("r_selectors")
        with nc.Block() as block:
            @block.sync
            def _(sp):
                sp.dma_start(lora_w[0:HEAD, :], io["e_w2"][0, :, :]).then_inc(lora_loaded, 16)
                sp.dma_start(lora_w[HEAD:P, :], io["e_a2"][0, :, :]).then_inc(lora_loaded, 16)
                sp.dma_start(lora_g[:, :], io["e_g2"][0, :, :]).then_inc(lora_loaded, 16)

            @block.scalar
            def _(act):
                start(act, "act")
                act.wait_ge(r_consts, 3)
                codes_act(act, 0)
                sigmoids_act(act, 0)
                square_act(act, 0)
                gate_act(act, 0)
                exps_act(act, 0, 0, 0)
                exps_act(act, 0, 0, 1)
                roots_act(act, 0, 0, 1)
                turn_act(act, 0, 0)
                turn_act(act, 0, 1)
                all_turns(act, turn_of_act)
                centred_act(act, last_chunk, True)
                roots_act(act, last_chunk + 2, 1, 1)

            @block.vector
            def _(dve):
                start(dve, "dve")
                nc.vector.memset(ones[:, :], 1.0).then_inc(r_consts, 1)
                nc.vector.memset(state[:, :, :], 0.0).then_inc(r_consts, 1)
                nc.vector.memset(unscale[:, :], 5.545177444479562).then_inc(r_consts, 1)
                nc.vector.tensor_copy(eye, ident[:, :]).then_inc(eyes, 1)
                for at in (0, EYE + 1):
                    nc.vector.tensor_scalar(rounded[:, at, :], ident[:, :], 0.0, None, ALU.mult).then_inc(eyes, 1)
                nc.vector.tensor_scalar(neg_eye[:, :], ident[:, :], -1.0, None, ALU.mult).then_inc(eyes, 1)
                dve.wait_ge(r_consts, 3)
                biased_dve(dve, 0)
                logsum_dve(dve, 0)
                k2_dve(dve, 0)
                floor_dve(dve, 0)
                bonus_dve(dve, 0)
                zr_dve(dve, 0, 0)
                r_dve(dve, 0, 0)
                all_turns(dve, turn_of_dve)
                y_floor_dve(dve, last_chunk)
                gn_dve(dve, last_chunk)

            @block.gpsimd
            def _(pool):
                start(pool, "pool")
                pool.memset(head_in[:, :, :], 0.0).then_inc(selectors, 1)
                pool.memset(head_out[:, :, :], 1.0).then_inc(selectors, 1)
                pool.wait_ge(selectors, 2)
                for i in range(RT):
                    pool.tensor_copy(head_in[:, i, 2 * i:2 * i + 2], head_ones[:, 0:P:HEAD]).then_inc(selectors, 1)
                by_row = head_out[:, :, :].rearrange("h i c -> h (i c)")
                pool.affine_select(out=by_row, in_=by_row, compare_op=ALU.is_ge, fill=0.0, base=0,
                                   pattern=[[1, RW]], channel_multiplier=-HEAD).then_inc(selectors, 1)
                pool.wait_ge(selectors, 2 + RT + 1)
                pool.affine_select(out=by_row, in_=by_row, compare_op=ALU.is_ge, fill=0.0, base=HEAD - 1,
                                   pattern=[[-1, RW]], channel_multiplier=HEAD).then_inc(selectors, 2)
                raw_pool(pool, 0)
                v_pool(pool, 0)
                centre_pool(pool, 0)
                rk_pool(pool, 0)
                k_pool(pool, 0, 0)
                b_pool(pool, 0, 0)
                all_turns(pool, turn_of_pool)
                out_pool(pool, last_chunk)

            @block.tensor
            def _(pe):
                start(pe, "pe")
                pe.wait_ge(lora_loaded, 48)
                pe.wait_ge(r_consts, 3)
                pe.wait_ge(eyes, 4)
                pe.wait_ge(selectors, 2 + RT + 3)
                for k in range(3):
                    lora_pe(pe, 0, k)
                k_sum_pe(pe, 0)
                bonus_pe(pe, 0)
                k_wide_pe(pe, 0)
                turn_pe(pe, 0, 0, 0)
                turn_pe(pe, 0, 0, 1)
                scores_pe(pe, 0, 0, 0)
                all_turns(pe, turn_of_pe)
                centre_pe(pe, last_chunk)
                y_sum_pe(pe, last_chunk)
                y_wide_pe(pe, last_chunk)

    Dense.q, Dense.u = 2 * EV, EV

    def residual_add_dve(dve, dn, c, slot, pair, par):
        dn.wait_unit(dve, pair, par)
        here = x_res[:, bass.ds(c, 1), :]
        nc.vector.tensor_tensor(here, here, dn.acc[slot][:, :], ALU.add).then_inc(unit_free, 1)

    with ExitStack() as sc:
        y_hi = sb(sc, "y_hi", [P, DT, SEQ], F32R)
        y_lo = sb(sc, "y_lo", [P, DT, SEQ], F32R)
        dn = Dense(sc, "o")
        w_out = io["e_w_out"].rearrange("a (k p) n -> (a p) k n", p=P)
        y_hi_done, y_lo_even, y_lo_odd = sem("y_hi_done"), sem("y_lo_even"), sem("y_lo_odd")
        y_tiles = (0, 1, 2, 3, 14, 15, 16, 17)

        def y_part(eng, k, done):
            eng.wait_ge(y_hi_done, k + 1)
            eng.tensor_tensor(y_lo[:, k, :], p_even[:, y_tiles[k], :], y_hi[:, k, :].bitcast(F32),
                              op=ALU.subtract).then_inc(done, 1)

        q0, u0 = Dense.q // 2, Dense.u
        with nc.Block() as block:
            @block.sync
            def _(sp):
                with sp.Fori(0, DT // 2) as i:
                    for s in range(2):
                        dn.load(sp, w_out, DT, bass.ds(i * (2 * P) + s * P, P), i * 2 + (q0 + s), 0)

            @block.gpsimd
            def _(pool):
                dn.take_lo(pool, DT, q0, 0)
                for k in range(1, DT, 2):
                    y_part(pool, k, y_lo_odd)
                dn.take_lo(pool, DT, q0 + 1, 0)
                with pool.Fori(1, DT // 2) as i:
                    for s in range(2):
                        dn.take_lo(pool, DT, i * 2 + (q0 + s), 0)

            @block.scalar
            def _(act):
                for k, tile in enumerate(y_tiles):
                    if k == 2:
                        dn.take_hi(act, DT, q0, 0)
                    nc.scalar.copy(y_hi[:, k, :], p_even[:, tile, :]).then_inc(y_hi_done, 1)
                dn.take_hi(act, DT, q0 + 1, 0)
                with act.Fori(1, DT // 2) as i:
                    for s in range(2):
                        dn.take_hi(act, DT, i * 2 + (q0 + s), 0)

            @block.tensor
            def _(pe):
                def parts(pe, k):
                    pe.wait_ge(y_lo_odd if k % 2 else y_lo_even, k // 2 + 1)

                with pe.Fori(0, DT // 2) as i:
                    for s in range(2):
                        dn.product(pe, DT, y_hi, y_lo, i * 2 + (u0 + s), s, i * 2 + (q0 + s), 0, parts)

            @block.vector
            def _(dve):
                for k in range(0, DT, 2):
                    y_part(nc.vector, k, y_lo_even)
                with dve.Fori(0, DT // 2) as i:
                    for s in range(2):
                        residual_add_dve(dve, dn, i * 2 + s, s, i * 2 + (q0 + s), 1)
        Dense.q += 2 * DT
        Dense.u += DT
    proj.close()

    def conv_ffn(layer):
        tag = f"f{layer}"
        with ExitStack() as sc:
            xn_hi = sb(sc, "xn_hi_" + tag, [P, DT, SEQ], F32R)
            xn_lo = sb(sc, "xn_lo_" + tag, [P, DT, SEQ], F32R)
            nm = Norm(sc, tag, "f_norm_g", DT * layer, None, xn_hi, xn_lo)
            dn = Dense(sc, tag)
            gate = sb(sc, "gate_" + tag, [P, SEQ])
            val = sb(sc, "val_" + tag, [P, SEQ])
            with ExitStack() as before_inner:
                nm.use(sb(before_inner, "scratch_" + tag, [P, 8, SEQ]))
            h_hi = sb(sc, "h_hi_" + tag, [P, FGROUP, SEQ], F32R)
            h_lo = sb(sc, "h_lo_" + tag, [P, FGROUP, SEQ], F32R)
            w_up = io["f_w_up"][layer, :, :].rearrange("(k p) n -> p k n", p=P)
            w_down = io["f_w_down"][layer, :, :].rearrange("(g k p) n -> g p k n", g=2, p=P)
            f_start, f_tap, f_silu, f_h, f_hi, f_lo = (
                sem("f_" + n) for n in ("start", "tap", "silu", "h", "hi", "lo"))
            made = layer * FT
            UP = 2 * FGROUP
            PAIRS = UP + 3 * DT // 2
            UNITS = 2 * FGROUP + DT
            q0, u0 = Dense.q // 2, Dense.u
            taps, bias = COL["f_conv_w"] + layer * 3 * 2 * FT, COL["f_conv_b"] + layer * 2 * FT

            def param(first, tile):
                return prm[:, bass.ds(tile + first, 1)]

            def tile_of(g, m, half):
                return g * FGROUP + m + half * FT

            def up_cols(g, m, half):
                return bass.ds(g * (FGROUP * P) + m * P + half * D_FF, P)

            def up_pair(g, m, half):
                return g * PAIRS + m * 2 + (half + q0)

            def up_unit(g, m, half):
                return g * UNITS + m * 2 + (half + u0)

            with nc.Block() as block:
                @block.sync
                def _(sp):
                    with sp.Fori(0, 2) as g:
                        with sp.Fori(0, FGROUP) as m:
                            for half in range(2):
                                dn.load(sp, w_up, DT, up_cols(g, m, half), up_pair(g, m, half), 0)
                        with sp.Fori(0, DT // 2) as i:
                            for s in range(2):
                                dn.load(sp, w_down[bass.ds(g, 1), :, :, :].rearrange("g p k n -> (g p) k n"), FGROUP,
                                        bass.ds(i * (2 * P) + s * P, P), g * PAIRS + i * 3 + (UP + q0 + s), s)

                @block.tensor
                def _(pe):
                    nm.sums_pe(pe)
                    with pe.Fori(0, 2) as g:
                        with pe.Fori(0, FGROUP) as m:
                            for half in range(2):
                                dn.product(pe, DT, xn_hi, xn_lo, up_unit(g, m, half), half, up_pair(g, m, half), 0,
                                           nm.wait_tile)
                        with pe.Fori(0, DT // 2) as i:
                            for s in range(2):
                                dn.product(pe, FGROUP, h_hi, h_lo, g * UNITS + i * 2 + (2 * FGROUP + u0 + s), s,
                                           g * PAIRS + i * 3 + (UP + q0 + s), s,
                                           lambda eng, k: eng.wait_ge(f_lo, g * FGROUP + (made + k + 2)))

                @block.scalar
                def _(act):
                    def begin(g, m, half):
                        act.wait_ge(f_lo if half else f_h, g * FGROUP + m + (made + 1))
                        dn.wait_unit(act, up_pair(g, m, half), 1)
                        nc.scalar.activation((gate, val)[half][:, :], dn.acc[half][:, :], ACT.Identity,
                                             scale=param(taps + 2 * 2 * FT, tile_of(g, m, half)),
                                             bias=param(bias, tile_of(g, m, half))).then_inc(f_start, 1)

                    def silu(g, m):
                        act.wait_ge(unit_free, up_unit(g, m, 0) + 3)
                        nc.scalar.activation(gate[:, :], gate[:, :], ACT.Silu).then_inc(f_silu, 1)

                    def keep_hi(g, m):
                        act.wait_ge(f_h, g * FGROUP + m + (made + 2))
                        nc.scalar.copy(h_hi[:, bass.ds(m, 1), :], val[:, :]).then_inc(f_hi, 1)

                    nm.squares_act(act)
                    for g in range(2):
                        dn.take_hi(act, DT, g * PAIRS + q0, 0)
                        if g == 0:
                            nm.root_act(act)
                            nm.hi_act(act)
                        dn.take_hi(act, DT, g * PAIRS + (q0 + 1), 0)
                        begin(g, 0, 0)
                        silu(g, 0)
                        with act.Fori(1, FGROUP) as m:
                            dn.take_hi(act, DT, up_pair(g, m, 0), 0)
                            begin(g, m + (-1), 1)
                            keep_hi(g, m + (-1))
                            dn.take_hi(act, DT, up_pair(g, m, 1), 0)
                            begin(g, m, 0)
                            silu(g, m)
                        down = g * PAIRS + UP + q0
                        dn.take_hi(act, FGROUP, down, 0, 0, 1)
                        begin(g, FGROUP - 1, 1)
                        dn.take_hi(act, FGROUP, down, 0, 1, 2)
                        keep_hi(g, FGROUP - 1)
                        dn.take_hi(act, FGROUP, down, 0, 2)
                        dn.take_hi(act, FGROUP, down + 1, 1)
                        with act.Fori(1, DT // 2) as i:
                            for s in range(2):
                                dn.take_hi(act, FGROUP, g * PAIRS + i * 3 + (UP + q0 + s), s)

                @block.vector
                def _(dve):
                    nm.sums_dve(dve)
                    nm.parts_dve(dve)
                    with dve.Fori(0, 2) as g:
                        with dve.Fori(0, FGROUP) as m:
                            for half in range(2):
                                n = g * (2 * FGROUP) + m * 2 + (half + 2 * made)
                                dve.wait_ge(f_start, n + 1)
                                for back in (1, 2):
                                    here = (gate, val)[half][:, back:SEQ]
                                    if back == 2:
                                        dve.wait_ge(f_tap, n + 1)
                                    nc.vector.scalar_tensor_tensor(
                                        out=here, in0=dn.acc[half][:, 0:SEQ - back],
                                        scalar=param(taps + (2 - back) * 2 * FT, tile_of(g, m, half)), in1=here,
                                        op0=ALU.mult, op1=ALU.add).then_inc(f_tap if back == 1 else unit_free, 1)
                            dve.wait_ge(f_silu, g * FGROUP + m + (made + 1))
                            dve.wait_ge(unit_free, up_unit(g, m, 1) + 3)
                            nc.vector.tensor_tensor(val[:, :], gate[:, :], val[:, :], ALU.mult).then_inc(f_h, 1)
                            dve.wait_ge(f_hi, g * FGROUP + m + (made + 1))
                            nc.vector.tensor_tensor(h_lo[:, bass.ds(m, 1), :], val[:, :],
                                                    h_hi[:, bass.ds(m, 1), :].bitcast(F32), ALU.subtract).then_inc(f_lo, 1)
                        with dve.Fori(0, DT // 2) as i:
                            residual_add_dve(dve, dn, i * 2, 0, g * PAIRS + i * 3 + (UP + q0 + 1), 0)
                            residual_add_dve(dve, dn, i * 2 + 1, 1, g * PAIRS + i * 3 + (UP + q0 + 2), 1)

                @block.gpsimd
                def _(pool):
                    if layer == 0:
                        pool.sem_inc(f_h, 1)
                        pool.sem_inc(f_lo, 1)
                    dn.take_lo(pool, DT, q0, 0)
                    nm.lo_pool(pool)
                    dn.take_lo(pool, DT, q0 + 1, 0)
                    for g in range(2):
                        if g == 0:
                            with pool.Fori(1, FGROUP) as m:
                                for half in range(2):
                                    dn.take_lo(pool, DT, up_pair(g, m, half), 0)
                        else:
                            with pool.Fori(0, FGROUP) as m:
                                for half in range(2):
                                    dn.take_lo(pool, DT, up_pair(g, m, half), 0)
                        with pool.Fori(0, DT // 2) as i:
                            for s in range(2):
                                dn.take_lo(pool, FGROUP, g * PAIRS + i * 3 + (UP + q0 + s), s)
            Dense.q += 2 * 2 * PAIRS
            Dense.u += 2 * UNITS

    conv_ffn(0)

    s5 = ctx.enter_context(ExitStack())
    u_s5 = sb(s5, "u_s5", [P, DT, SEQ])
    K9 = L5 + 1
    rot = sb(s5, "rot", [P, 2, S5_PAIRS, N5])
    power = sb(s5, "power", [P, 2, K9, S5_PAIRS])
    b_bar = sb(s5, "b_bar", [P, 2, S5_PAIRS, 16])
    c_s5 = sb(s5, "c_s5", [P, 3, S5_PAIRS, 16])
    decay8 = sb(s5, "decay8", [P, S5_PAIRS])
    with ExitStack() as sc:
        xn_hi = sb(sc, "xn_hi_s", [P, DT, SEQ], F32R)
        xn_lo = sb(sc, "xn_lo_s", [P, DT, SEQ], F32R)
        nm = Norm(sc, "s", "o_norm_g", 0, rot[:, :, :, :].rearrange("p a r n -> p (a r n)").rearrange("p (k t) -> p k t", k=8),
                  xn_hi, xn_lo)
        dn = Dense(sc, "s")
        s_rows = sb(sc, "s_rows", [S5_PAIRS, 3, P])
        dt_rows = sb(sc, "dt_rows", [S5_PAIRS, 2])
        b_raw = sb(sc, "b_raw", [P, 2, S5_PAIRS, 16])
        c_raw = sb(sc, "c_raw", [P, DT, 2, 64])
        small = sb(sc, "small", [P, 20, S5_PAIRS])
        s_ps = ps(sc, "s_ps", [P, 3, S5_PAIRS])
        c_ps = nm.rstd
        w_in = io["o_w_in"].rearrange("a (k p) n -> (a p) k n", p=P)
        s_loaded, c_loaded, s_turned, c_turned, dt_wide = (
            sem(n) for n in ("s_loaded", "c_loaded", "s_turned", "c_turned", "dt_wide"))
        s_act, s_arg, c_kept = sem("s_act"), sem("s_arg"), sem("c_kept")
        q0, u0 = Dense.q // 2, Dense.u
        V = {n: small[:, k, :] for k, n in enumerate(
            "lre dt lr ang turns mag s2 h c2 cos sin zr den qre qim t1 t2 ck sk aim".split())}
        TWO_PI = 6.283185307179586
        TURN1 = 6.28125
        TURN2 = 0.0019340515136718750
        TURN3 = TWO_PI - TURN1 - TURN2
        ROUND = 12582912.0
        with nc.Block() as block:
            @block.sync
            def _(sp):
                for k, name in enumerate(("o_A_re", "o_A_im")):
                    sp.dma_start(s_rows[:, k, :], io[name].rearrange("a (r g) n -> (a r) (g n)", g=2)).then_inc(s_loaded, 16)
                sp.dma_start(dt_rows[:, :], io["o_log_dt"].rearrange("a (r g) -> (a r) g", g=2)).then_inc(s_loaded, 16)
                for k in range(2):
                    sp.dma_start(c_raw[:, :, k, :], io["o_C_re"].rearrange("a (t g) c n -> (a g c) t n", g=8)).then_inc(c_loaded, 16)
                for k, name in enumerate(("o_B_re", "o_B_im")):
                    b = io[name].rearrange("a (r g) n c -> (a g) n r c", g=2)
                    for g in range(2):
                        sp.dma_start(b_raw[g * 64:(g + 1) * 64, k, :, :], b[g, :, :, :]).then_inc(s_loaded, 16)
                with sp.Fori(0, DT // 2) as i:
                    for s in range(2):
                        dn.load(sp, w_in, DT, bass.ds(i * (2 * P) + s * P, P), i * 2 + (q0 + s), 0)
                sp.wait_ge(c_turned, 1)
                for k in range(2):
                    sp.dma_start(c_raw[:, :, k, :], io["o_C_im"].rearrange("a (t g) c n -> (a g c) t n", g=8)).then_inc(c_loaded, 16)

            @block.gpsimd
            def _(pool):
                dn.take_lo(pool, DT, q0, 0)
                nm.lo_pool(pool)
                dn.take_lo(pool, DT, q0 + 1, 0)
                with pool.Fori(1, DT // 2) as i:
                    for s in range(2):
                        dn.take_lo(pool, DT, i * 2 + (q0 + s), 0)

            @block.tensor
            def _(pe):
                nm.sums_pe(pe)
                for s in range(2):
                    dn.product(pe, DT, xn_hi, xn_lo, u0 + s, s, q0 + s, 0, nm.wait_tile)
                pe.wait_ge(s_loaded, 7 * 16)
                pe.wait_ge(dt_wide, 1)
                for k in range(3):
                    last = nc.tensor.transpose(s_ps[:, k, :], s_rows[:, k, :], ident[0:S5_PAIRS, 0:S5_PAIRS])
                last.then_inc(s_turned, 1)

                def turn_c(n):
                    pe.wait_ge(c_loaded, 32 * (n + 1))
                    for t in range(DT):
                        last = nc.tensor.transpose(c_ps[:, t * P:(t + 1) * P],
                                                   c_raw[:, t, :, :].rearrange("p k n -> p (k n)"), ident[:, :])
                    last.then_inc(c_turned, 1)

                turn_c(0)
                with pe.Fori(1, DT // 2) as i:
                    for s in range(2):
                        dn.product(pe, DT, xn_hi, xn_lo, i * 2 + (u0 + s), s, i * 2 + (q0 + s), 0)
                pe.wait_ge(c_kept, 2)
                turn_c(1)

            @block.scalar
            def _(act):
                def keep_u(i, slot):
                    dn.wait_unit(act, i + q0, 1)
                    acc = dn.acc[slot][:, :].rearrange("p (n h j) -> p h n j", h=2, j=4)
                    for q in range(4):
                        for r in range(4):
                            here = u_s5[32 * r:32 * r + 32, bass.ds(i, 1), :].rearrange("p a (q h n) -> p (a q) h n", q=4, h=2)
                            last = nc.scalar.copy(here[:, q, :, :], acc[32 * q:32 * q + 32, :, :, 3 - r])
                    last.then_inc(unit_free, 1)

                nm.squares_act(act)
                dn.take_hi(act, DT, q0, 0)
                nm.root_act(act)
                nm.hi_act(act)
                dn.take_hi(act, DT, q0 + 1, 0)
                keep_u(0, 0)
                dn.take_hi(act, DT, q0 + 2, 0)
                keep_u(1, 1)
                act.wait_ge(s_arg, 1)
                nc.scalar.activation(V["dt"], V["dt"], ACT.Exp).then_inc(s_act, 1)
                act.wait_ge(s_arg, 2)
                nc.scalar.activation(V["mag"], V["lr"], ACT.Exp).then_inc(s_act, 1)
                act.wait_ge(s_arg, 3)
                nc.scalar.activation(V["s2"], V["h"], ACT.Sin).then_inc(s_act, 1)
                act.wait_ge(s_arg, 4)
                nc.scalar.activation(V["c2"], V["c2"], ACT.Sin).then_inc(s_act, 1)
                with act.Fori(1, DT // 2 - 1) as i:
                    for s in range(2):
                        dn.take_hi(act, DT, i * 2 + (q0 + (s + 1)), 0)
                        keep_u(i * 2 + s, s)
                dn.take_hi(act, DT, q0 + DT - 1, 0)
                keep_u(DT - 2, 0)
                keep_u(DT - 1, 1)

            @block.vector
            def _(dve):
                link = Link(dve, "s5_setup")

                def mul(o, a, b, op=ALU.mult):
                    link.run(nc.vector.tensor_tensor(o, a, b, op))

                def together(*steps):
                    for o, a, b, op in steps:
                        link.did(nc.vector.tensor_tensor(o, a, b, op))
                    link.wait()

                def affine(o, a, k1, k2=None, op0=ALU.mult, op1=ALU.add):
                    link.run(nc.vector.tensor_scalar(o, a, k1, k2, op0, op1) if k2 is not None
                             else nc.vector.tensor_scalar(o, a, k1, None, op0))

                def fused(o, a, k, b, op0=ALU.mult, op1=ALU.add):
                    link.run(nc.vector.scalar_tensor_tensor(out=o, in0=a, scalar=k, in1=b, op0=op0, op1=op1))

                def keep_c(n):
                    dve.wait_ge(c_turned, n + 1)
                    for g in range(2):
                        half = slice(g * 64, (g + 1) * 64)
                        src = c_ps[half, :].rearrange("p (r g c) -> p g r c", g=2, c=16)
                        nc.vector.tensor_copy(c_s5[half, n, :, :], src[:, g, :, :]).then_inc(c_kept, 1)

                nm.sums_dve(dve)
                nm.parts_dve(dve)
                dve.wait_ge(s_loaded, 7 * 16)
                nc.vector.tensor_copy(s_rows[:, 2, :].rearrange("p (g n) -> p g n", g=2),
                                      dt_rows[:, :].unsqueeze(2).to_broadcast([S5_PAIRS, 2, 64])).then_inc(dt_wide, 1)
                dve.wait_ge(s_turned, 1)
                affine(V["lre"], s_ps[:, 0, :], -1e-4, None, ALU.min)
                link.run(nc.vector.tensor_copy(V["aim"], s_ps[:, 1, :]))
                nc.vector.tensor_copy(V["dt"], s_ps[:, 2, :]).then_inc(s_arg, 1)
                dve.wait_ge(s_act, 1)
                mul(V["ang"], V["aim"], V["dt"])
                nc.vector.tensor_tensor(V["lr"], V["lre"], V["dt"], ALU.mult).then_inc(s_arg, 1)
                affine(V["turns"], V["ang"], 1 / TWO_PI, ROUND)
                affine(V["turns"], V["turns"], -ROUND, None, ALU.add)
                fused(V["ang"], V["turns"], -TURN1, V["ang"])
                fused(V["ang"], V["turns"], -TURN2, V["ang"])
                fused(V["ang"], V["turns"], -TURN3, V["ang"])
                dve.wait_ge(s_arg, 2)
                nc.vector.tensor_scalar(V["h"], V["ang"], 0.5, None, ALU.mult).then_inc(s_arg, 1)
                dve.wait_ge(s_arg, 3)
                fused(V["c2"], V["h"], -1.0, V["h"], ALU.mult, ALU.max)
                nc.vector.tensor_scalar(V["c2"], V["c2"], -1.0, TWO_PI / 4, ALU.mult, ALU.add).then_inc(s_arg, 1)
                dve.wait_ge(s_act, 4)
                fused(V["sin"], V["s2"], 2.0, V["c2"], ALU.mult, ALU.mult)
                mul(V["t1"], V["s2"], V["s2"])
                affine(V["cos"], V["t1"], -2.0, 1.0)
                link.run(nc.vector.memset(power[:, 0, 0, :], 1.0))
                link.run(nc.vector.memset(power[:, 1, 0, :], 0.0))
                a_re, a_im = power[:, 0, 1, :], power[:, 1, 1, :]
                mul(a_re, V["mag"], V["cos"])
                mul(a_im, V["mag"], V["sin"])
                for k in range(2, K9):
                    re, im = power[:, 0, k - 1, :], power[:, 1, k - 1, :]
                    together((V["t1"], re, a_re, ALU.mult), (V["t2"], im, a_im, ALU.mult),
                             (V["ck"], re, a_im, ALU.mult), (V["sk"], im, a_re, ALU.mult))
                    together((power[:, 0, k, :], V["t1"], V["t2"], ALU.subtract),
                             (power[:, 1, k, :], V["ck"], V["sk"], ALU.add))
                mul(V["t1"], V["lre"], V["lre"])
                mul(V["t2"], V["aim"], V["aim"])
                mul(V["den"], V["t1"], V["t2"], ALU.add)
                link.run(nc.vector.reciprocal(V["den"], V["den"]))
                affine(V["zr"], a_re, -1.0, None, ALU.add)
                for q, x, y, op in ((V["qre"], V["zr"], a_im, ALU.add), (V["qim"], a_im, V["zr"], ALU.subtract)):
                    mul(V["t1"], x, V["lre"])
                    mul(V["t2"], y, V["aim"])
                    mul(V["t1"], V["t1"], V["t2"], op)
                    mul(q, V["t1"], V["den"])
                wide = [P, S5_PAIRS, 16]
                q_re, q_im = (V[n].unsqueeze(2).to_broadcast(wide) for n in ("qre", "qim"))
                dve.wait_ge(n_lo_odd, nm.n * 4 + 4)
                dve.wait_ge(n_lo_even, nm.n * 4 + 4)
                tmp = rot[:, 1, 0:4, :].rearrange("p r n -> p (r n)").rearrange("p (r c) -> p r c", c=16)
                mul(b_bar[:, 0, :, :], b_raw[:, 0, :, :], q_re)
                mul(tmp, b_raw[:, 1, :, :], q_im)
                mul(b_bar[:, 0, :, :], b_bar[:, 0, :, :], tmp, ALU.subtract)
                mul(b_bar[:, 1, :, :], b_raw[:, 1, :, :], q_re)
                mul(tmp, b_raw[:, 0, :, :], q_im)
                mul(b_bar[:, 1, :, :], b_bar[:, 1, :, :], tmp, ALU.add)
                keep_c(0)
                mul(V["mag"], V["mag"], V["mag"])
                mul(V["mag"], V["mag"], V["mag"])
                mul(decay8[:, :], V["mag"], V["mag"])
                link.run(nc.vector.tensor_copy(V["ck"], V["cos"]))
                link.run(nc.vector.tensor_copy(V["sk"], V["sin"]))

                def square_turn():
                    together((V["t1"], V["ck"], V["ck"], ALU.mult), (V["t2"], V["sk"], V["sk"], ALU.mult))
                    fused(V["sk"], V["ck"], 2.0, V["sk"], ALU.mult, ALU.mult)
                    mul(V["ck"], V["t1"], V["t2"], ALU.subtract)

                for _ in range(3):
                    square_turn()
                link.run(nc.vector.memset(rot[:, 0, :, 0:1], 1.0))
                link.run(nc.vector.memset(rot[:, 1, :, 0:1], 0.0))
                n = 1
                while n < N5:
                    pairs = min(S5_PAIRS, 512 // n)
                    for lo in range(0, S5_PAIRS, pairs):
                        r = slice(lo, lo + pairs)
                        step = [P, pairs, n]
                        ck, sk = (V[x][:, r].unsqueeze(2).to_broadcast(step) for x in ("ck", "sk"))
                        cos, sin = rot[:, 0, r, 0:n], rot[:, 1, r, 0:n]
                        new = [rot[:, k, r, n:2 * n] for k in range(2)]
                        part = [b_raw[:, k, :, :].rearrange("p r c -> p (r c)")[:, 0:pairs * n].rearrange("p (r n) -> p r n", r=pairs)
                                for k in range(2)]
                        together((new[0], cos, ck, ALU.mult), (new[1], sin, ck, ALU.mult),
                                 (part[0], sin, sk, ALU.mult), (part[1], cos, sk, ALU.mult))
                        together((new[0], new[0], part[0], ALU.subtract), (new[1], new[1], part[1], ALU.add))
                    n *= 2
                    if n < N5:
                        square_turn()
                keep_c(1)
                dve.wait_ge(c_kept, 4)
                affine(c_s5[:, 2, :, :], c_s5[:, 0, :, :], -1.0)
                link.close()
        Dense.q += 2 * DT
        Dense.u += DT

    with ExitStack() as sc:
        gx = sb(sc, "gx", [P, 2, 2, 4, L5, 32])
        gx0 = sb(sc, "gx0", [P, 2, 4, 4, 32])
        hx = sb(sc, "hx", [P, 2, 2, 4, K9, 32])
        g_in = sb(sc, "g_in", [P, 4, 2, 2, P])
        fir0 = sb(sc, "fir0", [P, 4, 4, 32])
        fir1 = sb(sc, "fir1", [P, 4, P])
        d_rows = sb(sc, "d_rows", [P, S5_PAIRS])
        eye32 = sb(sc, "eye32", [P, 32])
        d_diag = sb(sc, "d_diag", [P, 4, 32])
        u_now = sb(sc, "u_now", [P, 2, 4, 2, N5])
        mg = [sb(sc, f"mg{k}", [P, L5, 4, 16]) for k in range(4)]
        mh = [sb(sc, f"mh{k}", [P, K9, 4, 16]) for k in range(4)]
        first0 = sb(sc, "first0", [P, 4, N5])
        keep8 = sb(sc, "keep8", [P, 4, N5])
        f_hat = sb(sc, "f_hat", [P, 2, 4, N5])
        s_hat = f_hat
        r_tmp = sb(sc, "r_tmp", [P, 2, 4, N5])
        s_prev = sb(sc, "s_prev", [P, 2, 2, 4, N5])
        f_ps = ps(sc, "f_ps", [P, 4, 2, N5])
        y_ps = ps(sc, "y5_ps", [P, 4, 2, N5])
        tk_ps = [ps(sc, f"tk_ps{k}", [P, HALF]) for k in range(2)]
        k0_ps = ps(sc, "k0_ps", [P, 4, 4, 32])
        k1_ps = ps(sc, "k1_ps", [P, 4, P])
        R5 = Rounds("s5", {
            "pool": {"mg": 4, "gx": 4, "mh": 4},
            "pe": {"turn": 4, "k": 2, "f": 1, "fir": 1, "y": 1},
            "act": {"g": 5, "filters": 5, "out": 16},
            "dve": {"gx0": 3, "hx": 4, "rin": 7, "scan": 2, "rout": 6},
        })
        s5_clear = sem("s5_clear")

        def make_pool(pool, i, s):
            def pw(part, n):
                return power[:, part, 0:n, bass.ds(i * 4, 4)].unsqueeze(3).to_broadcast([P, n, 4, 16])

            def over_k(t, n):
                return t[:, bass.ds(i * 4, 4), :].unsqueeze(1).to_broadcast([P, n, 4, 16])

            b_re, b_im = (over_k(b_bar[:, k, :, :], L5) for k in range(2))
            c_re, c_im, c_neg = (over_k(c_s5[:, k, :, :], K9) for k in range(3))
            for o, a, b in zip(mg, (b_re, b_im, b_im, b_re), (pw(0, L5), pw(1, L5), pw(0, L5), pw(1, L5))):
                R5.up(pool.tensor_tensor(o[:, :, :, :], a, b, op=ALU.mult), "mg")
            pool.wait_ge(s5_clear, 1)
            R5.wait(pool, "mg", i, 4)
            R5.wait(pool, "k", i, 2, back=2)
            R5.wait(pool, "gx0", i, 2, back=2)
            for part, op in enumerate((ALU.subtract, ALU.add)):
                for g in range(2):
                    half = slice(g * 64, (g + 1) * 64)
                    R5.up(pool.tensor_tensor(gx[half, s, part, :, :, g * 16:(g + 1) * 16].rearrange("p q k c -> p k q c"),
                                             mg[2 * part][half, :, :, :], mg[2 * part + 1][half, :, :, :], op=op), "gx")
            R5.wait(pool, "gx", i, 4)
            R5.wait(pool, "hx", i, 4, back=1)
            for o, a, b in zip(mh, (c_re, c_im, c_neg, c_im), (pw(0, K9), pw(1, K9), pw(1, K9), pw(0, K9))):
                R5.up(pool.tensor_tensor(o[:, :, :, :], a, b, op=ALU.mult), "mh")

        def prep_dve(dve, i, s):
            R5.wait(dve, "k", i, 1, back=1)
            R5.wait(dve, "gx", i, 4)
            for part in range(2):
                R5.up(nc.vector.tensor_copy(gx0[:, part, :, :, :],
                                            gx[:, s, part, :, 0, :].unsqueeze(2).to_broadcast([P, 4, 4, 32])), "gx0")
            R5.up(nc.vector.tensor_tensor(d_diag[:, :, :], d_rows[:, bass.ds(i * 4, 4)].unsqueeze(2).to_broadcast([P, 4, 32]),
                                          eye32[:, :].unsqueeze(1).to_broadcast([P, 4, 32]), ALU.mult), "gx0")
            R5.wait(dve, "mh", i, 4)
            R5.wait(dve, "y", i, 1, back=2)
            for part in range(2):
                for g in range(2):
                    half = slice(g * 64, (g + 1) * 64)
                    R5.up(nc.vector.tensor_tensor(hx[half, s, part, :, :, g * 16:(g + 1) * 16].rearrange("p q k c -> p k q c"),
                                                  mh[2 * part][half, :, :, :], mh[2 * part + 1][half, :, :, :],
                                                  ALU.subtract), "hx")

        def turn_pe(pe, i, s):
            R5.wait(pe, "gx", i, 4)
            for q in range(4):
                R5.wait(pe, "g", i, *((q + 4, 1) if q < 2 else (q, 0)))
                for part in range(2):
                    for grp in range(2):
                        at = (2 * part + grp) * P
                        last = nc.tensor.transpose(tk_ps[q % 2][:, at:at + P],
                                                   gx[:, s, part, q, 4 * grp:4 * grp + 4, :].rearrange("p k c -> p (k c)"),
                                                   ident[:, :])
                R5.up(last, "turn")
            R5.wait(pe, "filters", i, 4, back=1)
            R5.wait(pe, "gx0", i, 3)
            nc.tensor.matmul(k0_ps[:, :, 0, :], ident[:, :], d_diag[:, :, :], start=True, stop=False, skip_group_check=True)
            R5.wait(pe, "hx", i, 4)
            for q in range(4):
                for part in range(2):
                    last = nc.tensor.matmul(k0_ps[:, q, :, :], gx0[:, part, q, :, :].rearrange("p r c -> p (r c)"),
                                            hx[:, s, part, q, 0:4, :], start=False, stop=part == 1, skip_group_check=True)
            R5.up(last, "k")
            R5.wait(pe, "filters", i, 5, back=1)
            for q in range(4):
                for part in range(2):
                    last = nc.tensor.matmul(k1_ps[:, q, :], gx[:, s, part, q, 1:5, :].rearrange("p k c -> p (k c)"),
                                            hx[:, s, part, q, 0:4, :], start=part == 0, stop=part == 1)
            R5.up(last, "k")

        def turn_act(act, i, s):
            R5.wait(act, "y", i, 1, back=2)
            R5.up(nc.scalar.copy(u_now[:, s, :, :, :].rearrange("p q h n -> p (q h n)"), u_s5[:, bass.ds(i, 1), :]), "g")
            R5.wait(act, "f", i, 1, back=1)
            for q in range(4):
                R5.wait(act, "turn", i, q + 1)
                R5.up(nc.scalar.copy(g_in[:, q, :, :, :].rearrange("p a b n -> p (a b n)"), tk_ps[q % 2][:, :]), "g")
            R5.wait(act, "k", i, 1)
            R5.wait(act, "fir", i, 1, back=1)
            for r in range(4):
                rows = slice(32 * r, 32 * r + 32)
                R5.up(nc.scalar.copy(fir0[rows, :, 3 - r:4, :], k0_ps[rows, :, 0:r + 1, :]), "filters")
            R5.wait(act, "k", i, 2)
            R5.up(nc.scalar.copy(fir1[:, :, :], k1_ps[:, :, :]), "filters")

        def states_pe(pe, i, s):
            R5.wait(pe, "g", i, 5)
            R5.wait(pe, "rin", i, 5, back=1)
            for q in range(4):
                for part in range(2):
                    for grp in range(2):
                        last = nc.tensor.matmul(f_ps[:, q, part, :], g_in[:, q, part, grp, :], u_now[:, s, q, 1 - grp, :],
                                                start=grp == 0, stop=grp == 1)
            R5.up(last, "f")
            R5.wait(pe, "filters", i, 5)
            R5.wait(pe, "out", i, 16, back=1)
            for q in range(4):
                own = fir0[:, q, :, :].rearrange("p j c -> p (j c)")
                nc.tensor.matmul(y_ps[:, q, 0, :], own, u_now[:, s, q, 0, :], start=q % 2 == 0, stop=False, skip_group_check=True)
                nc.tensor.matmul(y_ps[:, q, 1, :], own, u_now[:, s, q, 1, :], start=False, stop=False, skip_group_check=True)
                last = nc.tensor.matmul(y_ps[:, q, 1, :], fir1[:, q, :], u_now[:, s, q, 0, :], start=False, stop=False,
                                        skip_group_check=True)
            R5.up(last, "fir")

        def output_pe(pe, i, s):
            R5.wait(pe, "rout", i, 6)
            for q in range(4):
                for h in range(2):
                    for part in range(2):
                        last = nc.tensor.matmul(y_ps[:, q, h, :],
                                                hx[:, s, part, q, 4 * h + 1:4 * h + 5, :].rearrange("p k c -> p (k c)"),
                                                s_prev[:, s, part, q, :], start=False, stop=part == 1,
                                                skip_group_check=True)
            R5.up(last, "y")

        def output_act(act, i, s):
            act.wait_ge(s5_clear, 5)
            R5.wait(act, "y", i)
            for q in range(4):
                for j in range(4):
                    here = u_s5[32 * q:32 * q + 32, bass.ds(i, 1), :].rearrange("p a (n h j) -> p (a h) n j", h=2, j=4)
                    R5.up(nc.scalar.activation(here[:, :, :, j], y_ps[32 * j:32 * j + 32, q, :, :], ACT.Gelu_apprx_tanh), "out")

        def scan_dve(dve, i, s):
            c_i, s_i = (rot[:, k, bass.ds(i * 4, 4), :] for k in range(2))
            R5.up(nc.vector.tensor_tensor(keep8[:, :, :], first0[:, :, :],
                                          decay8[:, bass.ds(i * 4, 4)].unsqueeze(2).to_broadcast([P, 4, N5]), ALU.mult), "rin")
            R5.wait(dve, "f", i)
            f_re, f_im = (f_ps[:, :, part, :] for part in range(2))
            x, y = f_hat[:, 0, :, :], f_hat[:, 1, :, :]
            xt, yt = r_tmp[:, 0, :, :], r_tmp[:, 1, :, :]
            R5.wait(dve, "rout", i, 6, back=1)
            for o, a, t in ((x, f_re, c_i), (y, f_im, c_i), (xt, f_im, s_i), (yt, f_re, s_i)):
                R5.up(nc.vector.tensor_tensor(o, a, t, ALU.mult), "rin")
            R5.wait(dve, "rin", i, 4)
            R5.up(nc.vector.tensor_tensor(x, x, xt, ALU.add), "rin")
            R5.wait(dve, "rin", i, 5)
            R5.up(nc.vector.tensor_tensor(y, y, yt, ALU.subtract), "rin")
            for part in range(2):
                R5.wait(dve, "rin", i, 6 + part)
                R5.up(nc.vector.tensor_tensor_scan(
                    s_hat[:, part, :, :].rearrange("p q n -> p (q n)"), keep8[:, :, :].rearrange("p q n -> p (q n)"),
                    f_hat[:, part, :, :].rearrange("p q n -> p (q n)"), 0.0, ALU.mult, ALU.add), "scan")
            R5.wait(dve, "scan", i, 2)
            R5.wait(dve, "y", i, 1, back=2)
            past = slice(0, N5 - 1)
            sx, sy = s_hat[:, 0, :, past], s_hat[:, 1, :, past]
            px, py = s_prev[:, s, 0, :, 1:N5], s_prev[:, s, 1, :, 1:N5]
            for o, a, t in ((px, sx, c_i), (py, sy, c_i), (xt[:, :, past], sy, s_i), (yt[:, :, past], sx, s_i)):
                R5.up(nc.vector.tensor_tensor(o, a, t[:, :, past], ALU.mult), "rout")
            R5.wait(dve, "rout", i, 4)
            R5.up(nc.vector.tensor_tensor(px, px, xt[:, :, past], ALU.subtract), "rout")
            R5.up(nc.vector.tensor_tensor(py, py, yt[:, :, past], ALU.add), "rout")

        def pipelined(eng, before, work, after):
            def step(i, s, more):
                if work:
                    work(eng, i, s)
                if more:
                    before(eng, i + 1, 1 - s)
                if after:
                    after(eng, i, s)
            before(eng, 0, 0)
            with eng.Fori(0, DT // 2 - 1) as n:
                for s in range(2):
                    step(n * 2 + s, s, True)
            step(DT - 2, 0, True)
            step(DT - 1, 1, False)

        with nc.Block() as block:
            @block.gpsimd
            def _(pool):
                R5.start(pool, "pool")
                with pool.Fori(0, DT // 2) as n:
                    for s in range(2):
                        make_pool(pool, n * 2 + s, s)

            @block.vector
            def _(dve):
                R5.start(dve, "dve")
                nc.vector.memset(gx[:, :, :, :, :, :], 0.0).then_inc(s5_clear, 1)
                nc.vector.memset(fir0[:, :, :, :], 0.0).then_inc(s5_clear, 1)
                nc.vector.memset(hx[:, :, :, :, :, :], 0.0).then_inc(s5_clear, 1)
                nc.vector.memset(first0[:, :, :], 1.0).then_inc(s5_clear, 1)
                nc.vector.memset(s_prev[:, :, :, :, 0:1], 0.0).then_inc(s5_clear, 1)
                dve.wait_ge(s5_clear, 5)
                nc.vector.memset(first0[:, :, 0:1], 0.0).then_inc(s5_clear, 1)
                own_d = d_rows[:, :].rearrange("p (i q) -> p i q", q=4)
                for r in range(4):
                    rows = slice(32 * r, 32 * r + 32)
                    nc.vector.tensor_copy(eye32[rows, :], ident[rows, 32 * r:32 * r + 32]).then_inc(s5_clear, 1)
                    for q in range(4):
                        nc.vector.tensor_copy(own_d[rows, :, q],
                                              prm[32 * q:32 * q + 32, COL["o_D"]:COL["o_D"] + DT]).then_inc(s5_clear, 1)
                dve.wait_ge(s5_clear, 6 + 20)
                pipelined(dve, prep_dve, None, scan_dve)

            @block.tensor
            def _(pe):
                R5.start(pe, "pe")
                pipelined(pe, turn_pe, states_pe, output_pe)

            @block.scalar
            def _(act):
                R5.start(act, "act")
                act.wait_ge(s5_clear, 5)
                pipelined(act, turn_act, None, output_act)


    with ExitStack() as sc:
        y_hi = sb(sc, "yg_hi", [P, DT, SEQ], F32R)
        y_lo = sb(sc, "yg_lo", [P, DT, SEQ], F32R)
        sig = sb(sc, "glu_sig", [P, 2, SEQ])
        dn = Dense(sc, "g")
        w_glu = io["o_w_glu"].rearrange("a (k p) n -> (a p) k n", p=P)
        glu_out = sem("glu_out")
        q0, u0 = Dense.q // 2, Dense.u
        with nc.Block() as block:
            def y_part(eng, k, done):
                eng.wait_ge(y_hi_done, DT + k + 1)
                eng.tensor_tensor(y_lo[:, k, :], u_s5[:, k, :], y_hi[:, k, :].bitcast(F32), op=ALU.subtract).then_inc(done, 1)

            def cols(i, half):
                return bass.ds((i + (1 - half) * DT) * P, P)

            @block.sync
            def _(sp):
                with sp.Fori(0, DT) as i:
                    for half in range(2):
                        dn.load(sp, w_glu, DT, cols(i, half), i * 2 + (q0 + half), 0)

            @block.gpsimd
            def _(pool):
                dn.take_lo(pool, DT, q0, 0)
                for k in range(1, DT, 2):
                    y_part(pool, k, y_lo_odd)
                dn.take_lo(pool, DT, q0 + 1, 0)
                with pool.Fori(1, DT) as i:
                    for half in range(2):
                        dn.take_lo(pool, DT, i * 2 + (q0 + half), 0)

            @block.scalar
            def _(act):
                for k in range(DT):
                    if k == 2:
                        dn.take_hi(act, DT, q0, 0)
                    nc.scalar.copy(y_hi[:, k, :], u_s5[:, k, :]).then_inc(y_hi_done, 1)
                with act.Fori(0, DT - 1) as i:
                    dn.take_hi(act, DT, i * 2 + (q0 + 1), 0)
                    dn.wait_unit(act, i * 2 + q0, 1)
                    act.wait_ge(glu_out, i + 1)
                    nc.scalar.activation(sig[:, 0, :], dn.acc[0][:, :], ACT.Sigmoid).then_inc(unit_free, 1)
                    dn.take_hi(act, DT, i * 2 + (q0 + 2), 0)
                dn.take_hi(act, DT, q0 + 2 * DT - 1, 0)
                dn.wait_unit(act, q0 + 2 * DT - 2, 1)
                act.wait_ge(glu_out, DT)
                nc.scalar.activation(sig[:, 0, :], dn.acc[0][:, :], ACT.Sigmoid).then_inc(unit_free, 1)

            @block.tensor
            def _(pe):
                def parts(pe, k):
                    pe.wait_ge(y_lo_odd if k % 2 else y_lo_even, DT // 2 + k // 2 + 1)

                with pe.Fori(0, DT) as i:
                    for half in range(2):
                        dn.product(pe, DT, y_hi, y_lo, i * 2 + (u0 + half), half, i * 2 + (q0 + half), 0, parts)

            @block.vector
            def _(dve):
                for k in range(0, DT, 2):
                    y_part(nc.vector, k, y_lo_even)
                dve.sem_inc(glu_out, 1)
                with dve.Fori(0, DT) as i:
                    dn.wait_unit(dve, i * 2 + (q0 + 1), 1)
                    dve.wait_ge(unit_free, i * 2 + (u0 + 3))
                    nc.vector.tensor_tensor(sig[:, 1, :], sig[:, 0, :], dn.acc[1][:, :], ALU.mult).then_inc(unit_free, 1)
                    dve.wait_ge(unit_free, i * 2 + (u0 + 4))
                    here = x_res[:, bass.ds(i, 1), :]
                    nc.vector.tensor_tensor(here, here, sig[:, 1, :], ALU.add).then_inc(glu_out, 1)
        Dense.q += 4 * DT
        Dense.u += 2 * DT
    s5.close()

    conv_ffn(1)

    with ExitStack() as sc:
        chan = sb(sc, "chan", [P, 2, SEQ])
        rows = sb(sc, "out_rows", [P, 2, SEQ])
        nm = Norm(sc, "out", "final_norm_g", 0, sb(sc, "scratch_out", [P, 8, SEQ]))
        turned = [ps(sc, f"out_ps{s}", [P, SEQ]) for s in range(2)]
        o_turned, o_kept = sem("o_turned"), sem("o_kept")
        o_stored = [sem("o_stored0"), sem("o_stored1")]
        out_v = out.rearrange("b (k t) c -> (b t) k c", t=P)
        with nc.Block() as block:
            @block.scalar
            def _(act):
                nm.squares_act(act)
                nm.root_act(act)
                act.sem_inc(o_kept, 2)
                with act.Fori(0, DT // 2) as n:
                    for s in range(2):
                        act.wait_ge(o_turned, n * 2 + (s + 3))
                        act.wait_ge(o_stored[s], n * 16 + 16)
                        nc.scalar.copy(rows[:, s, :], turned[s][:, :]).then_inc(o_kept, 1)

            @block.tensor
            def _(pe):
                nm.sums_pe(pe)
                pe.sem_inc(o_turned, 2)
                with pe.Fori(0, DT // 2) as n:
                    for s in range(2):
                        pe.wait_ge(n_scaled, n * 2 + (nm.n * DT + s + 1))
                        pe.wait_ge(o_kept, n * 2 + (s + 1))
                        for k in range(TB):
                            last = nc.tensor.transpose(turned[s][:, k * P:(k + 1) * P], chan[:, s, k * P:(k + 1) * P], ident[:, :])
                        last.then_inc(o_turned, 1)

            @block.vector
            def _(dve):
                nm.sums_dve(dve)
                with dve.Fori(0, DT // 2) as n:
                    for s in range(2):
                        dve.wait_ge(o_turned, n * 2 + (s + 1))
                        nm.scaled_dve(x_res[:, bass.ds(n * 2 + s, 1), :], chan[:, s, :], col_at("final_norm_g", n * 2 + s))

            @block.sync
            def _(sp):
                for s in range(2):
                    sp.sem_inc(o_stored[s], 16)
                with sp.Fori(0, DT // 2) as n:
                    for s in range(2):
                        sp.wait_ge(o_kept, n * 2 + (s + 3))
                        sp.dma_start(out_v[:, :, bass.ds(n * (2 * P) + s * P, P)],
                                     rows[:, s, :].rearrange("p (k c) -> p k c", c=P)).then_inc(o_stored[s], 16)
                for s in range(2):
                    sp.wait_ge(o_stored[s], 16 + 16 * (DT // 2))
    ctx.close()


INPUTS = ["x", "e_norm_g", "e_w_in", "e_mu", "e_w0", "e_w2", "e_a0", "e_a2", "e_g2", "e_k_k", "e_k_a", "e_r_k",
          "e_ln_w", "e_ln_b", "e_conv_w", "e_conv_b", "e_gate_a_w", "e_gate_a_b", "e_gate_x_w", "e_gate_x_b",
          "e_lru_lambda", "e_w_out", "o_norm_g", "o_w_in", "o_A_re", "o_A_im", "o_log_dt", "o_B_re", "o_B_im",
          "o_C_re", "o_C_im", "o_D", "o_w_glu", "f_norm_g", "f_w_up", "f_conv_w", "f_conv_b", "f_w_down",
          "final_norm_g"]


def kernel(**inputs):
    import numpy as np
    import concourse.bacc as bacc
    from concourse.bass_utils import run_bass_kernel_spmd

    nc = bacc.Bacc("TRN2", target_bir_lowering=False, num_devices=1)
    arrays = {f"in_{n}": np.ascontiguousarray(inputs[n]) for n in INPUTS}
    io = {n: nc.dram_tensor(f"in_{n}", arrays[f"in_{n}"].shape, F32, kind="ExternalInput").ap() for n in INPUTS}
    out = nc.dram_tensor("out_0", (1, SEQ, D_MODEL), F32, kind="ExternalOutput").ap()
    trunk(nc, io, out)
    result = run_bass_kernel_spmd(nc, [arrays], core_ids=[0])
    return result.results[0]["out_0"]
```
